# Optimizing a Trainium2 kernel written in Bass

```python
import jax, jax.numpy as jnp
from jax import lax
import numpy as np

D_MODEL = 1024
BATCH = 1
SEQ = 128
DEPTH = 1
DEC_BATCH = 1
DEC_SEQ = 512
PAST_LEN = 256

GRID_W = 64
MIX_WIDTH = D_MODEL
LRU_WIDTH = MIX_WIDTH // 2
LRU_HEADS = 8
LRU_HEAD_DIM = LRU_WIDTH // LRU_HEADS
LRU_C = 8.0
CONV_W = 4
CONV_PAD_LEFT = 2
RET_WIDTH = MIX_WIDTH - LRU_WIDTH
RET_HEADS = 4
RET_DK = RET_WIDTH // RET_HEADS
RET_DV = RET_WIDTH // RET_HEADS
RET_CHUNK = 64
RET_DECAY_OFFSET_FWD = 5.0
RET_DECAY_OFFSET_BWD = 5.5
ROPE_BASE = 10000.0
IN_PROJ_WIDTH = 2 * LRU_WIDTH + 4 * RET_WIDTH
IN_SPLITS = (LRU_WIDTH, 2 * LRU_WIDTH, 2 * LRU_WIDTH + RET_WIDTH,
             2 * LRU_WIDTH + 2 * RET_WIDTH, 2 * LRU_WIDTH + 3 * RET_WIDTH)
N_EXPERTS = 16
EC_CAPACITY_FACTOR = 2
EXPERT_FF = 2 * D_MODEL
N_MOD = 6
EPS = 1e-6

kernel_name = 'hybrid_rglru_retention_ecmoe_diffusion_step'

def _normal(k, shape, scale):
    return jax.random.normal(k, shape, jnp.float32) * scale

def _rms_norm(x, gain):
    xf = x.astype(jnp.float32)
    y = xf * lax.rsqrt(jnp.mean(xf * xf, axis=-1, keepdims=True) + EPS)
    return (y * gain.astype(jnp.float32)).astype(x.dtype)

def _dwconv_centred(x, w, b):
    n = x.shape[1]
    xp = jnp.pad(x, ((0, 0), (CONV_PAD_LEFT, CONV_W - 1 - CONV_PAD_LEFT), (0, 0)))
    y = b
    for tap in range(CONV_W):
        y = y + xp[:, tap:tap + n] * w[tap]
    return y

def _lin_combine(e1, e2):
    a1, b1 = e1
    a2, b2 = e2
    return a1 * a2, a2 * b1 + b2

def _rglru_dir(x, wa, ba, wi, bi, lam, h0, reverse):
    bsz, n, w = x.shape
    xf = x.astype(jnp.float32)
    xh = xf.reshape(bsz, n, LRU_HEADS, LRU_HEAD_DIM)
    r = jax.nn.sigmoid(jnp.einsum('bnhi,hij->bnhj', xh, wa.astype(jnp.float32)).reshape(bsz, n, w)
                       + ba.astype(jnp.float32))
    gi = jax.nn.sigmoid(jnp.einsum('bnhi,hij->bnhj', xh, wi.astype(jnp.float32)).reshape(bsz, n, w)
                        + bi.astype(jnp.float32))
    log_a = -LRU_C * r * jax.nn.softplus(-lam.astype(jnp.float32))
    a = jnp.exp(log_a)
    u = jnp.sqrt(-jnp.expm1(2.0 * log_a)) * gi * xf
    first = n - 1 if reverse else 0
    last = 0 if reverse else n - 1
    u = u.at[:, first].add(a[:, first] * h0.astype(jnp.float32))
    _, h = lax.associative_scan(_lin_combine, (a, u), reverse=reverse, axis=1)
    return h, h[:, last]

def _ret_log_decay(offset):
    return jnp.log1p(-jnp.exp2(-(offset + jnp.arange(RET_HEADS, dtype=jnp.float32))))

def _retention_dir(q, k, v, s0, log_g, strict):
    bsz, n, h, dk = q.shape
    dv = v.shape[-1]
    nc = n // RET_CHUNK
    qc = q.reshape(bsz, nc, RET_CHUNK, h, dk)
    kc = k.reshape(bsz, nc, RET_CHUNK, h, dk)
    vc = v.reshape(bsz, nc, RET_CHUNK, h, dv)
    pos = jnp.arange(RET_CHUNK, dtype=jnp.float32)
    diff = pos[:, None] - pos[None, :]
    mask = (diff > 0) if strict else (diff >= 0)
    d_intra = jnp.where(mask[None], jnp.exp(jnp.where(mask, diff, 0.0)[None] * log_g[:, None, None]), 0.0)
    xi = jnp.exp((pos + 1.0)[None, :] * log_g[:, None])
    zeta = jnp.exp((RET_CHUNK - 1.0 - pos)[None, :] * log_g[:, None])
    chunk_decay = jnp.exp(RET_CHUNK * log_g)[:, None, None]
    scores = jnp.einsum('bcihd,bcjhd->bchij', qc, kc) * d_intra
    o_inner = jnp.einsum('bchij,bcjhe->bcihe', scores, vc)
    kv = jnp.einsum('bcjhd,hj,bcjhe->bchde', kc, zeta, vc)

    def step(s, kv_c):
        return s * chunk_decay + kv_c, s

    s_final, s_prev = lax.scan(step, s0, jnp.moveaxis(kv, 1, 0))
    s_prev = jnp.moveaxis(s_prev, 0, 1)
    o_cross = jnp.einsum('bcihd,hi,bchde->bcihe', qc, xi, s_prev)
    return (o_inner + o_cross).reshape(bsz, n, h, dv), s_final

def _rope_grid(x):
    n = x.shape[1]
    rows = n // GRID_W
    row = jnp.repeat(jnp.arange(rows, dtype=jnp.float32), GRID_W)
    col = jnp.tile(jnp.arange(GRID_W, dtype=jnp.float32), rows)
    nf = RET_DK // 4
    freqs = ROPE_BASE ** (-jnp.arange(nf, dtype=jnp.float32) / nf)
    ang = jnp.concatenate([row[:, None] * freqs, col[:, None] * freqs], axis=-1)
    cos = jnp.cos(ang)[None, :, None, :]
    sin = jnp.sin(ang)[None, :, None, :]
    xa, xb = jnp.split(x, 2, axis=-1)
    return jnp.concatenate([xa * cos - xb * sin, xa * sin + xb * cos], axis=-1)

def _mixer(h, lp, lru_h0, ret_s0, latent):
    bsz, n, _ = h.shape
    f32 = jnp.float32
    proj = h @ lp['w_in']
    xl, yl, q, k, v, g = jnp.split(proj, IN_SPLITS, axis=-1)
    xl = _dwconv_centred(xl, lp['conv_w'], lp['conv_b'])
    hf, hf_last = _rglru_dir(xl, lp['lru_wa'][0], lp['lru_ba'][0], lp['lru_wi'][0], lp['lru_bi'][0],
                             lp['lru_lambda'][0], lru_h0[:, 0], reverse=False)
    hb, hb_first = _rglru_dir(xl, lp['lru_wa'][1], lp['lru_ba'][1], lp['lru_wi'][1], lp['lru_bi'][1],
                              lp['lru_lambda'][1], lru_h0[:, 1], reverse=True)
    lru_out = ((hf + hb) * jax.nn.gelu(yl.astype(f32))).astype(h.dtype)
    qh = q.astype(f32).reshape(bsz, n, RET_HEADS, RET_DK) * (RET_DK ** -0.5)
    kh = k.astype(f32).reshape(bsz, n, RET_HEADS, RET_DK)
    vh = v.astype(f32).reshape(bsz, n, RET_HEADS, RET_DV)
    if latent:
        qh = _rope_grid(qh)
        kh = _rope_grid(kh)
    of, sf = _retention_dir(qh, kh, vh, ret_s0[:, 0].astype(f32),
                            _ret_log_decay(RET_DECAY_OFFSET_FWD), strict=False)
    ob, sb = _retention_dir(jnp.flip(qh, 1), jnp.flip(kh, 1), jnp.flip(vh, 1), ret_s0[:, 1].astype(f32),
                            _ret_log_decay(RET_DECAY_OFFSET_BWD), strict=True)
    o = of + jnp.flip(ob, 1)
    o = o * lax.rsqrt(jnp.mean(o * o, axis=-1, keepdims=True) + EPS)
    ret_out = (o.reshape(bsz, n, RET_WIDTH) * jax.nn.silu(g.astype(f32))).astype(h.dtype)
    out = jnp.concatenate([lru_out, ret_out], axis=-1) @ lp['w_out']
    lru_state = jnp.stack([hf_last, hb_first], axis=1).astype(h.dtype)
    ret_state = jnp.stack([sf, sb], axis=1).astype(h.dtype)
    return out, lru_state, ret_state

def _expert_choice_ffn(h, router_w, wg, wu, wd):
    bsz, n, _ = h.shape
    cap = EC_CAPACITY_FACTOR * n // N_EXPERTS
    probs = jax.nn.softmax((h @ router_w).astype(jnp.float32), axis=-1)
    gate, idx = lax.top_k(jnp.swapaxes(probs, 1, 2), cap)
    b_idx = jnp.arange(bsz)[:, None, None]
    xs = h[b_idx, idx]
    hid = jax.nn.silu(jnp.einsum('becd,edf->becf', xs, wg)) * jnp.einsum('becd,edf->becf', xs, wu)
    ye = jnp.einsum('becf,efd->becd', hid, wd) * gate[..., None].astype(h.dtype)
    return jnp.zeros_like(h).at[b_idx, idx].add(ye)

def _block(x, mod, lp, lru_h0, ret_s0, latent):
    m = mod.reshape(mod.shape[0], N_MOD, D_MODEL)[:, :, None, :]
    sh1, sc1, g1, sh2, sc2, g2 = (m[:, i] for i in range(N_MOD))
    h = _rms_norm(x, lp['norm_mix_pre']) * (1.0 + sc1) + sh1
    mix, lru_state, ret_state = _mixer(h, lp, lru_h0, ret_s0, latent)
    x = x + g1 * _rms_norm(mix, lp['norm_mix_post'])
    h = _rms_norm(x, lp['norm_ffn_pre']) * (1.0 + sc2) + sh2
    f = _expert_choice_ffn(h, lp['router_w'], lp['exp_w_gate'], lp['exp_w_up'], lp['exp_w_down'])
    x = x + g2 * _rms_norm(f, lp['norm_ffn_post'])
    return x, lru_state, ret_state

def setup_inputs(seed: int = 0) -> dict:
    key = jax.random.key(seed)
    ks = jax.random.split(key, 27)
    a_c = jax.random.uniform(ks[22], (DEPTH, 2, LRU_WIDTH), jnp.float32, minval=0.9, maxval=0.999)
    a = a_c ** (1.0 / LRU_C)
    lam = jnp.log(a) - jnp.log1p(-a)
    return {
        'x_prompt': _normal(ks[0], (BATCH, SEQ, D_MODEL), 1.0),
        'x_sample': _normal(ks[1], (DEC_BATCH, DEC_SEQ, D_MODEL), 1.0),
        'c': _normal(ks[2], (DEC_BATCH, D_MODEL), 1.0),
        'state_lru': _normal(ks[3], (DEC_BATCH, DEPTH, 2, LRU_WIDTH), 0.5),
        'state_ret': _normal(ks[4], (DEC_BATCH, DEPTH, 2, RET_HEADS, RET_DK, RET_DV), 4.0),
        'c_ctx': _normal(ks[5], (D_MODEL,), 1.0),
        'ada_w': _normal(ks[6], (DEPTH, D_MODEL, N_MOD * D_MODEL), 0.5 * D_MODEL ** -0.5),
        'ada_b': _normal(ks[7], (DEPTH, N_MOD * D_MODEL), 0.01),
        'norm_mix_pre': 1.0 + _normal(ks[8], (DEPTH, D_MODEL), 0.05),
        'norm_mix_post': 1.0 + _normal(ks[9], (DEPTH, D_MODEL), 0.05),
        'norm_ffn_pre': 1.0 + _normal(ks[10], (DEPTH, D_MODEL), 0.05),
        'norm_ffn_post': 1.0 + _normal(ks[11], (DEPTH, D_MODEL), 0.05),
        'w_in': _normal(ks[12], (DEPTH, D_MODEL, IN_PROJ_WIDTH), D_MODEL ** -0.5),
        'conv_w': _normal(ks[13], (DEPTH, CONV_W, LRU_WIDTH), CONV_W ** -0.5),
        'conv_b': _normal(ks[14], (DEPTH, LRU_WIDTH), 0.01),
        'lru_wa': _normal(ks[15], (DEPTH, 2, LRU_HEADS, LRU_HEAD_DIM, LRU_HEAD_DIM), LRU_HEAD_DIM ** -0.5),
        'lru_ba': _normal(ks[16], (DEPTH, 2, LRU_WIDTH), 0.01),
        'lru_wi': _normal(ks[17], (DEPTH, 2, LRU_HEADS, LRU_HEAD_DIM, LRU_HEAD_DIM), LRU_HEAD_DIM ** -0.5),
        'lru_bi': _normal(ks[18], (DEPTH, 2, LRU_WIDTH), 0.01),
        'lru_lambda': lam,
        'w_out': _normal(ks[19], (DEPTH, MIX_WIDTH, D_MODEL), MIX_WIDTH ** -0.5),
        'router_w': _normal(ks[20], (DEPTH, D_MODEL, N_EXPERTS), D_MODEL ** -0.5),
        'exp_w_gate': _normal(ks[21], (DEPTH, N_EXPERTS, D_MODEL, EXPERT_FF), D_MODEL ** -0.5),
        'exp_w_up': _normal(ks[23], (DEPTH, N_EXPERTS, D_MODEL, EXPERT_FF), D_MODEL ** -0.5),
        'exp_w_down': _normal(ks[24], (DEPTH, N_EXPERTS, EXPERT_FF, D_MODEL), EXPERT_FF ** -0.5),
    }

def reference(x_prompt, x_sample, c, state_lru, state_ret, c_ctx, ada_w, ada_b,
              norm_mix_pre, norm_mix_post, norm_ffn_pre, norm_ffn_post, w_in, conv_w, conv_b,
              lru_wa, lru_ba, lru_wi, lru_bi, lru_lambda, w_out, router_w,
              exp_w_gate, exp_w_up, exp_w_down):
    bp = x_prompt.shape[0]
    y_prompt = x_prompt
    y_sample = x_sample
    new_lru = []
    new_ret = []
    for l in range(DEPTH):
        lp = {
            'norm_mix_pre': norm_mix_pre[l], 'norm_mix_post': norm_mix_post[l],
            'norm_ffn_pre': norm_ffn_pre[l], 'norm_ffn_post': norm_ffn_post[l],
            'w_in': w_in[l], 'conv_w': conv_w[l], 'conv_b': conv_b[l],
            'lru_wa': lru_wa[l], 'lru_ba': lru_ba[l], 'lru_wi': lru_wi[l], 'lru_bi': lru_bi[l],
            'lru_lambda': lru_lambda[l], 'w_out': w_out[l], 'router_w': router_w[l],
            'exp_w_gate': exp_w_gate[l], 'exp_w_up': exp_w_up[l], 'exp_w_down': exp_w_down[l],
        }
        mod_ctx = jax.nn.silu(c_ctx)[None, :] @ ada_w[l] + ada_b[l]
        mod_lat = jax.nn.silu(c) @ ada_w[l] + ada_b[l]
        zero_lru = jnp.zeros((bp, 2, LRU_WIDTH), x_prompt.dtype)
        zero_ret = jnp.zeros((bp, 2, RET_HEADS, RET_DK, RET_DV), x_prompt.dtype)
        y_prompt, lru_l, ret_l = _block(y_prompt, mod_ctx, lp, zero_lru, zero_ret, latent=False)
        y_sample, _, _ = _block(y_sample, mod_lat, lp, state_lru[:, l], state_ret[:, l], latent=True)
        new_lru.append(lru_l)
        new_ret.append(ret_l)
    new_state_lru = jnp.stack(new_lru, axis=1)
    new_state_ret = jnp.stack(new_ret, axis=1)
    return (y_prompt, y_sample, new_state_lru, new_state_ret)


_drawn_inputs = setup_inputs


def setup_inputs(seed=0):
    import zlib

    import numpy as np

    out = dict(_drawn_inputs(seed))
    spreads = {}
    factors = {'norm_ffn_post': 3.908, 'lru_ba': 8.0, 'lru_bi': 3.165}
    for name, (base, spread) in spreads.items():
        noise = np.random.default_rng([zlib.crc32(name.encode()), seed]).standard_normal(out[name].shape)
        drawn = base * np.exp(spread * noise) if base else spread * noise
        out[name] = __import__('jax').numpy.asarray(drawn.astype(out[name].dtype))
    for name, factor in factors.items():
        out[name] = (out[name] * factor).astype(out[name].dtype)
    return out
```

```python
from contextlib import ExitStack

import concourse.bass as bass
from concourse import mybir

F32 = mybir.dt.float32
F32R = mybir.dt.float32r
ALU = mybir.AluOpType
ACT = mybir.ActivationFunctionType
AX = mybir.AxisListType

P = 128
D = 1024
KT = D // P
LAT, CTX = 512, 128
TOK = LAT + CTX
TILES = TOK // P
LW = 512
CT = LW // P
HEADS, DK = 4, 128
NEXP = 16
CAP_L, CAP_C = 2 * LAT // NEXP, 2 * CTX // NEXP
SLOTS = CAP_L + CAP_C
FF = 2 * D
NB = FF // 512
EPS = 1e-6

RAW, WS = 4, 3
CH = 2048

ADA_FIRST = [0, 1, 2, 3]
WIN = [1, 0, 2, 3, 4, 5]
ADA_MID = [6, 7, 8, 9]
ADA_GATES = [4, 5, 10, 11]
N_WIN = 2 * len(ADA_FIRST)
N_MID = N_WIN + 2 * len(WIN)
N_GATES = N_MID + 2 * len(ADA_MID)
N_WOUT = N_GATES + 2 * len(ADA_GATES)
N_EXP = N_WOUT + 4
PER_E = 24
N_BODY = N_EXP + 4

S_ABS, S_EXP, S_C8, S_NC8, S_SS, S_RSTD, S_WO, S_X1 = 0, 8, 24, 32, 40, 58, 48, 64
S_FIN, S_MAX, S_SUM, S_REC, S_T, S_ST, S_O = 80, 88, 93, 98, 104, 112, 120
GATES_AT = {0: 0, 2: 1, 4: 2, 5: 3}
C_ID, C_XI, C_ZETA, C_IOTA, C_SELC, C_SELB = 0, 128, 160, 168, 328, 330
C_N = 586
R_C, R_PRE, R_FPRE, R_CW, R_CB, R_BA, R_BI, R_LAM, R_H0, R_ADAB = 0, 16, 24, 32, 48, 52, 60, 68, 76, 84
R_N = 116


def after_split(n):
    return ("pool", n // RAW + 1) if n % RAW == RAW - 1 else ("dve", (n // RAW) * (RAW - 1) + n % RAW + 1)


def build(nc, x_ctx, x_lat, c, state_lru, state_ret, c_ctx, ada_w, ada_b, norm_mix_pre, norm_mix_post,
          norm_ffn_pre, norm_ffn_post, w_in, conv_w, conv_b, lru_wa, lru_ba, lru_wi, lru_bi, lru_lambda,
          w_out, router_w, exp_gate, exp_up, exp_down, consts, decay, rope, y_ctx, y_lat, new_lru, new_ret):
    ctx = ExitStack()
    sb = lambda n, s, d=F32: ctx.enter_context(nc.sbuf_tensor(n, s, d))
    sem = lambda n: ctx.enter_context(nc.semaphore(n))

    raw = sb("raw", [P, RAW, CH])
    w_hi = sb("w_hi", [P, WS, CH], F32R)
    w_lo = sb("w_lo", [P, WS, CH], F32R)
    act_hi = sb("act_hi", [P, KT * TOK], F32R)
    act_lo = sb("act_lo", [P, KT * TOK], F32R)
    arena = sb("arena", [P, 18944])
    const = sb("const", [P, C_N])
    rows = sb("rows", [P, D])
    cond = sb("cond", [P, KT, 66], F32R)
    par = sb("par", [P, R_N])
    sil = sb("sil", [P, 16])
    modc = sb("modc", [P, 2, 32])
    aff = sb("aff", [P, 2, 2, KT])
    rw = sb("rw", [P, KT, NEXP])
    sp = sb("sp", [P, TILES, 2, NEXP])
    ecol = sb("ecol", [P, TILES, 2])
    gate = sb("gate", [P, 1])
    sm = sb("sm", [P, 128])
    psum = [ctx.enter_context(nc.psum_tensor(f"bank{i}", [P, 512], F32)) for i in range(8)]

    def region(at, *shape):
        n = 1
        for s in shape:
            n *= s
        v = arena[:, at:at + n]
        if len(shape) == 1:
            return v
        names = " ".join("abcd"[:len(shape)])
        return v.rearrange(f"p ({names}) -> p {names}", **{"abcd"[i]: shape[i] for i in range(len(shape))})

    gel = region(0, CT, TOK)
    qT = region(2560, HEADS, TOK)
    kT = region(5120, HEADS, TOK)
    v_t = region(7680, TILES, LW)
    xc = region(10240, CT, TOK)
    sg = region(10240, TILES, LW)
    x_in = region(12800, TILES, D)
    hT_tmp = region(0, 2, TOK)
    junk0 = region(5120, D)
    rope_tmp = region(7680, 2, LAT)
    par_rows = region(2560, P)
    lr_r, lr_g, lr_a, lr_t = (region(12800 + i * 2 * TOK, 2, TOK) for i in range(4))
    rope_c, rope_s = region(17920, LAT), region(17920 + LAT, LAT)
    sc = region(12800, 4, LAT)
    sc_c = region(14848, CTX)
    dec = region(14976, 2, 896)
    s0 = region(16768, 2, 2 * DK)
    o_t = region(17280 , TILES, DK)
    ro_t = region(17920, TILES, DK)
    kz = region(18560, 2, DK)
    x1 = region(0, TILES, D)
    xn2 = region(5120, TILES, D)
    facc = region(10240, TILES, D)
    h2T = region(10240, 2, KT, P)
    junk = region(12288, D)
    pT, pW, pS, pC = (region(10240 + i * TOK, TOK) for i in range(4))
    g_row = region(15360, 2, D)
    post = region(17408, D)
    mg1 = region(13312, D)
    sgl = region(15360, 2, 512)
    hid = region(16384, 2, 512)
    oneh = region(17408, TILES, SLOTS)
    xs_tmp = region(17808, 2, 4 * SLOTS)

    hT_hi = act_hi[:, :].rearrange("p (k t) -> p k t", k=KT)
    hT_lo = act_lo[:, :].rearrange("p (k t) -> p k t", k=KT)
    xs = [[a[:, i * KT * SLOTS:(i + 1) * KT * SLOTS].rearrange("p (k s) -> p k s", k=KT) for a in (act_hi, act_lo)]
          for i in range(2)]
    hidT = [[a[:, 1280 + i * 4 * SLOTS:1280 + (i + 1) * 4 * SLOTS] for a in (act_hi, act_lo)] for i in range(2)]
    ye = [a[0:SLOTS, 1920:1920 + D] for a in (act_hi, act_lo)]
    onehotT = act_hi[0:SLOTS, 2944:2944 + TOK]

    ident = const[:, C_ID:C_ID + P]
    xi = const[:, C_XI:C_XI + 32].rearrange("p (t h d) -> p t h d", t=4, h=HEADS)
    zeta = const[:, C_ZETA:C_ZETA + 8].rearrange("p (h d) -> p h d", h=HEADS)
    iota = const[:, C_IOTA:C_IOTA + 2 * SLOTS].rearrange("p (g s) -> p g s", g=2)
    selc = const[:, C_SELC:C_SELC + 2]
    selb = const[:, C_SELB:C_SELB + 2 * P].rearrange("p (g m) -> p g m", g=2)
    lst = rows[:, 512:768]
    lrow = rows[0:8, 768:896]
    gw = rows[:, :].rearrange("p (k d c j) -> p k d c j", k=2, d=2, c=CT)

    const_in, par_in, x_ld, x_re, rw_in, gw_in, rope_in = map(sem, (
        "const_in", "par_in", "x_loaded", "x_reloaded", "router_in", "lru_gates_in", "rope_in"))
    gbias1, gbias2, post_in, dec_in = map(sem, ("gate1_bias_in", "gate2_bias_in", "post_gain_in", "decay_in"))
    dec_in = [dec_in, sem("decay_in_odd")]
    raw_in = [sem(f"raw_in{i}") for i in range(RAW)]
    out_lru, out_ret, out_y = map(sem, ("lru_state_out", "ret_state_out", "y_out"))
    hi_done, lo_dve, lo_pool, w_used = map(sem, ("hi_done", "lo_done_dve", "lo_done_pool", "w_used"))
    dve_step, act_step, pool_step = map(sem, ("dve_step", "act_step", "pool_step"))
    par_ps, par_rd, sil_rd, lam_abs, lam_exp, cond_0, cond_rd, c8_rd = map(sem, (
        "par_ps", "par_ready", "silu_ready", "lambda_abs", "lambda_exp", "cond_zeroed", "cond_ready", "c8_ready"))
    ada_row, col_ps, col_rd = map(sem, ("ada_row", "columns_ps", "columns_ready"))
    x_sq, xn_rd, xT_ps, h_tmp, h_hi, h_lo = map(sem, ("x_squares", "xn_ready", "xT_ps", "h_tmp", "h_hi", "h_lo"))
    win_ps, yl_ev, xl_ev, rope_t, qk_rd, qk_ctx, v_ev, g_ev = map(sem, (
        "win_ps", "yl_out", "conv_done", "rope_terms", "qk_ready", "qk_ctx_out", "v_out", "g_out"))
    gt_ps, gt_ev, lr_exp, lr_gx, lr_w, lr_sq, lr_done = map(sem, (
        "lru_gate_ps", "lru_gates_out", "lru_exp", "lru_gx", "lru_w", "lru_sqrt", "lru_done"))
    cat_hi, cat_lo = sem("lru_cat_hi"), sem("lru_cat_lo")
    sc_ps, sc_ev, scc_ps, scc_ev, pv_ps, pvc_ps, kt_ps, kz_ev, st_ps, st_ev, ret_o, rt_ps, rt_hi, rt_lo = map(sem, (
        "score_ps", "score_masked", "ctx_score_ps", "ctx_score_masked", "pv_ps", "ctx_pv_ps", "kT_ps", "kz_ready",
        "state_ps", "state_copied", "ret_out", "ret_T_ps", "ret_T_hi", "ret_T_lo"))
    lst_ps, lst_ev = sem("lru_state_ps"), sem("lru_state_row")
    gr_ps, gr_ev, wo_ps, wo_ev, wo_sq, x1_rd, x1_sq, xn2_rd = map(sem, (
        "gate_row_ps", "gate_row", "wout_ps", "wout_copied", "wout_squares", "x1_ready", "x1_squares", "xn2_ready"))
    h2_ps, h2_act, h2_dve, lg_ps, lg_sub, lg_exp, pr_rd, pt_ps, sl_rd, sl_ps, fz = map(sem, (
        "h2_ps", "h2_act", "h2_dve", "logits_ps", "logits_less_max", "logits_exp", "probs_ready", "probsT_ps",
        "slots_ready", "slots_ps", "facc_zeroed"))
    sl_ev, hid_rd, ht_ps, ht_hi, ht_lo = map(sem, ("silu_out", "hid_ready", "hidT_ps", "hidT_hi", "hidT_lo"))
    oh_rd, oht_ps, oht_ev, ga_ps, xs_f, xs_h, xs_l, ye_h, ye_l, fs_ps, fs_add = map(sem, (
        "onehot_ready", "onehotT_ps", "onehotT_out", "gather_ps", "gathered", "gathered_hi", "gathered_lo",
        "ye_hi", "ye_lo", "scatter_ps", "scatter_added"))
    ec_rd, xs_m = sem("expert_columns"), sem("gathered_scaled")
    root_in, root_out = sem("root_argument"), sem("root_taken")
    fin_sq, fin_y = sem("f_squares"), sem("y_ready")

    aw = ada_w.rearrange("(k p) n -> p k n", p=P)
    wi = w_in.rearrange("(k p) n -> p k n", p=P)
    wo = w_out.rearrange("(k p) n -> p k n", p=P)

    def block_cols(w, blk, half):
        return w[:, 4 * half:4 * half + 4, blk * 512:(blk + 1) * 512]

    def prologue_source(n):
        if n < N_WIN:
            return block_cols(aw, ADA_FIRST[n // 2], n % 2)
        if n < N_MID:
            return block_cols(wi, WIN[(n - N_WIN) // 2], n % 2)
        if n < N_GATES:
            return block_cols(aw, ADA_MID[(n - N_MID) // 2], n % 2)
        if n < N_WOUT:
            return block_cols(aw, ADA_GATES[(n - N_GATES) // 2], n % 2)
        return block_cols(wo, (n - N_WOUT) // 2, n % 2)

    def expert_source(e, kind, b, half):
        if kind == "d":
            w = exp_down[bass.ds(e, 1), b * 512:(b + 1) * 512, :].rearrange("o (p j) n -> p (o j) n", p=P)
            return w[:, 2 * half:2 * half + 2, :]
        w = {"g": exp_gate, "u": exp_up}[kind]
        w = w[bass.ds(e, 1), :, b * 512:(b + 1) * 512].rearrange("o (k p) n -> p (o k) n", p=P)
        return w[:, 4 * half:4 * half + 4, :]

    def body_chunks(last):
        out = []
        for b in (1, 2, 3):
            for kind, blk in (("g", b), ("u", b), ("d", b - 1)):
                out += [(kind, blk, 0, 0), (kind, blk, 1, 0)]
        if not last:
            out += [("g", 0, 0, 1), ("g", 0, 1, 1)]
        out += [("d", 3, 0, 0), ("d", 3, 1, 0)]
        if not last:
            out += [("u", 0, 0, 1), ("u", 0, 1, 1)]
        return out

    def chunk_view(ring, n, cols):
        return ring[:, n % ring.shape[1], :].rearrange("p (k n) -> p k n", n=cols)

    def load(sp_e, n, e, src, cols):
        if n >= RAW or not isinstance(e, int):
            who, count = after_split(n - RAW)
            sp_e.wait_ge(lo_pool if who == "pool" else lo_dve, count + e * (PER_E // RAW * (1 if who == "pool" else RAW - 1)))
        sp_e.dma_start(chunk_view(raw, n, cols), src).then_inc(raw_in[n % RAW], 16)

    def split_hi(act, n, e=0):
        act.wait_ge(raw_in[n % RAW], e * (16 * PER_E // RAW) + 16 * (n // RAW + 1))
        if n >= WS:
            act.wait_ge(w_used, e * PER_E + (n - WS + 1))
        nc.scalar.copy(w_hi[:, n % WS, :], raw[:, n % RAW, :]).then_inc(hi_done, 1)

    def split_lo(eng, who, n, e=0):
        if after_split(n)[0] != who:
            return
        eng.wait_ge(hi_done, e * PER_E + (n + 1))
        ops, done = (nc.gpsimd, lo_pool) if who == "pool" else (nc.vector, lo_dve)
        ops.tensor_tensor(w_lo[:, n % WS, :], raw[:, n % RAW, :], w_hi[:, n % WS, :], ALU.subtract).then_inc(done, 1)

    def chunk_ready(pe, n, e=0):
        who, count = after_split(n)
        pe.wait_ge(lo_pool if who == "pool" else lo_dve, count + e * (PER_E // RAW * (1 if who == "pool" else RAW - 1)))

    def used(eng, n, e=0):
        eng.wait_ge(w_used, e * PER_E + (n + 1))

    def ada_chunk(i):
        return (0, N_MID - 8, N_GATES - 16)[i // 4] + 2 * i

    def win_ready(eng, bi, u):
        if u == (CT if bi < 4 else TILES) - 1:
            used(eng, N_WIN + 2 * bi + 1)
        else:
            eng.wait_ge(win_ps, (0, 3, 6, 9, 12, 16)[bi] + u + 1)

    def wout_ready(eng, n2, t):
        if t == TILES - 1:
            used(eng, N_WOUT + 2 * n2 + 1)
        else:
            eng.wait_ge(wo_ps, 4 * n2 + t + 1)

    def three(out, lh, ll, rh, rl, start, stop, **kw):
        nc.tensor.matmul(out, lh, rl, start=start, stop=False, **kw)
        nc.tensor.matmul(out, ll, rh, start=False, stop=False, **kw)
        return nc.tensor.matmul(out, lh, rh, start=False, stop=stop, **kw)

    LAST = NEXP - 1
    block = ctx.enter_context(nc.Block())

    @block.sync
    def _(sync):
        for n in range(N_EXP):
            load(sync, n, 0, prologue_source(n), 512)
        for i, (kind, half) in enumerate((("g", 0), ("g", 1), ("u", 0), ("u", 1))):
            load(sync, N_EXP + i, 0, expert_source(0, kind, 0, half), 512)

        def body(e, last):
            for i, (kind, b, half, nxt) in enumerate(body_chunks(last)):
                load(sync, N_BODY + i, e, expert_source(e + nxt, kind, b, half), D if kind == "d" else 512)

        with sync.Fori(0, LAST) as e:
            sync.compute_val(e * (FF * D) * 4)
            body(e, False)
        body(LAST, True)
        sync.wait_ge(out_lru, 16)
        sync.wait_ge(out_ret, 16 * 2 * HEADS)
        sync.wait_ge(out_y, 16 * TILES)

    @block.scalar
    def _(act):
        pr = par_rows
        act.dma_start(const[:, :], consts).then_inc(const_in, 16)
        for r0, a in ((R_C, c), (R_C + 8, c_ctx), (R_PRE, norm_mix_pre), (R_FPRE, norm_ffn_pre), (R_CW, conv_w),
                      (R_CB, conv_b), (R_BA, lru_ba), (R_BI, lru_bi), (R_LAM, lru_lambda), (R_H0, state_lru),
                      (R_ADAB, ada_b[0:16, :]), (R_ADAB + 16, ada_b[24:40, :])):
            act.dma_start(pr[r0:r0 + a.shape[0], :], a).then_inc(par_in, 16)
        for t in range(TILES):
            act.dma_start(x_in[:, t, :], x_lat[t * P:(t + 1) * P, :] if t < 4 else x_ctx).then_inc(x_ld, 16)
        act.dma_start(rw[:, :, :], router_w.rearrange("(k p) n -> p k n", p=P)).then_inc(rw_in, 16)
        act.dma_start(rope_c, rope[0]).then_inc(rope_in, 16)
        act.dma_start(rope_s, rope[1]).then_inc(rope_in, 16)
        for n in range(WS):
            split_hi(act, n)
        act.wait_ge(par_rd, 1)
        nc.scalar.activation(sil[:, :], par[:, R_C:R_C + 16], ACT.Silu).then_inc(sil_rd, 1)
        act.wait_ge(lam_abs, 1)
        nc.scalar.activation(sm[:, S_EXP:S_EXP + 8], sm[:, S_ABS:S_ABS + 8], ACT.Exp, scale=-1.0).then_inc(lam_exp, 1)
        act.wait_ge(x_ld, 16 * TILES)
        for t in range(TILES):
            if t:
                act.wait_ge(x_sq, t)
            nc.scalar.activation(junk0, x_in[:, t, :], ACT.Square, accum_out=sm[:, S_SS + t:S_SS + t + 1]).then_inc(x_sq, 1)
        roots = [0]

        def root(at, n=TILES):
            roots[0] += 1
            act.wait_ge(root_in, roots[0])
            nc.scalar.activation(sm[:, at:at + n], sm[:, at:at + n], ACT.Sqrt).then_inc(root_out, 1)

        root(S_RSTD)
        for n in range(WS, N_WIN + WS):
            split_hi(act, n)
        act.wait_ge(col_ps, 4)
        for kind, w in ((0, lru_wa), (1, lru_wi)):
            for par_h in range(2):
                for d in range(2):
                    act.dma_start(gw[64 * par_h:64 * par_h + 64, kind, d, :, :],
                                  w[d, par_h::2].rearrange("h i j -> i h j")).then_inc(gw_in, 16)
        for kt in range(KT):
            act.wait_ge(h_tmp, kt + 1)
            nc.scalar.copy(hT_hi[:, kt, :], hT_tmp[:, kt % 2, :]).then_inc(h_hi, 1)

        def yl_out(ct):
            if ct == 0:
                win_ready(act, 0, CT - 1)
                act.wait_ge(h_lo, KT)
            nc.scalar.activation(gel[:, ct, 0:LAT], psum[ct][:, :], ACT.Gelu_apprx_tanh).then_inc(yl_ev, 1)
            nc.scalar.activation(gel[:, ct, LAT:], psum[4][:, ct * P:(ct + 1) * P], ACT.Gelu_apprx_tanh).then_inc(yl_ev, 1)

        def qk_ctx_out(i, dst, bank):
            win_ready(act, 2 + i, CT - 1)
            nc.scalar.copy(dst[:, :, LAT:], psum[bank][:, :].rearrange("p (h t) -> p h t", h=HEADS)).then_inc(qk_ctx, 1)

        def lru_gates_out(s):
            ct, d, ctxp = s // 4, s // 2 % 2, s % 2
            act.wait_ge(gt_ps, s + 1)
            if s % 4 == 0:
                if ct:
                    act.wait_ge(lr_done, ct)
                else:
                    act.wait_ge(xn_rd, TILES)
                    act.wait_ge(xT_ps, KT)
            for kind, dst, r0 in ((0, lr_r, R_BA), (1, lr_g, R_BI)):
                src = psum[6][:, kind * P:(kind + 1) * P] if ctxp else psum[6 + kind][:, :]
                at = slice(LAT, TOK) if ctxp else slice(0, LAT)
                nc.scalar.activation(dst[:, d, at], src, ACT.Sigmoid,
                                     bias=par[:, r0 + 4 * d + ct:r0 + 4 * d + ct + 1]).then_inc(gt_ev, 1)

        def lru_exp(ct):
            act.wait_ge(gt_ev, 8 * (ct + 1))
            if ct == 0:
                act.wait_ge(c8_rd, 1)
            for d in range(2):
                j = 4 * d + ct
                nc.scalar.activation(lr_a[:, d, :], lr_r[:, d, :], ACT.Exp, scale=sm[:, S_C8 + j:S_C8 + j + 1]).then_inc(lr_exp, 1)
                nc.scalar.activation(lr_t[:, d, :], lr_r[:, d, :], ACT.Tanh, scale=sm[:, S_NC8 + j:S_NC8 + j + 1]).then_inc(lr_exp, 1)

        def lru_sqrt(ct):
            act.wait_ge(lr_w, ct + 1)
            nc.scalar.activation(lr_t[:, :, :], lr_t[:, :, :], ACT.Sqrt).then_inc(lr_sq, 1)

        def lru_cat(ct):
            act.wait_ge(lr_done, ct + 1)
            if ct == 0:
                used(act, N_MID - 1)
            nc.scalar.copy(hT_hi[:, ct, :], gel[:, ct, :]).then_inc(cat_hi, 1)

        def tok_out(i, t):
            win_ready(act, 4 + i, t)
            bank = psum[t] if t < 4 else psum[4 + i]
            if i == 0:
                nc.scalar.copy(v_t[:, t, :], bank[:, :]).then_inc(v_ev, 1)
            else:
                if t == 0:
                    act.wait_ge(lr_done, CT)
                nc.scalar.activation(sg[:, t, :], bank[:, :], ACT.Silu).then_inc(g_ev, 1)

        for m in range(N_WIN, N_MID):
            bi, half = (m - N_WIN) // 2, m % 2
            ct = GATES_AT.get(m - N_WIN - 4)
            if ct is not None:
                for s in range(4 * ct, 4 * ct + 4):
                    lru_gates_out(s)
            split_hi(act, m + WS)
            if half:
                if bi == 0:
                    for u in range(CT):
                        yl_out(u)
                if bi in (2, 3):
                    qk_ctx_out(bi - 2, (qT, kT)[bi - 2], 4 + bi % 2)
                if bi == 4:
                    for t in range(TILES):
                        tok_out(0, t)
            if ct is not None:
                lru_exp(ct)
                lru_sqrt(ct)
        for t in range(TILES):
            tok_out(1, t)
        for ct in range(CT):
            lru_cat(ct)
        act.wait_ge(lst_ev, 1)
        act.dma_start(new_lru, lrow).then_inc(out_lru, 16)

        def ret_loads(h):
            if h == 0:
                act.wait_ge(lr_done, CT)
                act.wait_ge(rope_t, 2 * HEADS)
                act.wait_ge(qk_rd, 2 * HEADS)
            if h >= 2:
                act.wait_ge(sc_ev, 4 * (h - 1))
                act.wait_ge(scc_ev, h - 1)
                act.wait_ge(pv_ps, h - 1)
            act.dma_start(dec[:, h % 2, :], decay[h]).then_inc(dec_in[h % 2], 16)
            act.dma_start(s0[:, h % 2, :].rearrange("p (d e) -> p d e", d=2),
                          state_ret[:, h].rearrange("d k e -> k d e")).then_inc(dec_in[h % 2], 16)

        ret_loads(0)
        ret_loads(1)
        for h in range(HEADS):
            m0 = N_MID + 2 * h
            act.wait_ge(st_ps, h + 1)
            if h >= 1:
                act.wait_ge(out_ret, 32 * h)
            nc.scalar.copy(lst[:, 0:2 * DK], psum[6][:, P:3 * P]).then_inc(st_ev, 1)
            act.wait_ge(st_ev, h + 1)
            for d in range(2):
                act.dma_start(new_ret[d, h], lst[:, d * DK:(d + 1) * DK]).then_inc(out_ret, 16)
            if h + 2 < HEADS:
                ret_loads(h + 2)
            root(S_O)
            act.wait_ge(rt_ps, h + 1)
            nc.scalar.copy(hT_hi[:, 4 + h, 0:LAT], psum[7][:, :]).then_inc(rt_hi, 1)
            nc.scalar.copy(hT_hi[:, 4 + h, LAT:], psum[6][:, 0:P]).then_inc(rt_hi, 1)
            split_hi(act, m0 + WS)
            split_hi(act, m0 + 1 + WS)
        act.wait_ge(ret_o, HEADS)
        act.wait_ge(rt_ps, HEADS)
        act.wait_ge(kt_ps, HEADS)
        act.dma_start(mg1[4:5, :], ada_b[16:24, :].rearrange("(o a) b -> o (a b)", o=1)).then_inc(gbias1, 16)
        act.dma_start(post, norm_mix_post.partition_broadcast(P)).then_inc(post_in, 16)
        act.wait_ge(col_ps, 8)
        act.wait_ge(out_ret, 32 * HEADS)
        act.wait_ge(out_lru, 16)
        act.dma_start(rows[4:5, :], ada_b[40:48, :].rearrange("(o a) b -> o (a b)", o=1)).then_inc(gbias2, 16)
        for n in range(N_GATES + WS, N_WOUT + WS):
            split_hi(act, n)
        act.wait_ge(pv_ps, HEADS)
        act.wait_ge(st_ps, HEADS)
        for t in range(TILES):
            act.dma_start(xn2[:, t, :], x_lat[t * P:(t + 1) * P, :] if t < 4 else x_ctx).then_inc(x_re, 16)
        for n2 in range(2):
            for t in range(TILES):
                act.wait_ge(wo_ev, 5 * n2 + t + 1)
                if n2 or t:
                    act.wait_ge(wo_sq, 5 * n2 + t)
                nc.scalar.activation(junk[:, 0:512], x1[:, t, n2 * 512:(n2 + 1) * 512], ACT.Square,
                                     accum_out=sm[:, S_WO + 2 * t + n2:S_WO + 2 * t + n2 + 1]).then_inc(wo_sq, 1)
                if t in (1, 3):
                    split_hi(act, N_WOUT + WS + 2 * n2 + t // 2)
        root(S_T)
        for t in range(TILES):
            act.wait_ge(x1_rd, t + 1)
            if t:
                act.wait_ge(x1_sq, t)
            else:
                act.wait_ge(wo_sq, 2 * TILES)
            nc.scalar.activation(junk, x1[:, t, :], ACT.Square, accum_out=sm[:, S_X1 + t:S_X1 + t + 1]).then_inc(x1_sq, 1)
            if t:
                root(S_O + t - 1, 1)
        root(S_O + TILES - 1, 1)
        for t in range(TILES):
            act.wait_ge(h2_ps, 2 * t + 1)
            if t >= 2:
                act.wait_ge(lg_ps, t - 1)
            g = t // 4
            for j in range(4):
                nc.scalar.activation(h2T[:, t % 2, j, :], psum[2 * (t % 2)][:, j * P:(j + 1) * P], ACT.Identity,
                                     scale=aff[:, 1, g, j:j + 1], bias=modc[:, g, 16 + j:17 + j]).then_inc(h2_act, 1)
        act.wait_ge(lg_sub, 1)
        nc.scalar.activation(sm[:, 0:80], sm[:, 0:80], ACT.Exp).then_inc(lg_exp, 1)

        def gathered_half(e, pr2, hf):
            act.wait_ge(xs_f, 2 * e + (hf + 1))
            nc.scalar.copy(xs[pr2][0][:, 4 * hf:4 * hf + 4, :], xs_tmp[:, hf, :].rearrange("p (k s) -> p k s", k=4)).then_inc(xs_h, 1)

        gathered_half(0, 0, 0)
        gathered_half(0, 0, 1)

        def silu(n, e, b):
            used(act, n, e)
            nc.scalar.activation(sgl[0:SLOTS, b % 2, :], psum[b % 2][0:SLOTS, :], ACT.Silu).then_inc(sl_ev, 1)

        def hidT_hi(e, b):
            act.wait_ge(ht_ps, 4 * e + (b + 1))
            nc.scalar.copy(hidT[b % 2][0], psum[6][:, 0:4 * SLOTS]).then_inc(ht_hi, 1)

        def chunk_then(e, last, i):
            n = N_BODY + i + WS
            if not last or i + WS < 20:
                split_hi(act, n, e)

        split_hi(act, N_EXP + 3)
        split_hi(act, N_BODY)
        silu(N_EXP + 1, 0, 0)
        split_hi(act, N_BODY + 1)
        split_hi(act, N_BODY + 2)

        def body(e, pr2, last):
            for i, (kind, b, half, nxt) in enumerate(body_chunks(last)):
                chunk_then(e, last, i)
                if half and kind == "g":
                    silu(N_BODY + i, e, b)
                if kind == "g" and half and not nxt:
                    hidT_hi(e, b - 1)
                if kind == "u" and b == 1 and half:
                    act.wait_ge(oht_ps, e + 1)
                    nc.scalar.copy(onehotT[:, 0:LAT], psum[6][0:SLOTS, :]).then_inc(oht_ev, 1)
                    nc.scalar.copy(onehotT[:, LAT:], psum[7][0:SLOTS, 0:P]).then_inc(oht_ev, 1)
                    nc.scalar.copy(gate[0:SLOTS, :], psum[7][0:SLOTS, P:P + 1]).then_inc(oht_ev, 1)
                if not last and kind == "g" and b == 3 and half == 0:
                    gathered_half(e + 1, 1 - pr2, 0)
                if not last and kind == "d" and b == 2 and half == 0:
                    gathered_half(e + 1, 1 - pr2, 1)
                if kind == "d" and b == 2 and half:
                    hidT_hi(e, 3)
                if kind == "d" and b == 3 and half:
                    used(act, N_BODY + i, e)
                    for hf in range(2):
                        nc.scalar.activation(ye[0][:, hf * 512:(hf + 1) * 512], psum[4 + hf][0:SLOTS, :], ACT.Copy,
                                             scale=gate[0:SLOTS, 0:1]).then_inc(ye_h, 1)

        with act.Fori(0, LAST - 1, 2) as e:
            body(e, 0, False)
            body(e + 1, 1, False)
        body(LAST - 1, 0, False)
        body(LAST, 1, True)
        act.wait_ge(ye_l, 2 * NEXP)
        act.wait_ge(oh_rd, NEXP)
        act.wait_ge(ga_ps, 2 * NEXP)
        act.dma_start(post, norm_ffn_post.partition_broadcast(P)).then_inc(post_in, 16)
        for t in range(TILES):
            act.wait_ge(fs_add, 10 * LAST + 2 * t + 3)
            if t:
                act.wait_ge(fin_sq, t)
            else:
                act.wait_ge(x1_sq, TILES)
            nc.scalar.activation(xn2[:, 0, :], facc[:, t, :], ACT.Square, accum_out=sm[:, S_FIN + t:S_FIN + t + 1]).then_inc(fin_sq, 1)
        root(S_O)
        for t in range(TILES):
            act.wait_ge(fin_y, t + 1)
            act.dma_start(y_lat[t * P:(t + 1) * P, :] if t < 4 else y_ctx, facc[:, t, :]).then_inc(out_y, 16)


    @block.tensor
    def _(pe):
        mm, tr = nc.tensor.matmul, nc.tensor.transpose

        pe.wait_ge(const_in, 16)
        pe.wait_ge(par_in, 16 * 12)
        tr(psum[7][:, 0:R_N], par_rows[0:R_N, :], ident[0:R_N, 0:R_N]).then_inc(par_ps, 1)

        def ada_block(i, bank):
            for half in range(2):
                n = ada_chunk(i) + half
                chunk_ready(pe, n)
                wh, wl = chunk_view(w_hi, n, 512), chunk_view(w_lo, n, 512)
                for k in range(4):
                    kk = 4 * half + k
                    mm(psum[bank][0:66, :], cond[:, kk, :], wl[:, k, :], start=(kk == 0), stop=False)
                    last = mm(psum[bank][0:66, :], cond[:, kk, :], wh[:, k, :], start=False, stop=(kk == 7))
                last.then_inc(w_used, 1)

        def columns(i, bank, at):
            pe.wait_ge(ada_row, i + 1)
            for q in range(4):
                last = mm(psum[bank][:, at + 2 * q:at + 2 * q + 2], rows[0:4, q * P:(q + 1) * P], selc[0:4, :],
                          start=True, stop=True)
            last.then_inc(col_ps, 1)

        pe.wait_ge(cond_rd, 1)
        for i in range(4):
            if i:
                pe.wait_ge(ada_row, i)
            ada_block(i, 6)
            if i:
                if i >= 2:
                    pe.wait_ge(col_rd, i - 1)
                columns(i - 1, 7, 128)
        pe.wait_ge(col_rd, 3)
        columns(3, 7, 128)

        pe.wait_ge(xn_rd, TILES)
        for kt in range(KT):
            if kt >= 2:
                pe.wait_ge(h_tmp, kt - 1)
            for t in range(4):
                tr(psum[kt % 2][:, t * P:(t + 1) * P], x_in[:, t, kt * P:(kt + 1) * P], ident)
            tr(psum[2 + kt % 2][:, 0:P], x_in[:, 4, kt * P:(kt + 1) * P], ident).then_inc(xT_ps, 1)

        def lru_gates(s):
            ct, d, ctxp = s // 4, s // 2 % 2, s % 2
            if s:
                pe.wait_ge(gt_ev, 2 * s)
            else:
                pe.wait_ge(col_rd, 4)
                pe.wait_ge(gw_in, 16 * 8)
            pe.wait_ge(xl_ev, ct + 1)
            for kind in range(2):
                for hh in (slice(0, 64), slice(64, 128)):
                    dst = psum[6][hh, kind * P:(kind + 1) * P] if ctxp else psum[6 + kind][hh, :]
                    src = xc[hh, ct, LAT:] if ctxp else xc[hh, ct, 0:LAT]
                    last = mm(dst, gw[hh, kind, d, ct, :], src, start=True, stop=True)
            last.then_inc(gt_ps, 1)

        def bank_free(bi, u):
            if bi == 0:
                pe.wait_ge(h_tmp, KT)
            elif bi == 1:
                pe.wait_ge(yl_ev, 2 * (u + 1))
            elif bi == 2:
                pe.wait_ge(xl_ev, u + 1)
                if u == 0:
                    pe.wait_ge(yl_ev, 2 * CT)
            elif bi == 3:
                pe.wait_ge(rope_t, u + 1)
                if u == 0:
                    pe.wait_ge(xl_ev, CT)
            elif bi == 4:
                pe.wait_ge(rope_t, HEADS + u + 1) if u < 4 else pe.wait_ge(qk_ctx, 1)
            else:
                pe.wait_ge(v_ev, u + 1) if u < 4 else pe.wait_ge(qk_ctx, 2)

        for n in range(N_WIN, N_MID):
            bi, half = (n - N_WIN) // 2, n % 2
            chunk_ready(pe, n)
            pe.wait_ge(h_lo, 4 * (half + 1) if bi == 0 else KT)
            wh, wl = chunk_view(w_hi, n, 512), chunk_view(w_lo, n, 512)
            units = CT if bi < 4 else TILES
            for u in range(units):
                if half == 0:
                    bank_free(bi, u)
                for k in range(4):
                    kk = 4 * half + k
                    first, final = kk == 0, kk == 7
                    if bi < 4:
                        a, b = wh[:, k, u * P:(u + 1) * P], wl[:, k, u * P:(u + 1) * P]
                        three(psum[u][:, :], a, b, hT_hi[:, kk, 0:LAT], hT_lo[:, kk, 0:LAT], first, final)
                        last = three(psum[4 + bi % 2][:, u * P:(u + 1) * P], a, b, hT_hi[:, kk, LAT:], hT_lo[:, kk, LAT:],
                                     first and u == 0, final and u == 3, skip_group_check=True)
                    else:
                        at = slice(u * P, (u + 1) * P)
                        last = three(psum[u if u < 4 else bi][:, :], hT_hi[:, kk, at], hT_lo[:, kk, at],
                                     wh[:, k, :], wl[:, k, :], first, final)
                if u == units - 1:
                    last.then_inc(w_used, 1)
                elif half:
                    last.then_inc(win_ps, 1)
                if n - N_WIN - 4 in GATES_AT and u < 4:
                    lru_gates(4 * GATES_AT[n - N_WIN - 4] + u)

        pe.wait_ge(lr_done, CT)
        pe.wait_ge(gt_ev, 32)
        tr(psum[6][0:8, 0:P], sm[:, S_ST:S_ST + 8], ident).then_inc(lst_ps, 1)

        for h in range(HEADS):
            hc = slice(h * DK, (h + 1) * DK)
            if h == 0:
                pe.wait_ge(qk_rd, 2 * HEADS)
                pe.wait_ge(qk_ctx, 2)
                pe.wait_ge(v_ev, TILES)
                pe.wait_ge(g_ev, TILES)
                pe.wait_ge(lst_ev, 1)
            else:
                pe.wait_ge(ada_row, 4 + h)
                pe.wait_ge(col_rd, 4 + h)
            for j in range(4):
                if j >= 2:
                    pe.wait_ge(sc_ev, 4 * h + j - 1)
                mm(psum[j % 2][:, :], kT[:, h, j * P:(j + 1) * P], qT[:, h, 0:LAT], start=True, stop=True).then_inc(sc_ps, 1)
                if j == 1:
                    pe.wait_ge(dec_in[h % 2], 32 * (h // 2 + 1))
                    for t in range(4):
                        mm(psum[3 + t // 2][:, (t % 2) * 2 * DK:(t % 2 + 1) * 2 * DK], qT[:, h, t * P:(t + 1) * P],
                           s0[:, h % 2, :], start=True, stop=True)
            mm(psum[5][:, 0:P], kT[:, h, LAT:], qT[:, h, LAT:], start=True, stop=True).then_inc(scc_ps, 1)
            if h:
                pe.wait_ge(st_ev, h)
                pe.wait_ge(rt_lo, 2 * h)
            tr(psum[6][:, 3 * P:], kT[:, h, LAT:], ident).then_inc(kt_ps, 1)
            pe.wait_ge(scc_ev, h + 1)
            mm(psum[5][:, P:2 * P], sc_c, v_t[:, 4, hc], start=True, stop=True)
            pe.wait_ge(sc_ev, 4 * h + 4)
            for t in range(4):
                for j in range(4):
                    last = mm(psum[2][:, t * DK:(t + 1) * DK], sc[:, j, t * P:(t + 1) * P], v_t[:, j, hc],
                              start=(j == 0), stop=(j == 3))
            last.then_inc(pv_ps, 1)
            pe.wait_ge(kz_ev, h + 1)
            for d in range(2):
                last = mm(psum[6][:, (1 + d) * P:(2 + d) * P], kz[:, d, :], v_t[:, 4, hc], start=True, stop=True)
            last.then_inc(st_ps, 1)
            ada_block(4 + h, 0)
            columns(4 + h, 1, 0)
            pe.wait_ge(ret_o, h + 1)
            pe.wait_ge(st_ev, h + 1)
            for t in range(4):
                tr(psum[7][:, t * P:(t + 1) * P], ro_t[:, t, :], ident)
            tr(psum[6][:, 0:P], ro_t[:, 4, :], ident).then_inc(rt_ps, 1)

        pe.wait_ge(col_rd, 8)
        gate_banks = (2, 3, 5, 6)

        def gate_rows(src):
            for g in range(2):
                for half in range(2):
                    mm(psum[gate_banks[2 * g + half]][:, :], selb[0:5, g, :], src[0:5, half * 512:(half + 1) * 512],
                       start=True, stop=True).then_inc(gr_ps, 1)

        for i in range(8, 12):
            pe.wait_ge(ada_row, i if i < 10 else i - 1)
            ada_block(i, i % 2)
        pe.wait_ge(rt_lo, 2 * HEADS)
        pe.wait_ge(st_ev, HEADS)
        pe.wait_ge(ada_row, 12)
        pe.wait_ge(gbias1, 16)
        gate_rows(mg1)

        pe.wait_ge(cat_lo, CT)
        for n in range(N_WOUT, N_EXP):
            n2, half = (n - N_WOUT) // 2, n % 2
            chunk_ready(pe, n)
            wh, wl = chunk_view(w_hi, n, 512), chunk_view(w_lo, n, 512)
            for t in range(TILES):
                if half == 0 and n2 == 0 and t == 2:
                    pe.wait_ge(gr_ev, 4)
                if half == 0 and n2:
                    pe.wait_ge(wo_ev, t + 1)
                at = slice(t * P, (t + 1) * P)
                for k in range(4):
                    kk = 4 * half + k
                    last = three(psum[t][:, :], hT_hi[:, kk, at], hT_lo[:, kk, at], wh[:, k, :], wl[:, k, :], kk == 0, kk == 7)
                if t == TILES - 1:
                    last.then_inc(w_used, 1)
                elif half:
                    last.then_inc(wo_ps, 1)

        pe.wait_ge(rw_in, 16)

        def logits(t):
            pe.wait_ge(h2_act, 4 * (t + 1))
            pe.wait_ge(h2_dve, t + 1)
            for k in range(KT):
                last = mm(psum[4][:, t * NEXP:(t + 1) * NEXP], h2T[:, t % 2, k, :], rw[:, k, :], start=(k == 0), stop=(k == 7))
            last.then_inc(lg_ps, 1)

        pe.wait_ge(wo_ev, 2 * TILES)
        for t in range(TILES):
            pe.wait_ge(xn2_rd, t + 1)
            if t >= 2:
                pe.wait_ge(h2_act, 4 * (t - 1))
                pe.wait_ge(h2_dve, t - 1)
            for k in range(KT):
                last = tr(psum[2 * (t % 2) + k // 4][:, (k % 4) * P:(k % 4 + 1) * P], xn2[:, t, k * P:(k + 1) * P], ident)
                if k % 4 == 3:
                    last.then_inc(h2_ps, 1)
            if t:
                logits(t - 1)
        logits(TILES - 1)
        pe.wait_ge(pr_rd, 1)
        for t in range(TILES):
            dst = psum[5][0:NEXP, t * P:(t + 1) * P] if t < 4 else psum[6][0:NEXP, 0:P]
            last = tr(dst, sp[:, t, 0, :], ident)
        last.then_inc(pt_ps, 1)
        pe.wait_ge(sl_rd, 1)
        for t in range(TILES):
            last = tr(psum[7][:, t * NEXP:(t + 1) * NEXP], pS[0:NEXP, t * P:(t + 1) * P], ident[0:NEXP, 0:NEXP])
        last.then_inc(sl_ps, 1)

        def gather(hf):
            for k in range(4):
                for t in range(TILES):
                    last = mm(psum[7][:, k * SLOTS:(k + 1) * SLOTS], xn2[:, t, (4 * hf + k) * P:(4 * hf + k + 1) * P],
                              oneh[:, t, :], start=(t == 0), stop=(t == 4))
            last.then_inc(ga_ps, 1)

        def up_or_gate(n, e, bank, half, x):
            chunk_ready(pe, n, e)
            wh, wl = chunk_view(w_hi, n, 512), chunk_view(w_lo, n, 512)
            for k in range(4):
                kk = 4 * half + k
                last = three(psum[bank][0:SLOTS, :], x[0][:, kk, :], x[1][:, kk, :], wh[:, k, :], wl[:, k, :], kk == 0, kk == 7)
            last.then_inc(w_used, 1)

        def down(n, e, b, half):
            chunk_ready(pe, n, e)
            wh, wl = chunk_view(w_hi, n, D), chunk_view(w_lo, n, D)
            for j in range(2):
                jj = 2 * half + j
                x = [a[:, jj * SLOTS:(jj + 1) * SLOTS] for a in hidT[b % 2]]
                for q in range(2):
                    at = slice(q * 512, (q + 1) * 512)
                    last = three(psum[4 + q][0:SLOTS, :], x[0], x[1], wh[:, j, at], wl[:, j, at],
                                 b == 0 and jj == 0, b == 3 and jj == 3)
            last.then_inc(w_used, 1)

        def hid_T(e, b):
            pe.wait_ge(hid_rd, 4 * e + (b + 1))
            hb = hid[0:SLOTS, b % 2, :].rearrange("s (p j) -> s j p", j=4)
            for j in range(4):
                last = tr(psum[6][:, j * SLOTS:(j + 1) * SLOTS], hb[:, j, :], ident[0:SLOTS, 0:SLOTS])
            last.then_inc(ht_ps, 1)

        pe.wait_ge(oh_rd, 1)
        gather(0)
        pe.wait_ge(xs_f, 1)
        gather(1)
        pe.wait_ge(xs_l, 2)
        for i in range(4):
            up_or_gate(N_EXP + i, 0, 0 if i < 2 else 2, i % 2, xs[0])

        def body(e, pr2, last):
            for i, (kind, b, half, nxt) in enumerate(body_chunks(last)):
                n = N_BODY + i
                if kind in "gu":
                    if half == 0:
                        if kind == "g":
                            if nxt:
                                pe.wait_ge(xs_l, 2 * e + 4)
                            if b >= 2 or nxt:
                                pe.wait_ge(sl_ev, 4 * e + (b - 1 + 4 * nxt))
                        elif b >= 2 or nxt:
                            pe.wait_ge(hid_rd, 4 * e + (b - 1 + 4 * nxt))
                    up_or_gate(n, e, b % 2 + (2 if kind == "u" else 0), half, xs[1 - pr2 if nxt else pr2])
                else:
                    if half == 0:
                        pe.wait_ge(ht_lo, 4 * e + (b + 1))
                    down(n, e, b, half)
                if not half:
                    continue
                if kind == "g" and not nxt:
                    if b == 1:
                        pe.wait_ge(fs_add, 10 * e + 1)
                    else:
                        pe.wait_ge(ht_lo, 4 * e + (b - 1))
                        if b == 2:
                            pe.wait_ge(oht_ev, 3 * e + 3)
                    hid_T(e, b - 1)
                if kind == "u" and b == 1:
                    pe.wait_ge(ht_lo, 4 * e + 1)
                    for t in range(TILES):
                        dst = psum[6][0:SLOTS, t * P:(t + 1) * P] if t < 4 else psum[7][0:SLOTS, 0:P]
                        tr(dst, oneh[:, t, :], ident)
                    for t in range(TILES):
                        last_mm = mm(psum[7][0:SLOTS, P:P + 1], oneh[:, t, :], ecol[:, t, 0:1], start=(t == 0), stop=(t == 4))
                    last_mm.then_inc(oht_ps, 1)
                if not last and kind == "d" and b == 1:
                    pe.wait_ge(oht_ev, 3 * e + 3)
                    pe.wait_ge(oh_rd, e + 2)
                    gather(0)
                if not last and kind == "u" and b == 3:
                    pe.wait_ge(xs_f, 2 * e + 3)
                    gather(1)
                if kind == "d" and b == 2:
                    pe.wait_ge(ht_lo, 4 * e + 3)
                    hid_T(e, 3)
            pe.wait_ge(ye_l, 2 * e + 2)
            if not last:
                pe.wait_ge(xs_f, 2 * e + 4)
            for i in range(2 * TILES):
                t, hf = i // 2, i % 2
                if i >= 4:
                    pe.wait_ge(fs_add, 10 * e + (i - 2))
                bank = (7, 6, 4, 5)[i % 4]
                at = slice(hf * 512, (hf + 1) * 512)
                mm(psum[bank][:, :], onehotT[:, t * P:(t + 1) * P], ye[1][:, at], start=True, stop=False)
                mm(psum[bank][:, :], onehotT[:, t * P:(t + 1) * P], ye[0][:, at], start=False, stop=True).then_inc(fs_ps, 1)

        with pe.Fori(0, LAST - 1, 2) as e:
            body(e, 0, False)
            body(e + 1, 1, False)
        body(LAST - 1, 0, False)
        body(LAST, 1, True)
        pe.wait_ge(gbias2, 16)
        pe.wait_ge(fs_add, 10 * NEXP + 1)
        gate_rows(rows)

    @block.vector
    def _(dve):
        tt, ts, stt, cp = nc.vector.tensor_tensor, nc.vector.tensor_scalar, nc.vector.scalar_tensor_tensor, nc.vector.tensor_copy
        steps = [0]

        def step(ins):
            steps[0] += 1
            ins.then_inc(dve_step, 1)
            dve.wait_ge(dve_step, steps[0])

        def bc(a, *shape):
            return a.unsqueeze(len(a.shape)).to_broadcast(list(a.shape) + list(shape))

        dve.wait_ge(par_ps, 1)
        cp(par[:, :], psum[7][:, 0:R_N]).then_inc(par_rd, 1)
        dve.wait_ge(par_rd, 1)
        lam = par[:, R_LAM:R_LAM + 8]
        stt(sm[:, S_ABS:S_ABS + 8], lam, -1.0, lam, ALU.mult, ALU.max).then_inc(lam_abs, 1)
        dve.wait_ge(sil_rd, 1)
        dve.wait_ge(cond_0, 1)
        sil2 = sil[:, :].rearrange("p (g k) -> p k g", g=2)
        parts = cond[:, :, 0:4].rearrange("p k (g a) -> p k g a", a=2)
        step(cp(parts[:, :, :, 0], sil2))
        tt(parts[:, :, :, 1], sil2, parts[:, :, :, 0], ALU.subtract).then_inc(cond_rd, 1)
        for n in range(WS):
            split_lo(dve, "dve", n)
        dve.wait_ge(lam_exp, 1)
        u, s, s2, q = (sm[:, a:a + 8] for a in (S_EXP, 16, S_T, S_T + 8))
        step(ts(s, u, 2.0, None, ALU.add))
        step(nc.vector.reciprocal(s, s))
        step(tt(s, s, u, ALU.mult))
        step(tt(s2, s, s, ALU.mult))
        step(ts(q, s2, 1.0 / 17, None, ALU.mult))
        for k in (15, 13, 11, 9, 7, 5, 3):
            step(stt(q, q, 1.0 / k, s2, ALU.add, ALU.mult))
        step(stt(q, q, 1.0, s, ALU.add, ALU.mult))
        step(ts(s2, lam, -1.0, 0.0, ALU.mult, ALU.max))
        step(stt(s, q, 2.0, s2, ALU.mult, ALU.add))
        ts(sm[:, S_C8:S_C8 + 8], s, -8.0, None, ALU.mult)
        ts(sm[:, S_NC8:S_NC8 + 8], s, 8.0, None, ALU.mult).then_inc(c8_rd, 1)

        def rstd(dst, src, n):
            rstd_start(dst, src, n)
            roots[1] += 1
            dve.wait_ge(root_out, roots[1])

        roots = [0, 0]

        def rstd_start(dst, src, n):
            step(ts(dst, src, 1.0 / n, EPS, ALU.mult, ALU.add))
            nc.vector.reciprocal(dst, dst).then_inc(root_in, 1)
            roots[0] += 1

        dve.wait_ge(x_sq, TILES)
        rstd(sm[:, S_RSTD:S_RSTD + TILES], sm[:, S_SS:S_SS + TILES], D)
        for t in range(TILES):
            ts(x_in[:, t, :], x_in[:, t, :], sm[:, S_RSTD + t:S_RSTD + t + 1], None, ALU.mult).then_inc(xn_rd, 1)

        def row_copy(i, bank, dst):
            used(dve, ada_chunk(i) + 1)
            if 1 <= i < 9:
                dve.wait_ge(col_ps, i)
            cp(dst[0:4, :], psum[bank][0:4, :]).then_inc(ada_row, 1)

        def col_out(i, bank, at):
            dve.wait_ge(col_ps, i + 1)
            tt(modc[:, :, 4 * i:4 * i + 4], psum[bank][:, at:at + 8].rearrange("p (q g) -> p g q", g=2),
               par[:, R_ADAB + 4 * i:R_ADAB + 4 * i + 4].unsqueeze(1).to_broadcast([P, 2, 4]), ALU.add).then_inc(col_rd, 1)

        for m in range(N_WIN):
            split_lo(dve, "dve", m + WS)
            if m % 2:
                row_copy(m // 2, 6, rows[:, 0:512])
            elif m >= 4:
                col_out(m // 2 - 2, 7, 128)
        col_out(2, 7, 128)
        col_out(3, 7, 128)
        dve.wait_ge(col_rd, 4)
        for g in range(2):
            step(stt(aff[:, 0, g, :], modc[:, g, 8:16], 1.0, par[:, R_PRE:R_PRE + 8], ALU.add, ALU.mult))

        def h_low(kt):
            dve.wait_ge(h_hi, kt + 1)
            tt(hT_lo[:, kt, :], hT_tmp[:, kt % 2, :], hT_hi[:, kt, :], ALU.subtract).then_inc(h_lo, 1)

        for kt in range(KT):
            dve.wait_ge(xT_ps, kt + 1)
            if kt >= 2:
                dve.wait_ge(h_lo, kt - 1)
            ts(hT_tmp[:, kt % 2, 0:LAT], psum[kt % 2][:, :], aff[:, 0, 0, kt:kt + 1], modc[:, 0, kt:kt + 1], ALU.mult, ALU.add)
            ts(hT_tmp[:, kt % 2, LAT:], psum[2 + kt % 2][:, 0:P], aff[:, 0, 1, kt:kt + 1],
               modc[:, 1, kt:kt + 1], ALU.mult, ALU.add).then_inc(h_tmp, 1)
            if kt:
                h_low(kt - 1)
        h_low(KT - 1)

        def conv(ct):
            win_ready(dve, 1, ct)
            if ct == 0:
                win_ready(dve, 1, CT - 1)
            w = [par[:, R_CW + 4 * tap + ct:R_CW + 4 * tap + ct + 1] for tap in range(4)]
            parts = ((psum[ct][:, :], xc[:, ct, 0:LAT]), (psum[5][:, ct * P:(ct + 1) * P], xc[:, ct, LAT:]))
            for src, dst in parts:
                last = ts(dst, src, w[2], par[:, R_CB + ct:R_CB + ct + 1], ALU.mult, ALU.add)
            step(last)
            for tap, lo, hi in ((0, 2, 0), (1, 1, 0), (3, 0, 1)):
                for src, dst in parts:
                    n = dst.shape[1]
                    a, b = slice(lo, n - hi), slice(hi, n - lo)
                    last = stt(dst[:, a], src[:, b], w[tap], dst[:, a], ALU.mult, ALU.add)
                if tap < 3:
                    step(last)
            last.then_inc(xl_ev, 1)

        def rope_terms(i, dst, h):
            n = 4 * i + h
            win_ready(dve, 2 + i, h)
            if n == 0:
                dve.wait_ge(rope_in, 32)
            if n >= 2:
                dve.wait_ge(qk_rd, n - 1)
            tt(dst[:, h, 0:LAT], psum[h][:, :], rope_c, ALU.mult)
            tt(rope_tmp[0:64, n % 2, :], psum[h][64:128, :], rope_s[64:128, :], ALU.mult)
            tt(rope_tmp[64:128, n % 2, :], psum[h][0:64, :], rope_s[0:64, :], ALU.mult).then_inc(rope_t, 1)

        def lru(ct):
            dve.wait_ge(lr_exp, 4 * (ct + 1))
            step(tt(lr_r, lr_a, lr_a, ALU.mult))
            stt(lr_t, lr_r, 1.0, lr_t, ALU.add, ALU.mult).then_inc(lr_w, 1)
            dve.wait_ge(lr_sq, ct + 1)
            dve.wait_ge(lr_gx, ct + 1)
            step(tt(lr_t, lr_t, lr_g, ALU.mult))
            for d, h0 in ((0, par[:, R_H0 + ct:R_H0 + ct + 1]), (1, par[:, R_H0 + 4 + ct:R_H0 + 5 + ct])):
                for lo, n, init in ((0, LAT, h0), (LAT, CTX, 0.0)):
                    o, a, b = (x[:, d, lo:lo + n] for x in (lr_r, lr_a, lr_t))
                    if d:
                        o, a, b = o[:, ::-1], a[:, ::-1], b[:, ::-1]
                    last = nc.vector.tensor_tensor_scan(o, a, b, init, ALU.mult, ALU.add)
            step(last)
            cp(sm[:, S_ST + ct:S_ST + ct + 1], lr_r[:, 0, TOK - 1:TOK])
            step(cp(sm[:, S_ST + 4 + ct:S_ST + 5 + ct], lr_r[:, 1, LAT:LAT + 1]))
            step(tt(lr_r[:, 0, :], lr_r[:, 0, :], lr_r[:, 1, :], ALU.add))
            dve.wait_ge(yl_ev, 2 * (ct + 1))
            tt(gel[:, ct, :], gel[:, ct, :], lr_r[:, 0, :], ALU.mult).then_inc(lr_done, 1)

        for m in range(N_WIN, N_MID):
            bi, half = (m - N_WIN) // 2, m % 2
            split_lo(dve, "dve", m + WS)
            if half and bi in (1, 2, 3):
                for ct in range(CT):
                    conv(ct) if bi == 1 else rope_terms(bi - 2, (qT, kT)[bi - 2], ct)
            if m - N_WIN - 4 in GATES_AT:
                lru(GATES_AT[m - N_WIN - 4])
        dve.wait_ge(lst_ps, 1)
        cp(lrow, psum[6][0:8, 0:P]).then_inc(lst_ev, 1)
        for ct in range(CT):
            dve.wait_ge(cat_hi, ct + 1)
            tt(hT_lo[:, ct, :], gel[:, ct, :], hT_hi[:, ct, :], ALU.subtract).then_inc(cat_lo, 1)

        for h in range(HEADS):
            hc = slice(h * DK, (h + 1) * DK)
            m0 = N_MID + 2 * h
            dve.wait_ge(dec_in[h % 2], 32 * (h // 2 + 1))
            for j in range(4):
                dve.wait_ge(sc_ps, 4 * h + j + 1)
                tt(sc[:, j, :], psum[j % 2][:, :], dec[:, h % 2, 384 - P * j:896 - P * j], ALU.mult).then_inc(sc_ev, 1)
            dve.wait_ge(scc_ps, h + 1)
            tt(sc_c, psum[5][:, 0:P], dec[:, h % 2, 384:512], ALU.mult).then_inc(scc_ev, 1)
            dve.wait_ge(kt_ps, h + 1)
            ts(kz[:, 0, :], psum[6][:, 3 * P:], zeta[:, h, 0:1], None, ALU.mult)
            ts(kz[:, 1, :], psum[6][:, 3 * P:], zeta[:, h, 1:2], None, ALU.mult).then_inc(kz_ev, 1)
            dve.wait_ge(pv_ps, h + 1)
            cp(o_t[:, 4, :], psum[5][:, P:2 * P])
            for d in range(2):
                for t in range(4):
                    cross = psum[3 + t // 2][:, (t % 2) * 2 * DK + d * DK:(t % 2) * 2 * DK + (d + 1) * DK]
                    if d == 0:
                        last = ts(o_t[:, t, :], cross, xi[:, t, h, 0:1], None, ALU.mult)
                    else:
                        last = stt(o_t[:, t, :], cross, xi[:, t, h, 1:2], o_t[:, t, :], ALU.mult, ALU.add)
                step(last)
            step(tt(o_t[:, 0:4, :], o_t[:, 0:4, :], psum[2][:, :].rearrange("p (t e) -> p t e", t=4), ALU.add))
            if h:
                dve.wait_ge(rt_ps, h)
            step(tt(ro_t, o_t, o_t, ALU.mult))
            step(nc.vector.tensor_reduce(sm[:, S_O:S_O + TILES], ro_t, AX.X, ALU.add))
            rstd(sm[:, S_O:S_O + TILES], sm[:, S_O:S_O + TILES], DK)
            step(tt(ro_t, o_t, bc(sm[:, S_O:S_O + TILES], DK), ALU.mult))
            if h == 0:
                dve.wait_ge(g_ev, TILES)
            tt(ro_t, ro_t, sg[:, :, hc], ALU.mult).then_inc(ret_o, 1)
            row_copy(4 + h, 0, rows[:, 0:512])
            split_lo(dve, "dve", m0 + WS)
            split_lo(dve, "dve", m0 + 1 + WS)
            col_out(4 + h, 1, 0)
            dve.wait_ge(rt_hi, 2 * h + 2)
            tt(hT_lo[:, 4 + h, 0:LAT], psum[7][:, :], hT_hi[:, 4 + h, 0:LAT], ALU.subtract).then_inc(rt_lo, 1)
            tt(hT_lo[:, 4 + h, LAT:], psum[6][:, 0:P], hT_hi[:, 4 + h, LAT:], ALU.subtract).then_inc(rt_lo, 1)

        for i in range(8, 12):
            if i == 10:
                dve.wait_ge(out_ret, 32 * HEADS)
                dve.wait_ge(out_lru, 16)
            row_copy(i, i % 2, (mg1 if i < 10 else rows[:, :])[:, (i % 2) * 512:(i % 2 + 1) * 512])
            for n in (N_GATES + 2 * (i - 8) + WS, N_GATES + 2 * (i - 8) + 1 + WS):
                split_lo(dve, "dve", n)

        def gate_row(first, banks=(2, 3, 5, 6)):
            dve.wait_ge(post_in, 16 * (first // 4 + 1))
            for g in range(2):
                for half in range(2):
                    at = slice(half * 512, (half + 1) * 512)
                    dve.wait_ge(gr_ps, first + 2 * g + half + 1)
                    tt(g_row[:, g, at], psum[banks[2 * g + half]][:, :], post[:, at], ALU.mult).then_inc(gr_ev, 1)

        gate_row(0)
        dve.wait_ge(col_rd, 8)
        for g in range(2):
            step(stt(aff[:, 1, g, :], modc[:, g, 24:32], 1.0, par[:, R_FPRE:R_FPRE + 8], ALU.add, ALU.mult))
        for n2 in range(2):
            for t in range(TILES):
                wout_ready(dve, n2, t)
                cp(x1[:, t, n2 * 512:(n2 + 1) * 512], psum[t][:, :]).then_inc(wo_ev, 1)
                if t in (1, 3):
                    split_lo(dve, "dve", N_WOUT + WS + 2 * n2 + t // 2)
        dve.wait_ge(wo_sq, 2 * TILES)
        both = sm[:, S_WO:S_WO + 2 * TILES].rearrange("p (t n) -> p t n", n=2)
        dve.wait_ge(gr_ev, 4)
        dve.wait_ge(wo_ev, 2 * TILES)
        step(tt(sm[:, S_T:S_T + TILES], both[:, :, 0], both[:, :, 1], ALU.add))
        rstd(sm[:, S_T:S_T + TILES], sm[:, S_T:S_T + TILES], D)
        dve.wait_ge(x_re, 16 * TILES)

        def norm2_start(t):
            dve.wait_ge(x1_sq, t + 1)
            rstd_start(sm[:, S_O + t:S_O + t + 1], sm[:, S_X1 + t:S_X1 + t + 1], D)

        def normed2(t):
            roots[1] += 1
            dve.wait_ge(root_out, roots[1])
            ts(xn2[:, t, :], x1[:, t, :], sm[:, S_O + t:S_O + t + 1], None, ALU.mult).then_inc(xn2_rd, 1)

        for t in range(TILES):
            step(stt(x1[:, t, :], x1[:, t, :], sm[:, S_T + t:S_T + t + 1], g_row[:, t // 4, :], ALU.mult, ALU.mult))
            tt(x1[:, t, :], x1[:, t, :], xn2[:, t, :], ALU.add).then_inc(x1_rd, 1)
            if t >= 1:
                norm2_start(t - 1)
            if t >= 2:
                normed2(t - 2)
        norm2_start(TILES - 1)
        normed2(TILES - 2)
        normed2(TILES - 1)
        for t in range(TILES):
            dve.wait_ge(h2_ps, 2 * t + 2)
            if t >= 2:
                dve.wait_ge(lg_ps, t - 1)
            dst, g = h2T[:, t % 2, 4:8, :], t // 4
            step(tt(dst, psum[2 * (t % 2) + 1][:, :].rearrange("p (k t) -> p k t", k=4), bc(aff[:, 1, g, 4:8], P), ALU.mult))
            tt(dst, dst, bc(modc[:, g, 20:24], P), ALU.add).then_inc(h2_dve, 1)
        lg = psum[4][:, 0:TILES * NEXP].rearrange("p (t e) -> p t e", t=TILES)
        ex = sm[:, 0:TILES * NEXP].rearrange("p (t e) -> p t e", t=TILES)
        dve.wait_ge(lg_ps, TILES)
        step(nc.vector.tensor_reduce(sm[:, S_MAX:S_MAX + TILES], lg, AX.X, ALU.max))
        tt(ex, lg, bc(sm[:, S_MAX:S_MAX + TILES], NEXP), ALU.subtract).then_inc(lg_sub, 1)
        dve.wait_ge(lg_exp, 1)
        step(nc.vector.tensor_reduce(sm[:, S_SUM:S_SUM + TILES], ex, AX.X, ALU.add))
        step(nc.vector.reciprocal(sm[:, S_REC:S_REC + TILES], sm[:, S_SUM:S_SUM + TILES]))
        tt(sp[:, :, 0, :], ex, bc(sm[:, S_REC:S_REC + TILES], NEXP), ALU.mult).then_inc(pr_rd, 1)
        dve.wait_ge(pt_ps, 1)
        ex16 = slice(0, NEXP)
        cp(pW[ex16, 0:LAT], psum[5][ex16, :])
        step(cp(pW[ex16, LAT:], psum[6][ex16, 0:P]))
        m8 = sm[ex16, S_T:S_T + 8]
        for at, cap in ((slice(0, LAT), CAP_L), (slice(LAT, TOK), CAP_C)):
            for _ in range(cap // 8):
                step(nc.vector.max(m8, pW[ex16, at]))
                step(nc.vector.match_replace(pW[ex16, at], m8, pW[ex16, at], -1.0))
        nc.vector.memset(pC[ex16, :], 1.0)
        step(ts(pS[ex16, :], pW[ex16, :], 0.0, None, ALU.is_lt))
        for at in (slice(0, LAT), slice(LAT, TOK)):
            last = nc.vector.tensor_tensor_scan(pT[ex16, at], pC[ex16, at], pS[ex16, at], 0.0, ALU.mult, ALU.add)
        step(last)
        tt(pS[ex16, :], pS[ex16, :], pT[ex16, :], ALU.mult).then_inc(sl_rd, 1)
        dve.wait_ge(sl_ps, 1)
        step(cp(sp[:, :, 1, :], psum[7][:, 0:TILES * NEXP].rearrange("p (t e) -> p t e", t=TILES)))

        def onehot(e1, e):
            cp(ecol[:, :, :], sp[:, :, :, bass.ds(e1, 1)].rearrange("p t a o -> p t (a o)")).then_inc(ec_rd, 1)
            dve.wait_ge(ec_rd, e + 1) if not isinstance(e, int) or e else dve.wait_ge(ec_rd, 1)
            for t in range(TILES):
                last = ts(oneh[:, t, :], iota[:, t // 4, :], ecol[:, t, 1:2], None, ALU.is_equal)
            last.then_inc(oh_rd, 1)

        def gathered(e, hf):
            dve.wait_ge(ga_ps, 2 * e + (hf + 1))
            ps = psum[7][:, 0:4 * SLOTS].rearrange("p (k s) -> p k s", k=4)
            dst = xs_tmp[:, hf, :].rearrange("p (k s) -> p k s", k=4)
            k4 = slice(4 * hf, 4 * hf + 4)
            for g, at, n in ((0, slice(0, CAP_L), CAP_L), (1, slice(CAP_L, SLOTS), CAP_C)):
                last = tt(dst[:, :, at], ps[:, :, at], bc(aff[:, 1, g, k4], n), ALU.mult)
            last.then_inc(xs_m, 1)
            dve.wait_ge(xs_m, 2 * e + (hf + 1))
            for g, at, n in ((0, slice(0, CAP_L), CAP_L), (1, slice(CAP_L, SLOTS), CAP_C)):
                last = tt(dst[:, :, at], dst[:, :, at], bc(modc[:, g, 16 + 4 * hf:20 + 4 * hf], n), ALU.add)
            last.then_inc(xs_f, 1)

        def gathered_lo(e, pr2, hf):
            dve.wait_ge(xs_h, 2 * e + (hf + 1))
            k4 = slice(4 * hf, 4 * hf + 4)
            tt(xs[pr2][1][:, k4, :], xs_tmp[:, hf, :].rearrange("p (k s) -> p k s", k=4), xs[pr2][0][:, k4, :],
               ALU.subtract).then_inc(xs_l, 1)

        def hidden(n, e, b):
            used(dve, n, e)
            dve.wait_ge(sl_ev, 4 * e + (b + 1))
            tt(hid[0:SLOTS, b % 2, :], psum[2 + b % 2][0:SLOTS, :], sgl[0:SLOTS, b % 2, :], ALU.mult).then_inc(hid_rd, 1)

        def hidT_lo(e, b):
            dve.wait_ge(ht_hi, 4 * e + (b + 1))
            tt(hidT[b % 2][1], psum[6][:, 0:4 * SLOTS], hidT[b % 2][0], ALU.subtract).then_inc(ht_lo, 1)

        onehot(0, 0)
        gathered(0, 0)
        gathered(0, 1)
        gathered_lo(0, 0, 0)
        gathered_lo(0, 0, 1)
        split_lo(dve, "dve", N_EXP + 3)
        split_lo(dve, "dve", N_BODY)
        split_lo(dve, "dve", N_BODY + 1)
        split_lo(dve, "dve", N_BODY + 2)
        hidden(N_EXP + 3, 0, 0)
        nc.vector.memset(facc[:, 4, :], 0.0).then_inc(fs_add, 1)
        dve.wait_ge(fz, 1)
        dve.wait_ge(fs_add, 1)

        def body(e, pr2, last):
            chunks = body_chunks(last)
            for i, (kind, b, half, nxt) in enumerate(chunks):
                if not last or i + WS < len(chunks):
                    split_lo(dve, "dve", N_BODY + i + WS, e)
                if not last and kind == "g" and b == 3 and half == 0:
                    gathered(e + 1, 0)
                    gathered_lo(e + 1, 1 - pr2, 0)
                if not last and kind == "d" and b == 2 and half == 0:
                    gathered(e + 1, 1)
                    gathered_lo(e + 1, 1 - pr2, 1)
                if not half:
                    continue
                if kind == "g" and not nxt:
                    hidT_lo(e, b - 1)
                if kind == "u":
                    hidden(N_BODY + i, e, b) if not nxt else hidden_next(N_BODY + i, e)
                if kind == "u" and b == 1 and not last:
                    dve.wait_ge(oht_ps, e + 1)
                    onehot(e + 1, e + 1)
                if kind == "d" and b == 2:
                    hidT_lo(e, 3)
                if kind == "d" and b == 3:
                    for hf in range(2):
                        dve.wait_ge(ye_h, 2 * e + (hf + 1))
                        at = slice(hf * 512, (hf + 1) * 512)
                        stt(ye[1][:, at], psum[4 + hf][0:SLOTS, :], gate[0:SLOTS, 0:1], ye[0][:, at], ALU.mult,
                            ALU.subtract).then_inc(ye_l, 1)
            for i in range(2 * TILES):
                bank = (7, 6, 4, 5)[i % 4]
                dst = facc[:, i // 2, (i % 2) * 512:(i % 2 + 1) * 512]
                dve.wait_ge(fs_ps, 10 * e + (i + 1))
                tt(dst, dst, psum[bank][:, :], ALU.add).then_inc(fs_add, 1)

        def hidden_next(n, e):
            used(dve, n, e)
            dve.wait_ge(sl_ev, 4 * e + 5)
            tt(hid[0:SLOTS, 0, :], psum[2][0:SLOTS, :], sgl[0:SLOTS, 0, :], ALU.mult).then_inc(hid_rd, 1)

        with dve.Fori(0, LAST - 1, 2) as e:
            body(e, 0, False)
            body(e + 1, 1, False)
        body(LAST - 1, 0, False)
        body(LAST, 1, True)
        gate_row(4)
        dve.wait_ge(fin_sq, TILES)
        rstd(sm[:, S_O:S_O + TILES], sm[:, S_FIN:S_FIN + TILES], D)
        dve.wait_ge(gr_ev, 8)
        for t in range(TILES):
            step(stt(facc[:, t, :], facc[:, t, :], sm[:, S_O + t:S_O + t + 1], g_row[:, t // 4, :], ALU.mult, ALU.mult))
            tt(facc[:, t, :], facc[:, t, :], x1[:, t, :], ALU.add).then_inc(fin_y, 1)

    @block.gpsimd
    def _(pool):
        nc.gpsimd.memset(cond[:, :, :].bitcast(F32), 0.0).then_inc(cond_0, 1)
        for n in range(WS):
            split_lo(pool, "pool", n)
        for m in range(N_WIN):
            split_lo(pool, "pool", m + WS)
        for m in range(N_WIN, N_MID):
            bi, half = (m - N_WIN) // 2, m % 2
            split_lo(pool, "pool", m + WS)
            if half and bi in (2, 3):
                for h in range(HEADS):
                    pool.wait_ge(rope_t, 4 * (bi - 2) + h + 1)
                    dst = (qT, kT)[bi - 2][:, h, 0:LAT]
                    nc.gpsimd.tensor_tensor(dst, dst, rope_tmp[:, h % 2, :], ALU.add).then_inc(qk_rd, 1)
            if m - N_WIN - 4 in GATES_AT:
                ct = GATES_AT[m - N_WIN - 4]
                pool.wait_ge(gt_ev, 8 * (ct + 1))
                nc.gpsimd.tensor_tensor(lr_g, lr_g, xc[:, ct, :].unsqueeze(1).to_broadcast([P, 2, TOK]), ALU.mult).then_inc(lr_gx, 1)
        for n in range(N_MID + WS, N_EXP + WS):
            split_lo(pool, "pool", n)
        pool.wait_ge(sl_ps, 1)
        nc.gpsimd.memset(facc[:, 0:4, :], 0.0).then_inc(fz, 1)
        for n in range(N_EXP + WS, N_BODY + WS):
            split_lo(pool, "pool", n)

        def body(e, last):
            for i in range(20 if last else PER_E):
                if not last or i + WS < 20:
                    split_lo(pool, "pool", N_BODY + i + WS, e)

        with pool.Fori(0, LAST) as e:
            body(e, False)
        body(LAST, True)

    ctx.close()


def tables():
    import numpy as np

    f = np.float64
    dec_f = np.log1p(-np.exp2(-(5.0 + np.arange(HEADS, dtype=f))))
    dec_b = np.log1p(-np.exp2(-(5.5 + np.arange(HEADS, dtype=f))))
    scale = DK ** -0.5
    diff = np.arange(896)[None, :] - 384 - np.arange(P)[:, None]
    decay = np.where(diff >= 0, np.exp(np.maximum(diff, 0) * dec_f[:, None, None]),
                     np.exp(np.maximum(-diff, 0) * dec_b[:, None, None])) * scale
    pos = np.arange(LAT, dtype=f).reshape(4, P)
    xi = np.stack([np.exp((pos[..., None] + 1) * dec_f), np.exp((LAT - pos[..., None]) * dec_b)], -1) * scale
    j = np.arange(CTX, dtype=f)[:, None]
    zeta = np.stack([np.exp((CTX - 1 - j) * dec_f), np.exp(j * dec_b)], -1)
    const = np.zeros((P, C_N))
    const[:, C_ID:C_ID + P] = np.eye(P)
    const[:, C_XI:C_XI + 32] = xi.transpose(1, 0, 2, 3).reshape(P, 32)
    const[:, C_ZETA:C_ZETA + 8] = zeta.reshape(P, 8)
    const[:, C_IOTA:C_IOTA + 2 * SLOTS] = np.concatenate(
        [np.arange(1, CAP_L + 1), np.full(CAP_C, -1), np.full(CAP_L, -1), np.arange(1, CAP_C + 1)])
    const[0:4, C_SELC:C_SELC + 2] = [[1, 0], [1, 0], [0, 1], [0, 1]]
    selb = const[:, C_SELB:C_SELB + 2 * P].reshape(P, 2, P)
    for g in range(2):
        selb[2 * g:2 * g + 2, g, :] = 1
        selb[4, g, :] = 1
    const[:, C_SELB:C_SELB + 2 * P] = selb.reshape(P, 2 * P)
    grid = np.float32(64)
    row, col = np.arange(LAT) // 64, np.arange(LAT) % 64
    nf = DK // 4
    freqs = 10000.0 ** (-np.arange(nf, dtype=f) / nf)
    ang = np.concatenate([row[:, None] * freqs, col[:, None] * freqs], -1).T
    rope = np.stack([np.concatenate([np.cos(ang)] * 2), np.concatenate([np.sin(ang), -np.sin(ang)])])
    return {"consts": const.astype(np.float32), "decay": decay.astype(np.float32), "rope": rope.astype(np.float32)}


def kernel(x_prompt, x_sample, c, state_lru, state_ret, c_ctx, ada_w, ada_b, norm_mix_pre, norm_mix_post,
           norm_ffn_pre, norm_ffn_post, w_in, conv_w, conv_b, lru_wa, lru_ba, lru_wi, lru_bi, lru_lambda,
           w_out, router_w, exp_w_gate, exp_w_up, exp_w_down):
    import numpy as np
    import concourse.bacc as bacc
    from concourse.bass_utils import run_bass_kernel_spmd

    ins = {
        "x_ctx": x_prompt[0], "x_lat": x_sample[0], "c": c.reshape(8, P), "state_lru": state_lru.reshape(8, P),
        "state_ret": state_ret.reshape(2, HEADS, DK, DK), "c_ctx": c_ctx.reshape(8, P), "ada_w": ada_w[0],
        "ada_b": ada_b.reshape(48, P), "norm_mix_pre": norm_mix_pre.reshape(8, P), "norm_mix_post": norm_mix_post[0],
        "norm_ffn_pre": norm_ffn_pre.reshape(8, P), "norm_ffn_post": norm_ffn_post[0], "w_in": w_in[0],
        "conv_w": conv_w.reshape(16, P), "conv_b": conv_b.reshape(4, P), "lru_wa": lru_wa[0], "lru_ba": lru_ba.reshape(8, P),
        "lru_wi": lru_wi[0], "lru_bi": lru_bi.reshape(8, P), "lru_lambda": lru_lambda.reshape(8, P), "w_out": w_out[0],
        "router_w": router_w[0], "exp_gate": exp_w_gate[0], "exp_up": exp_w_up[0], "exp_down": exp_w_down[0],
        **tables(),
    }
    outs = {"y_ctx": (CTX, D), "y_lat": (LAT, D), "new_lru": (8, P), "new_ret": (2, HEADS, DK, DK)}
    nc = bacc.Bacc("TRN2", target_bir_lowering=False, num_devices=1)
    arrays, args = {}, {}
    for name, a in ins.items():
        arrays[f"in_{name}"] = np.ascontiguousarray(a)
        args[name] = nc.dram_tensor(f"in_{name}", a.shape, F32, kind="ExternalInput").ap()
    for name, shape in outs.items():
        args[name] = nc.dram_tensor(f"out_{name}", shape, F32, kind="ExternalOutput").ap()
    build(nc, **args)
    r = run_bass_kernel_spmd(nc, [arrays], core_ids=[0]).results[0]
    return (r["out_y_ctx"].reshape(1, CTX, D), r["out_y_lat"].reshape(1, LAT, D),
            r["out_new_lru"].reshape(1, 1, 2, LW), r["out_new_ret"].reshape(1, 1, 2, HEADS, DK, DK))
```

```python
from contextlib import ExitStack

import concourse.bass as bass
from concourse import mybir

F32 = mybir.dt.float32
F32R = mybir.dt.float32r
ALU = mybir.AluOpType
ACT = mybir.ActivationFunctionType
AX = mybir.AxisListType

P = 128
D = 1024
KT = D // P
LAT, CTX = 512, 128
TOK = LAT + CTX
TILES = TOK // P
LW = 512
CT = LW // P
HEADS, DK = 4, 128
NEXP = 16
CAP_L, CAP_C = 2 * LAT // NEXP, 2 * CTX // NEXP
SLOTS = CAP_L + CAP_C
FF = 2 * D
NB = FF // 512
EPS = 1e-6

RAW, WS = 4, 3
CH = 2048

ADA_FIRST = [0, 1, 2, 3]
WIN = [1, 0, 2, 3, 4, 5]
ADA_MID = [6, 7, 8, 9]
ADA_GATES = [4, 5, 10, 11]
N_WIN = 2 * len(ADA_FIRST)
N_MID = N_WIN + 2 * len(WIN)
N_GATES = N_MID + 2 * len(ADA_MID)
N_WOUT = N_GATES + 2 * len(ADA_GATES)
N_EXP = N_WOUT + 4
PER_E = 24
N_BODY = N_EXP + 6
DVE_COLS = 1536

S_ABS, S_EXP, S_C8, S_NC8, S_SS, S_RSTD, S_WO, S_X1 = 0, 8, 24, 32, 40, 58, 48, 64
S_FIN, S_MAX, S_SUM, S_REC, S_T, S_ST, S_O = 80, 88, 93, 98, 104, 112, 120
GATES_AT = {0: 0, 2: 1, 4: 2, 6: 3}
C_ID, C_XI, C_ZETA, C_IOTA, C_SELC, C_SELB = 0, 128, 160, 168, 328, 330
C_N = 586
R_C, R_PRE, R_FPRE, R_CW, R_CB, R_BA, R_BI, R_LAM, R_H0, R_ADAB = 0, 16, 24, 32, 48, 52, 60, 68, 76, 84
R_N = 116


def build(nc, x_ctx, x_lat, c, state_lru, state_ret, c_ctx, ada_w, ada_b, norm_mix_pre, norm_mix_post,
          norm_ffn_pre, norm_ffn_post, w_in, conv_w, conv_b, lru_wa, lru_ba, lru_wi, lru_bi, lru_lambda,
          w_out, router_w, exp_gate, exp_up, exp_down, consts, decay, rope, y_ctx, y_lat, new_lru, new_ret):
    ctx = ExitStack()
    sb = lambda n, s, d=F32: ctx.enter_context(nc.sbuf_tensor(n, s, d))
    sem = lambda n: ctx.enter_context(nc.semaphore(n))

    raw = sb("raw", [P, RAW, CH])
    w_hi = sb("w_hi", [P, WS, CH], F32R)
    w_lo = sb("w_lo", [P, WS, CH], F32R)
    act_hi = sb("act_hi", [P, KT * TOK], F32R)
    act_lo = sb("act_lo", [P, KT * TOK], F32R)
    arena = sb("arena", [P, 18944])
    const = sb("const", [P, C_N])
    rows = sb("rows", [P, D])
    cond = sb("cond", [P, KT, 66], F32R)
    par = sb("par", [P, R_N])
    sil = sb("sil", [P, 16])
    modc = sb("modc", [P, 2, 32])
    aff = sb("aff", [P, 2, 2, KT])
    rw = sb("rw", [P, KT, NEXP])
    sp = sb("sp", [P, TILES, 2, NEXP])
    ecol = sb("ecol", [P, TILES, 2])
    gate = sb("gate", [P, 1])
    sm = sb("sm", [P, 128])
    psum = [ctx.enter_context(nc.psum_tensor(f"bank{i}", [P, 512], F32)) for i in range(8)]

    def region(at, *shape):
        n = 1
        for s in shape:
            n *= s
        v = arena[:, at:at + n]
        if len(shape) == 1:
            return v
        names = " ".join("abcd"[:len(shape)])
        return v.rearrange(f"p ({names}) -> p {names}", **{"abcd"[i]: shape[i] for i in range(len(shape))})

    gel = region(0, CT, TOK)
    qT = region(2560, HEADS, TOK)
    kT = region(5120, HEADS, TOK)
    v_t = region(7680, TILES, LW)
    xc = region(10240, CT, TOK)
    sg = region(10240, TILES, LW)
    x_in = region(12800, TILES, D)
    hT_tmp = region(0, 2, TOK)
    junk0 = region(5120, D)
    rope_tmp = region(7680, 2, LAT)
    par_rows = region(2560, P)
    lr_r, lr_g, lr_a, lr_t = (region(12800 + i * 2 * TOK, 2, TOK) for i in range(4))
    rope_c, rope_s = region(17920, LAT), region(17920 + LAT, LAT)
    sc = region(12800, 4, LAT)
    sc_c = region(14848, CTX)
    dec = region(14976, 2, 896)
    s0 = region(16768, 2, 2 * DK)
    o_t = region(17280 , TILES, DK)
    ro_t = region(17920, TILES, DK)
    kz = region(18560, 2, DK)
    x1 = region(0, TILES, D)
    xn2 = region(5120, TILES, D)
    facc = region(10240, TILES, D)
    h2T = region(10240, 2, KT, P)
    junk = region(12288, D)
    pT, pW, pS, pC = (region(10240 + i * TOK, TOK) for i in range(4))
    g_row = region(15360, 2, D)
    post = region(17408, D)
    mg1 = region(13312, D)
    sgl = region(15360, 2, 512)
    hid = region(16384, 2, 512)
    oneh = region(17408, TILES, SLOTS)
    xs_tmp = region(17808, 2, 4 * SLOTS)

    hT_hi = act_hi[:, :].rearrange("p (k t) -> p k t", k=KT)
    hT_lo = act_lo[:, :].rearrange("p (k t) -> p k t", k=KT)
    xs = [[a[:, i * KT * SLOTS:(i + 1) * KT * SLOTS].rearrange("p (k s) -> p k s", k=KT) for a in (act_hi, act_lo)]
          for i in range(2)]
    hidT = [[a[:, 1280 + i * 4 * SLOTS:1280 + (i + 1) * 4 * SLOTS] for a in (act_hi, act_lo)] for i in range(2)]
    ye = [a[0:SLOTS, 1920:1920 + D] for a in (act_hi, act_lo)]
    onehotT = act_hi[0:SLOTS, 2944:2944 + TOK]

    ident = const[:, C_ID:C_ID + P]
    xi = const[:, C_XI:C_XI + 32].rearrange("p (t h d) -> p t h d", t=4, h=HEADS)
    zeta = const[:, C_ZETA:C_ZETA + 8].rearrange("p (h d) -> p h d", h=HEADS)
    iota = const[:, C_IOTA:C_IOTA + 2 * SLOTS].rearrange("p (g s) -> p g s", g=2)
    selc = const[:, C_SELC:C_SELC + 2]
    selb = const[:, C_SELB:C_SELB + 2 * P].rearrange("p (g m) -> p g m", g=2)
    lst = rows[:, 512:768]
    lrow = rows[0:8, 768:896]
    gw = rows[:, :].rearrange("p (k d c j) -> p k d c j", k=2, d=2, c=CT)

    const_in, par_in, x_ld, x_re, rw_in, gw_in, rope_in = map(sem, (
        "const_in", "par_in", "x_loaded", "x_reloaded", "router_in", "lru_gates_in", "rope_in"))
    gbias1, gbias2, post_in, dec_in = map(sem, ("gate1_bias_in", "gate2_bias_in", "post_gain_in", "decay_in"))
    dec_in = [dec_in, sem("decay_in_odd")]
    raw_in = [sem(f"raw_in{i}") for i in range(RAW)]
    out_lru, out_ret, out_y = map(sem, ("lru_state_out", "ret_state_out", "y_out"))
    hi_done, lo_dve, lo_pool, w_used = map(sem, ("hi_done", "lo_done_dve", "lo_done_pool", "w_used"))
    dve_step, act_step, pool_step = map(sem, ("dve_step", "act_step", "pool_step"))
    par_ps, par_rd, sil_rd, lam_abs, lam_exp, cond_0, cond_rd, c8_rd = map(sem, (
        "par_ps", "par_ready", "silu_ready", "lambda_abs", "lambda_exp", "cond_zeroed", "cond_ready", "c8_ready"))
    ada_row, col_ps, col_rd = map(sem, ("ada_row", "columns_ps", "columns_ready"))
    x_sq, xn_rd, xT_ps, h_tmp, h_hi, h_lo = map(sem, ("x_squares", "xn_ready", "xT_ps", "h_tmp", "h_hi", "h_lo"))
    win_ps, yl_ev, xl_ev, rope_t, qk_rd, qk_ctx, v_ev, g_ev = map(sem, (
        "win_ps", "yl_out", "conv_done", "rope_terms", "qk_ready", "qk_ctx_out", "v_out", "g_out"))
    gt_ps, gt_ev, lr_exp, lr_gx, lr_w, lr_sq, lr_done = map(sem, (
        "lru_gate_ps", "lru_gates_out", "lru_exp", "lru_gx", "lru_w", "lru_sqrt", "lru_done"))
    cat_hi, cat_lo = sem("lru_cat_hi"), sem("lru_cat_lo")
    sc_ps, sc_ev, scc_ps, scc_ev, pv_ps, ret_rd, kt_ps, kz_ev, st_ps, st_ev, ret_o, rt_ps, rt_hi, rt_lo = map(sem, (
        "score_ps", "score_masked", "ctx_score_ps", "ctx_score_masked", "pv_ps", "ret_read", "kT_ps", "kz_ready",
        "state_ps", "state_copied", "ret_out", "ret_T_ps", "ret_T_hi", "ret_T_lo"))
    lst_ps, lst_ev = sem("lru_state_ps"), sem("lru_state_row")
    gr_ps, gr_ev, wo_ps, wo_ev, wo_sq, x1_rd, x1_sq, xn2_rd = map(sem, (
        "gate_row_ps", "gate_row", "wout_ps", "wout_copied", "wout_squares", "x1_ready", "x1_squares", "xn2_ready"))
    h2_ps, h2_act, h2_dve, lg_ps, lg_sub, lg_exp, pr_rd, pt_ps, sl_rd, sl_ps, fz = map(sem, (
        "h2_ps", "h2_act", "h2_dve", "logits_ps", "logits_less_max", "logits_exp", "probs_ready", "probsT_ps",
        "slots_ready", "slots_ps", "facc_zeroed"))
    sl_ev, hid_rd, ht_ps, ht_hi, ht_lo = map(sem, ("silu_out", "hid_ready", "hidT_ps", "hidT_hi", "hidT_lo"))
    oh_rd, oht_ps, oht_ev, ga_ps, xs_f, xs_h, xs_l, ye_h, ye_l, fs_ps, fs_add = map(sem, (
        "onehot_ready", "onehotT_ps", "onehotT_out", "gather_ps", "gathered", "gathered_hi", "gathered_lo",
        "ye_hi", "ye_lo", "scatter_ps", "scatter_added"))
    ec_rd, xs_m = sem("expert_columns"), sem("gathered_scaled")
    root_in, root_out = sem("root_argument"), sem("root_taken")
    fin_sq, fin_y = sem("f_squares"), sem("y_ready")

    aw = ada_w.rearrange("(k p) n -> p k n", p=P)
    wi = w_in.rearrange("(k p) n -> p k n", p=P)
    wo = w_out.rearrange("(k p) n -> p k n", p=P)

    def block_cols(w, blk, half):
        return w[:, 4 * half:4 * half + 4, blk * 512:(blk + 1) * 512]

    def prologue_source(n):
        if n < N_WIN:
            return block_cols(aw, ADA_FIRST[n // 2], n % 2)
        if n < N_MID:
            return block_cols(wi, WIN[(n - N_WIN) // 2], n % 2)
        if n < N_GATES:
            return block_cols(aw, ADA_MID[(n - N_MID) // 2], n % 2)
        if n < N_WOUT:
            return block_cols(aw, ADA_GATES[(n - N_GATES) // 2], n % 2)
        return block_cols(wo, (n - N_WOUT) // 2, n % 2)

    def expert_source(e, kind, b, half):
        if kind == "d":
            w = exp_down[bass.ds(e, 1), b * 512:(b + 1) * 512, :].rearrange("o (p j) n -> p (o j) n", p=P)
            return w[:, 2 * half:2 * half + 2, :]
        w = {"g": exp_gate, "u": exp_up}[kind]
        w = w[bass.ds(e, 1), :, b * 512:(b + 1) * 512].rearrange("o (k p) n -> p (o k) n", p=P)
        return w[:, 4 * half:4 * half + 4, :]

    def body_chunks(last):
        order = [("u", 1, 0), ("d", 0, 0), ("g", 2, 0), ("u", 2, 0), ("d", 1, 0), ("g", 3, 0), ("u", 3, 0), ("d", 2, 0)]
        if not last:
            order += [("g", 0, 1)]
        order += [("d", 3, 0)]
        if not last:
            order += [("u", 0, 1), ("g", 1, 1)]
        return [(kind, b, half, nxt) for kind, b, nxt in order for half in range(2)]

    FIRST_CHUNKS = [(kind, b, half) for kind, b in (("g", 0), ("u", 0), ("g", 1)) for half in range(2)]

    SCATTER_BANKS = (7, 6, 4, 5, 7, 6, 4, 5, 7, 4)
    SCATTER_AT = {("u", 0, 1): range(0, 4), ("g", 1, 0): range(4, 7), ("g", 1, 1): range(7, 10)}

    def chunk_view(ring, n, cols):
        return ring[:, n % ring.shape[1], :].rearrange("p (k n) -> p k n", n=cols)

    def load(sp_e, n, e, src, cols):
        if n >= RAW or not isinstance(e, int):
            sp_e.wait_ge(lo_pool, e * PER_E + (n - RAW + 1))
            sp_e.wait_ge(lo_dve, e * PER_E + (n - RAW + 1))
        sp_e.dma_start(chunk_view(raw, n, cols), src).then_inc(raw_in[n % RAW], 16)

    def split_hi(act, n, e=0):
        act.wait_ge(raw_in[n % RAW], e * (16 * PER_E // RAW) + 16 * (n // RAW + 1))
        if n >= WS:
            act.wait_ge(w_used, e * PER_E + (n - WS + 1))
        nc.scalar.copy(w_hi[:, n % WS, :], raw[:, n % RAW, :]).then_inc(hi_done, 1)

    def split_lo(eng, who, n, e=0):
        eng.wait_ge(hi_done, e * PER_E + (n + 1))
        ops, done, at = {"dve": (nc.vector, lo_dve, slice(0, DVE_COLS)), "pool": (nc.gpsimd, lo_pool, slice(DVE_COLS, CH))}[who]
        ops.tensor_tensor(w_lo[:, n % WS, at], raw[:, n % RAW, at], w_hi[:, n % WS, at], ALU.subtract).then_inc(done, 1)

    def chunk_ready(pe, n, e=0):
        pe.wait_ge(lo_dve, e * PER_E + (n + 1))
        pe.wait_ge(lo_pool, e * PER_E + (n + 1))

    def used(eng, n, e=0):
        eng.wait_ge(w_used, e * PER_E + (n + 1))

    def ada_chunk(i):
        return (0, N_MID - 8, N_GATES - 16)[i // 4] + 2 * i

    def win_ready(eng, bi, u):
        if u == (CT if bi < 4 else TILES) - 1:
            used(eng, N_WIN + 2 * bi + 1)
        else:
            eng.wait_ge(win_ps, (0, 3, 6, 9, 12, 16)[bi] + u + 1)

    def wout_ready(eng, n2, t):
        if t == TILES - 1:
            used(eng, N_WOUT + 2 * n2 + 1)
        else:
            eng.wait_ge(wo_ps, 4 * n2 + t + 1)

    def three(out, lh, ll, rh, rl, start, stop, **kw):
        nc.tensor.matmul(out, lh, rl, start=start, stop=False, **kw)
        nc.tensor.matmul(out, ll, rh, start=False, stop=False, **kw)
        return nc.tensor.matmul(out, lh, rh, start=False, stop=stop, **kw)

    LAST = NEXP - 1
    block = ctx.enter_context(nc.Block())

    @block.sync
    def _(sync):
        for n in range(N_EXP):
            load(sync, n, 0, prologue_source(n), 512)
        for i, (kind, b, half) in enumerate(FIRST_CHUNKS):
            load(sync, N_EXP + i, 0, expert_source(0, kind, b, half), 512)

        def body(e, last):
            for i, (kind, b, half, nxt) in enumerate(body_chunks(last)):
                load(sync, N_BODY + i, e, expert_source(e + nxt, kind, b, half), D if kind == "d" else 512)

        with sync.Fori(0, LAST) as e:
            sync.compute_val(e * (FF * D) * 4)
            body(e, False)
        body(LAST, True)
        sync.wait_ge(out_lru, 16)
        sync.wait_ge(out_ret, 16 * 2 * HEADS)
        sync.wait_ge(out_y, 16 * TILES)

    @block.scalar
    def _(act):
        pr = par_rows
        act.dma_start(const[:, :], consts).then_inc(const_in, 16)
        for r0, a in ((R_C, c), (R_C + 8, c_ctx), (R_PRE, norm_mix_pre), (R_FPRE, norm_ffn_pre), (R_CW, conv_w),
                      (R_CB, conv_b), (R_BA, lru_ba), (R_BI, lru_bi), (R_LAM, lru_lambda), (R_H0, state_lru),
                      (R_ADAB, ada_b[0:16, :]), (R_ADAB + 16, ada_b[24:40, :])):
            act.dma_start(pr[r0:r0 + a.shape[0], :], a).then_inc(par_in, 16)
        for t in range(TILES):
            act.dma_start(x_in[:, t, :], x_lat[t * P:(t + 1) * P, :] if t < 4 else x_ctx).then_inc(x_ld, 16)
        act.dma_start(rw[:, :, :], router_w.rearrange("(k p) n -> p k n", p=P)).then_inc(rw_in, 16)
        act.dma_start(rope_c, rope[0]).then_inc(rope_in, 16)
        act.dma_start(rope_s, rope[1]).then_inc(rope_in, 16)
        for n in range(WS):
            split_hi(act, n)
        act.wait_ge(par_rd, 1)
        nc.scalar.activation(sil[:, :], par[:, R_C:R_C + 16], ACT.Silu).then_inc(sil_rd, 1)
        act.wait_ge(lam_abs, 1)
        nc.scalar.activation(sm[:, S_EXP:S_EXP + 8], sm[:, S_ABS:S_ABS + 8], ACT.Exp, scale=-1.0).then_inc(lam_exp, 1)
        act.wait_ge(x_ld, 16 * TILES)
        for t in range(TILES):
            if t:
                act.wait_ge(x_sq, t)
            nc.scalar.activation(junk0, x_in[:, t, :], ACT.Square, accum_out=sm[:, S_SS + t:S_SS + t + 1]).then_inc(x_sq, 1)
        roots = [0]

        def root(at, n=TILES):
            roots[0] += 1
            act.wait_ge(root_in, roots[0])
            nc.scalar.activation(sm[:, at:at + n], sm[:, at:at + n], ACT.Sqrt).then_inc(root_out, 1)

        root(S_RSTD)
        for n in range(WS, N_WIN + WS):
            split_hi(act, n)
        act.wait_ge(col_ps, 4)
        for kind, w in ((0, lru_wa), (1, lru_wi)):
            for par_h in range(2):
                for d in range(2):
                    act.dma_start(gw[64 * par_h:64 * par_h + 64, kind, d, :, :],
                                  w[d, par_h::2].rearrange("h i j -> i h j")).then_inc(gw_in, 16)
        for kt in range(KT):
            act.wait_ge(h_tmp, kt + 1)
            nc.scalar.copy(hT_hi[:, kt, :], hT_tmp[:, kt % 2, :]).then_inc(h_hi, 1)

        def yl_out(ct):
            win_ready(act, 0, ct)
            if ct == 0:
                act.wait_ge(h_lo, KT)
            nc.scalar.activation(gel[:, ct, 0:LAT], psum[ct][:, :], ACT.Gelu_apprx_tanh).then_inc(yl_ev, 1)

        def yl_ctx_out(ct):
            nc.scalar.activation(gel[:, ct, LAT:], psum[4][:, ct * P:(ct + 1) * P], ACT.Gelu_apprx_tanh).then_inc(yl_ev, 1)

        def qk_ctx_out(i, dst, bank):
            win_ready(act, 2 + i, CT - 1)
            nc.scalar.copy(dst[:, :, LAT:], psum[bank][:, :].rearrange("p (h t) -> p h t", h=HEADS)).then_inc(qk_ctx, 1)

        def lru_gates_out(s):
            ct, d, ctxp = s // 4, s // 2 % 2, s % 2
            act.wait_ge(gt_ps, s + 1)
            if s % 4 == 0:
                if ct:
                    act.wait_ge(lr_done, ct)
                else:
                    act.wait_ge(xn_rd, TILES)
                    act.wait_ge(xT_ps, KT)
            for kind, dst, r0 in ((0, lr_r, R_BA), (1, lr_g, R_BI)):
                src = psum[6][:, kind * P:(kind + 1) * P] if ctxp else psum[6 + kind][:, :]
                at = slice(LAT, TOK) if ctxp else slice(0, LAT)
                nc.scalar.activation(dst[:, d, at], src, ACT.Sigmoid,
                                     bias=par[:, r0 + 4 * d + ct:r0 + 4 * d + ct + 1]).then_inc(gt_ev, 1)

        def lru_exp(ct):
            act.wait_ge(gt_ev, 8 * (ct + 1))
            if ct == 0:
                act.wait_ge(c8_rd, 1)
            for d in range(2):
                j = 4 * d + ct
                nc.scalar.activation(lr_a[:, d, :], lr_r[:, d, :], ACT.Exp, scale=sm[:, S_C8 + j:S_C8 + j + 1]).then_inc(lr_exp, 1)
                nc.scalar.activation(lr_t[:, d, :], lr_r[:, d, :], ACT.Tanh, scale=sm[:, S_NC8 + j:S_NC8 + j + 1]).then_inc(lr_exp, 1)

        def lru_sqrt(ct):
            act.wait_ge(lr_w, ct + 1)
            nc.scalar.activation(lr_t[:, :, :], lr_t[:, :, :], ACT.Sqrt).then_inc(lr_sq, 1)

        def lru_cat(ct):
            act.wait_ge(lr_done, ct + 1)
            if ct == 0:
                used(act, N_MID - 1)
            nc.scalar.copy(hT_hi[:, ct, :], gel[:, ct, :]).then_inc(cat_hi, 1)

        def tok_out(i, t):
            win_ready(act, 4 + i, t)
            bank = psum[t] if t < 4 else psum[4 + i]
            if i == 0:
                if t == 0:
                    act.wait_ge(qk_rd, 2 * HEADS)
                nc.scalar.copy(v_t[:, t, :], bank[:, :]).then_inc(v_ev, 1)
            else:
                if t == 0:
                    act.wait_ge(lr_done, CT)
                nc.scalar.activation(sg[:, t, :], bank[:, :], ACT.Silu).then_inc(g_ev, 1)

        for m in range(N_WIN, N_MID):
            bi, half = (m - N_WIN) // 2, m % 2
            ct = GATES_AT.get(m - N_WIN - 4)
            if ct is not None:
                for s in range(4 * ct, 4 * ct + 4):
                    lru_gates_out(s)
            if half and bi == 0:
                for u in range(CT - 1):
                    yl_out(u)
            if half and bi >= 4:
                for t in range(TILES - 1):
                    tok_out(bi - 4, t)
            split_hi(act, m + WS)
            if half and bi == 0:
                yl_out(CT - 1)
                for u in range(CT):
                    yl_ctx_out(u)
            if half and bi in (2, 3):
                qk_ctx_out(bi - 2, (qT, kT)[bi - 2], 4 + bi % 2)
            if half and bi >= 4:
                tok_out(bi - 4, TILES - 1)
            if ct is not None:
                lru_exp(ct)
                lru_sqrt(ct)
        for ct in range(CT):
            lru_cat(ct)
        act.wait_ge(lst_ev, 1)
        act.dma_start(new_lru, lrow).then_inc(out_lru, 16)

        def ret_loads(h):
            if h == 0:
                act.wait_ge(lr_done, CT)
                act.wait_ge(rope_t, 2 * HEADS)
                act.wait_ge(qk_rd, 2 * HEADS)
            if h >= 2:
                act.wait_ge(sc_ev, 4 * (h - 1))
                act.wait_ge(scc_ev, h - 1)
                act.wait_ge(pv_ps, h - 1)
            act.dma_start(dec[:, h % 2, :], decay[h]).then_inc(dec_in[h % 2], 16)
            act.dma_start(s0[:, h % 2, :].rearrange("p (d e) -> p d e", d=2),
                          state_ret[:, h].rearrange("d k e -> k d e")).then_inc(dec_in[h % 2], 16)

        def ret_state(h):
            act.wait_ge(st_ps, h + 1)
            if h >= 1:
                act.wait_ge(out_ret, 32 * h)
            nc.scalar.copy(lst[:, 0:2 * DK], psum[6][:, P:3 * P]).then_inc(st_ev, 1)
            act.wait_ge(st_ev, h + 1)
            for d in range(2):
                act.dma_start(new_ret[d, h], lst[:, d * DK:(d + 1) * DK]).then_inc(out_ret, 16)
            if h + 2 < HEADS:
                ret_loads(h + 2)

        ret_loads(0)
        ret_loads(1)
        ret_state(0)
        for h in range(HEADS):
            m0 = N_MID + 2 * h
            root(S_O)
            if h + 1 < HEADS:
                ret_state(h + 1)
            split_hi(act, m0 + WS)
            act.wait_ge(rt_ps, h + 1)
            nc.scalar.copy(hT_hi[:, 4 + h, 0:LAT], psum[7][:, :]).then_inc(rt_hi, 1)
            nc.scalar.copy(hT_hi[:, 4 + h, LAT:], psum[6][:, 0:P]).then_inc(rt_hi, 1)
            split_hi(act, m0 + 1 + WS)
        act.wait_ge(ret_o, HEADS)
        act.wait_ge(rt_ps, HEADS)
        act.wait_ge(kt_ps, HEADS)
        act.dma_start(mg1[4:5, :], ada_b[16:24, :].rearrange("(o a) b -> o (a b)", o=1)).then_inc(gbias1, 16)
        act.dma_start(post, norm_mix_post.partition_broadcast(P)).then_inc(post_in, 16)
        act.wait_ge(col_ps, 8)
        act.wait_ge(out_ret, 32 * HEADS)
        act.wait_ge(out_lru, 16)
        act.dma_start(rows[4:5, :], ada_b[40:48, :].rearrange("(o a) b -> o (a b)", o=1)).then_inc(gbias2, 16)
        for n in range(N_GATES + WS, N_WOUT + WS):
            split_hi(act, n)
        act.wait_ge(pv_ps, HEADS)
        act.wait_ge(st_ps, HEADS)
        for t in range(TILES):
            act.dma_start(xn2[:, t, :], x_lat[t * P:(t + 1) * P, :] if t < 4 else x_ctx).then_inc(x_re, 16)
        for n2 in range(2):
            for t in range(TILES):
                act.wait_ge(wo_ev, 5 * n2 + t + 1)
                if n2 or t:
                    act.wait_ge(wo_sq, 5 * n2 + t)
                nc.scalar.activation(junk[:, 0:512], x1[:, t, n2 * 512:(n2 + 1) * 512], ACT.Square,
                                     accum_out=sm[:, S_WO + 2 * t + n2:S_WO + 2 * t + n2 + 1]).then_inc(wo_sq, 1)
                if t in (1, 3):
                    split_hi(act, N_WOUT + WS + 2 * n2 + t // 2)
        root(S_T)
        for t in range(TILES):
            act.wait_ge(x1_rd, t + 1)
            if t:
                act.wait_ge(x1_sq, t)
            else:
                act.wait_ge(wo_sq, 2 * TILES)
            nc.scalar.activation(junk, x1[:, t, :], ACT.Square, accum_out=sm[:, S_X1 + t:S_X1 + t + 1]).then_inc(x1_sq, 1)
            if t:
                root(S_O + t - 1, 1)
        root(S_O + TILES - 1, 1)
        for t in range(TILES):
            act.wait_ge(h2_ps, 2 * t + 1)
            if t >= 2:
                act.wait_ge(lg_ps, t - 1)
            g = t // 4
            for j in range(4):
                nc.scalar.activation(h2T[:, t % 2, j, :], psum[2 * (t % 2)][:, j * P:(j + 1) * P], ACT.Identity,
                                     scale=aff[:, 1, g, j:j + 1], bias=modc[:, g, 16 + j:17 + j]).then_inc(h2_act, 1)
        act.wait_ge(lg_sub, 1)
        nc.scalar.activation(sm[:, 0:80], sm[:, 0:80], ACT.Exp).then_inc(lg_exp, 1)

        def gathered_half(e, pr2, hf):
            act.wait_ge(xs_f, 2 * e + (hf + 1))
            nc.scalar.copy(xs[pr2][0][:, 4 * hf:4 * hf + 4, :], xs_tmp[:, hf, :].rearrange("p (k s) -> p k s", k=4)).then_inc(xs_h, 1)

        gathered_half(0, 0, 0)
        gathered_half(0, 0, 1)

        def silu(n, e, b):
            used(act, n, e)
            nc.scalar.activation(sgl[0:SLOTS, b % 2, :], psum[b % 2][0:SLOTS, :], ACT.Silu).then_inc(sl_ev, 1)

        def hidT_hi(e, b):
            act.wait_ge(ht_ps, 4 * e + (b + 1))
            nc.scalar.copy(hidT[b % 2][0], psum[6][:, 0:4 * SLOTS]).then_inc(ht_hi, 1)

        for i, (kind, b, half) in enumerate(FIRST_CHUNKS):
            split_hi(act, N_EXP + i + WS)
            if half and kind == "g":
                silu(N_EXP + i, 0, b)
        hidT_hi(0, 0)

        def body(e, pr2, last):
            for i, (kind, b, half, nxt) in enumerate(body_chunks(last)):
                if not last or i + WS < len(body_chunks(last)):
                    split_hi(act, N_BODY + i + WS, e)
                if half and kind == "g":
                    silu(N_BODY + i, e, b)
                    if b:
                        hidT_hi(e + nxt, b - 1)
                if kind == "u" and b == 1 and half:
                    act.wait_ge(oht_ps, e + 1)
                    nc.scalar.copy(onehotT[:, 0:LAT], psum[6][0:SLOTS, :]).then_inc(oht_ev, 1)
                    nc.scalar.copy(onehotT[:, LAT:], psum[7][0:SLOTS, 0:P]).then_inc(oht_ev, 1)
                    nc.scalar.copy(gate[0:SLOTS, :], psum[7][0:SLOTS, P:P + 1]).then_inc(oht_ev, 1)
                if not last and kind == "g" and b == 3 and half == 0:
                    gathered_half(e + 1, 1 - pr2, 0)
                if not last and kind == "d" and b == 2 and half == 0:
                    gathered_half(e + 1, 1 - pr2, 1)
                if kind == "d" and b == 2 and half:
                    hidT_hi(e, 3)
                if kind == "d" and b == 3 and half:
                    used(act, N_BODY + i, e)
                    for hf in range(2):
                        nc.scalar.activation(ye[0][:, hf * 512:(hf + 1) * 512], psum[4 + hf][0:SLOTS, :], ACT.Copy,
                                             scale=gate[0:SLOTS, 0:1]).then_inc(ye_h, 1)

        with act.Fori(0, LAST - 1, 2) as e:
            body(e, 0, False)
            body(e + 1, 1, False)
        body(LAST - 1, 0, False)
        body(LAST, 1, True)
        act.wait_ge(ye_l, 2 * NEXP)
        act.wait_ge(oh_rd, NEXP)
        act.wait_ge(ga_ps, 2 * NEXP)
        act.dma_start(post, norm_ffn_post.partition_broadcast(P)).then_inc(post_in, 16)
        for t in range(TILES):
            act.wait_ge(fs_add, 10 * LAST + 2 * t + 3)
            if t:
                act.wait_ge(fin_sq, t)
            else:
                act.wait_ge(x1_sq, TILES)
            nc.scalar.activation(xn2[:, 0, :], facc[:, t, :], ACT.Square, accum_out=sm[:, S_FIN + t:S_FIN + t + 1]).then_inc(fin_sq, 1)
        root(S_O)
        for t in range(TILES):
            act.wait_ge(fin_y, t + 1)
            act.dma_start(y_lat[t * P:(t + 1) * P, :] if t < 4 else y_ctx, facc[:, t, :]).then_inc(out_y, 16)


    @block.tensor
    def _(pe):
        mm, tr = nc.tensor.matmul, nc.tensor.transpose

        pe.wait_ge(const_in, 16)
        pe.wait_ge(par_in, 16 * 12)
        tr(psum[7][:, 0:R_N], par_rows[0:R_N, :], ident[0:R_N, 0:R_N]).then_inc(par_ps, 1)

        def ada_block(i, bank):
            for half in range(2):
                n = ada_chunk(i) + half
                chunk_ready(pe, n)
                wh, wl = chunk_view(w_hi, n, 512), chunk_view(w_lo, n, 512)
                for k in range(4):
                    kk = 4 * half + k
                    mm(psum[bank][0:66, :], cond[:, kk, :], wl[:, k, :], start=(kk == 0), stop=False)
                    last = mm(psum[bank][0:66, :], cond[:, kk, :], wh[:, k, :], start=False, stop=(kk == 7))
                last.then_inc(w_used, 1)

        def columns(i, bank, at):
            pe.wait_ge(ada_row, i + 1)
            for q in range(4):
                last = mm(psum[bank][:, at + 2 * q:at + 2 * q + 2], rows[0:4, q * P:(q + 1) * P], selc[0:4, :],
                          start=True, stop=True)
            last.then_inc(col_ps, 1)

        pe.wait_ge(cond_rd, 1)
        for i in range(4):
            if i:
                pe.wait_ge(ada_row, i)
            ada_block(i, 6)
            if i:
                if i >= 2:
                    pe.wait_ge(col_rd, i - 1)
                columns(i - 1, 7, 128)
        pe.wait_ge(col_rd, 3)
        columns(3, 7, 128)

        pe.wait_ge(xn_rd, TILES)
        for kt in range(KT):
            if kt >= 2:
                pe.wait_ge(h_tmp, kt - 1)
            for t in range(4):
                tr(psum[kt % 2][:, t * P:(t + 1) * P], x_in[:, t, kt * P:(kt + 1) * P], ident)
            tr(psum[2 + kt % 2][:, 0:P], x_in[:, 4, kt * P:(kt + 1) * P], ident).then_inc(xT_ps, 1)

        def lru_gates(s):
            ct, d, ctxp = s // 4, s // 2 % 2, s % 2
            if s:
                pe.wait_ge(gt_ev, 2 * s)
            else:
                pe.wait_ge(col_rd, 4)
                pe.wait_ge(gw_in, 16 * 8)
            pe.wait_ge(xl_ev, CT + 1 if ctxp else ct + 1)
            for kind in range(2):
                for hh in (slice(0, 64), slice(64, 128)):
                    dst = psum[6][hh, kind * P:(kind + 1) * P] if ctxp else psum[6 + kind][hh, :]
                    src = xc[hh, ct, LAT:] if ctxp else xc[hh, ct, 0:LAT]
                    last = mm(dst, gw[hh, kind, d, ct, :], src, start=True, stop=True)
            last.then_inc(gt_ps, 1)

        def bank_free(bi, u):
            if bi == 0:
                pe.wait_ge(h_tmp, KT)
            elif bi == 1:
                pe.wait_ge(yl_ev, u + 1)
            elif bi == 2:
                pe.wait_ge(xl_ev, u + 1)
                if u == 0:
                    pe.wait_ge(yl_ev, 2 * CT)
            elif bi == 3:
                pe.wait_ge(rope_t, u + 1)
                if u == 0:
                    pe.wait_ge(xl_ev, CT + 1)
            elif bi == 4:
                pe.wait_ge(rope_t, HEADS + u + 1) if u < 4 else pe.wait_ge(qk_ctx, 1)
            else:
                pe.wait_ge(v_ev, u + 1) if u < 4 else pe.wait_ge(qk_ctx, 2)

        for n in range(N_WIN, N_MID):
            bi, half = (n - N_WIN) // 2, n % 2
            chunk_ready(pe, n)
            pe.wait_ge(h_lo, 4 * (half + 1) if bi == 0 else KT)
            wh, wl = chunk_view(w_hi, n, 512), chunk_view(w_lo, n, 512)
            units = CT if bi < 4 else TILES
            for u in range(units):
                if half == 0:
                    bank_free(bi, u)
                for k in range(4):
                    kk = 4 * half + k
                    first, final = kk == 0, kk == 7
                    if bi < 4:
                        a, b = wh[:, k, u * P:(u + 1) * P], wl[:, k, u * P:(u + 1) * P]
                        three(psum[u][:, :], a, b, hT_hi[:, kk, 0:LAT], hT_lo[:, kk, 0:LAT], first, final)
                        last = three(psum[4 + bi % 2][:, u * P:(u + 1) * P], a, b, hT_hi[:, kk, LAT:], hT_lo[:, kk, LAT:],
                                     first and u == 0, final and u == 3, skip_group_check=True)
                    else:
                        at = slice(u * P, (u + 1) * P)
                        last = three(psum[u if u < 4 else bi][:, :], hT_hi[:, kk, at], hT_lo[:, kk, at],
                                     wh[:, k, :], wl[:, k, :], first, final)
                if u == units - 1:
                    last.then_inc(w_used, 1)
                elif half:
                    last.then_inc(win_ps, 1)
                if n - N_WIN - 4 in GATES_AT and u < 4:
                    lru_gates(4 * GATES_AT[n - N_WIN - 4] + u)

        pe.wait_ge(lr_done, CT)
        pe.wait_ge(gt_ev, 32)
        tr(psum[6][0:8, 0:P], sm[:, S_ST:S_ST + 8], ident).then_inc(lst_ps, 1)

        def ret_scores(h):
            for j in range(4):
                if j >= 2:
                    pe.wait_ge(sc_ev, 4 * h + j - 1)
                mm(psum[j % 2][:, :], kT[:, h, j * P:(j + 1) * P], qT[:, h, 0:LAT], start=True, stop=True).then_inc(sc_ps, 1)
                if j == 1:
                    if h:
                        pe.wait_ge(ret_rd, h)
                    pe.wait_ge(dec_in[h % 2], 32 * (h // 2 + 1))
                    for t in range(4):
                        mm(psum[3 + t // 2][:, (t % 2) * 2 * DK:(t % 2 + 1) * 2 * DK], qT[:, h, t * P:(t + 1) * P],
                           s0[:, h % 2, :], start=True, stop=True)
            mm(psum[5][:, 0:P], kT[:, h, LAT:], qT[:, h, LAT:], start=True, stop=True).then_inc(scc_ps, 1)
            if h:
                pe.wait_ge(st_ev, h)
            if h >= 2:
                pe.wait_ge(rt_lo, 2 * (h - 1))
            tr(psum[6][:, 3 * P:], kT[:, h, LAT:], ident).then_inc(kt_ps, 1)

        def ret_values(h):
            hc = slice(h * DK, (h + 1) * DK)
            pe.wait_ge(scc_ev, h + 1)
            mm(psum[5][:, P:2 * P], sc_c, v_t[:, 4, hc], start=True, stop=True)
            pe.wait_ge(sc_ev, 4 * h + 4)
            for t in range(4):
                for j in range(4):
                    last = mm(psum[2][:, t * DK:(t + 1) * DK], sc[:, j, t * P:(t + 1) * P], v_t[:, j, hc],
                              start=(j == 0), stop=(j == 3))
            last.then_inc(pv_ps, 1)
            pe.wait_ge(kz_ev, h + 1)
            for d in range(2):
                last = mm(psum[6][:, (1 + d) * P:(2 + d) * P], kz[:, d, :], v_t[:, 4, hc], start=True, stop=True)
            last.then_inc(st_ps, 1)

        pe.wait_ge(qk_rd, 2 * HEADS)
        pe.wait_ge(qk_ctx, 2)
        pe.wait_ge(v_ev, TILES)
        pe.wait_ge(g_ev, TILES)
        pe.wait_ge(lst_ev, 1)
        ret_scores(0)
        ret_values(0)
        for h in range(HEADS):
            if h + 1 < HEADS:
                ret_scores(h + 1)
            if h:
                pe.wait_ge(rt_lo, 2 * h)
            ada_block(4 + h, 7)
            if h + 1 < HEADS:
                ret_values(h + 1)
            columns(4 + h, 7, 0)
            pe.wait_ge(col_rd, 5 + h)
            pe.wait_ge(ret_o, h + 1)
            pe.wait_ge(st_ev, min(h + 2, HEADS))
            for t in range(4):
                tr(psum[7][:, t * P:(t + 1) * P], ro_t[:, t, :], ident)
            tr(psum[6][:, 0:P], ro_t[:, 4, :], ident).then_inc(rt_ps, 1)

        pe.wait_ge(col_rd, 8)
        gate_banks = (2, 3, 5, 6)

        def gate_rows(src):
            for g in range(2):
                for half in range(2):
                    mm(psum[gate_banks[2 * g + half]][:, :], selb[0:5, g, :], src[0:5, half * 512:(half + 1) * 512],
                       start=True, stop=True).then_inc(gr_ps, 1)

        for i in range(8, 12):
            pe.wait_ge(ada_row, i if i < 10 else i - 1)
            ada_block(i, i % 2)
        pe.wait_ge(rt_lo, 2 * HEADS)
        pe.wait_ge(st_ev, HEADS)
        pe.wait_ge(ada_row, 12)
        pe.wait_ge(gbias1, 16)
        gate_rows(mg1)

        pe.wait_ge(cat_lo, CT)
        for n in range(N_WOUT, N_EXP):
            n2, half = (n - N_WOUT) // 2, n % 2
            chunk_ready(pe, n)
            wh, wl = chunk_view(w_hi, n, 512), chunk_view(w_lo, n, 512)
            for t in range(TILES):
                if half == 0 and n2 == 0 and t == 2:
                    pe.wait_ge(gr_ev, 4)
                if half == 0 and n2:
                    pe.wait_ge(wo_ev, t + 1)
                at = slice(t * P, (t + 1) * P)
                for k in range(4):
                    kk = 4 * half + k
                    last = three(psum[t][:, :], hT_hi[:, kk, at], hT_lo[:, kk, at], wh[:, k, :], wl[:, k, :], kk == 0, kk == 7)
                if t == TILES - 1:
                    last.then_inc(w_used, 1)
                elif half:
                    last.then_inc(wo_ps, 1)

        pe.wait_ge(rw_in, 16)

        def logits(t):
            pe.wait_ge(h2_act, 4 * (t + 1))
            pe.wait_ge(h2_dve, t + 1)
            for k in range(KT):
                last = mm(psum[4][:, t * NEXP:(t + 1) * NEXP], h2T[:, t % 2, k, :], rw[:, k, :], start=(k == 0), stop=(k == 7))
            last.then_inc(lg_ps, 1)

        pe.wait_ge(wo_ev, 2 * TILES)
        for t in range(TILES):
            pe.wait_ge(xn2_rd, t + 1)
            if t >= 2:
                pe.wait_ge(h2_act, 4 * (t - 1))
                pe.wait_ge(h2_dve, t - 1)
            for k in range(KT):
                last = tr(psum[2 * (t % 2) + k // 4][:, (k % 4) * P:(k % 4 + 1) * P], xn2[:, t, k * P:(k + 1) * P], ident)
                if k % 4 == 3:
                    last.then_inc(h2_ps, 1)
            if t:
                logits(t - 1)
        logits(TILES - 1)
        pe.wait_ge(pr_rd, 1)
        for t in range(TILES):
            dst = psum[5][0:NEXP, t * P:(t + 1) * P] if t < 4 else psum[6][0:NEXP, 0:P]
            last = tr(dst, sp[:, t, 0, :], ident)
        last.then_inc(pt_ps, 1)
        pe.wait_ge(sl_rd, 1)
        for t in range(TILES):
            last = tr(psum[7][:, t * NEXP:(t + 1) * NEXP], pS[0:NEXP, t * P:(t + 1) * P], ident[0:NEXP, 0:NEXP])
        last.then_inc(sl_ps, 1)

        def gather(hf):
            for k in range(4):
                for t in range(TILES):
                    last = mm(psum[7][:, k * SLOTS:(k + 1) * SLOTS], xn2[:, t, (4 * hf + k) * P:(4 * hf + k + 1) * P],
                              oneh[:, t, :], start=(t == 0), stop=(t == 4))
            last.then_inc(ga_ps, 1)

        def up_or_gate(n, e, bank, half, x):
            dst = psum[bank][0:SLOTS, :]
            wh, wl = chunk_view(w_hi, n, 512), chunk_view(w_lo, n, 512)
            pe.wait_ge(hi_done, e * PER_E + (n + 1))
            for k in range(4):
                kk = 4 * half + k
                mm(dst, x[1][:, kk, :], wh[:, k, :], start=(kk == 0), stop=False)
                mm(dst, x[0][:, kk, :], wh[:, k, :], start=False, stop=False)
            chunk_ready(pe, n, e)
            for k in range(4):
                kk = 4 * half + k
                last = mm(dst, x[0][:, kk, :], wl[:, k, :], start=False, stop=(kk == 7))
            last.then_inc(w_used, 1)

        def down(n, e, b, half):
            wh, wl = chunk_view(w_hi, n, D), chunk_view(w_lo, n, D)
            steps = [(j, [a[:, (2 * half + j) * SLOTS:(2 * half + j + 1) * SLOTS] for a in hidT[b % 2]], q)
                     for j in range(2) for q in range(2)]
            pe.wait_ge(hi_done, e * PER_E + (n + 1))
            for j, x, q in steps:
                at = slice(q * 512, (q + 1) * 512)
                mm(psum[4 + q][0:SLOTS, :], x[1], wh[:, j, at], start=(b == 0 and half == 0 and j == 0), stop=False)
                mm(psum[4 + q][0:SLOTS, :], x[0], wh[:, j, at], start=False, stop=False)
            chunk_ready(pe, n, e)
            for j, x, q in steps:
                last = mm(psum[4 + q][0:SLOTS, :], x[0], wl[:, j, q * 512:(q + 1) * 512], start=False,
                          stop=(b == 3 and half == 1 and j == 1))
            last.then_inc(w_used, 1)

        def hid_T(e, b):
            pe.wait_ge(hid_rd, 4 * e + (b + 1))
            hb = hid[0:SLOTS, b % 2, :].rearrange("s (p j) -> s j p", j=4)
            for j in range(4):
                last = tr(psum[6][:, j * SLOTS:(j + 1) * SLOTS], hb[:, j, :], ident[0:SLOTS, 0:SLOTS])
            last.then_inc(ht_ps, 1)

        pe.wait_ge(oh_rd, 1)
        gather(0)
        pe.wait_ge(xs_f, 1)
        gather(1)
        pe.wait_ge(xs_l, 2)
        for i, (kind, b, half) in enumerate(FIRST_CHUNKS):
            up_or_gate(N_EXP + i, 0, b + (2 if kind == "u" else 0), half, xs[0])
        hid_T(0, 0)

        def scatter(e, i):
            if i == 0:
                pe.wait_ge(ye_l, 2 * e + 2)
            if i >= 4:
                pe.wait_ge(fs_add, 10 * e + 2 + (i - 4 if i < 9 else 6))
            at = slice((i % 2) * 512, (i % 2 + 1) * 512)
            t = i // 2
            mm(psum[SCATTER_BANKS[i]][:, :], onehotT[:, t * P:(t + 1) * P], ye[1][:, at], start=True, stop=False)
            mm(psum[SCATTER_BANKS[i]][:, :], onehotT[:, t * P:(t + 1) * P], ye[0][:, at], start=False, stop=True).then_inc(fs_ps, 1)

        def body(e, pr2, last):
            for i, (kind, b, half, nxt) in enumerate(body_chunks(last)):
                n, own = N_BODY + i, e + nxt
                if kind in "gu":
                    if half == 0:
                        if kind == "g":
                            if b == 0:
                                pe.wait_ge(xs_l, 2 * own + 2)
                            pe.wait_ge(sl_ev, 4 * own + (b - 1))
                        elif b != 1:
                            pe.wait_ge(hid_rd, 4 * own + (b - 1))
                    up_or_gate(n, e, b % 2 + (2 if kind == "u" else 0), half, xs[1 - pr2 if nxt else pr2])
                else:
                    if half == 0:
                        pe.wait_ge(ht_lo, 4 * e + (b + 1))
                    down(n, e, b, half)
                if half and kind == "g" and b:
                    if b == 1:
                        pe.wait_ge(fs_add, 10 * e + 7)
                    else:
                        pe.wait_ge(ht_lo, 4 * e + (b - 1))
                        if b == 2:
                            pe.wait_ge(oht_ev, 3 * e + 3)
                    hid_T(own, b - 1)
                if half and kind == "u" and b == 1:
                    pe.wait_ge(ht_lo, 4 * e + 1)
                    pe.wait_ge(fs_add, 10 * e + 1)
                    for t in range(TILES):
                        dst = psum[6][0:SLOTS, t * P:(t + 1) * P] if t < 4 else psum[7][0:SLOTS, 0:P]
                        tr(dst, oneh[:, t, :], ident)
                    for t in range(TILES):
                        last_mm = mm(psum[7][0:SLOTS, P:P + 1], oneh[:, t, :], ecol[:, t, 0:1], start=(t == 0), stop=(t == 4))
                    last_mm.then_inc(oht_ps, 1)
                if not last and half and kind == "d" and b == 1:
                    pe.wait_ge(oht_ev, 3 * e + 3)
                    pe.wait_ge(oh_rd, e + 2)
                    gather(0)
                if not last and half and kind == "u" and b == 3:
                    pe.wait_ge(xs_f, 2 * e + 3)
                    gather(1)
                if half and kind == "d" and b == 2:
                    pe.wait_ge(ht_lo, 4 * e + 3)
                    hid_T(e, 3)
                if nxt and (kind, b, half) in SCATTER_AT:
                    if b == 0:
                        pe.wait_ge(xs_f, 2 * e + 4)
                    for j in SCATTER_AT[kind, b, half]:
                        scatter(e, j)
            if last:
                for j in range(2 * TILES):
                    scatter(e, j)

        with pe.Fori(0, LAST - 1, 2) as e:
            body(e, 0, False)
            body(e + 1, 1, False)
        body(LAST - 1, 0, False)
        body(LAST, 1, True)
        pe.wait_ge(gbias2, 16)
        pe.wait_ge(fs_add, 10 * NEXP + 1)
        gate_rows(rows)

    @block.vector
    def _(dve):
        tt, ts, stt, cp = nc.vector.tensor_tensor, nc.vector.tensor_scalar, nc.vector.scalar_tensor_tensor, nc.vector.tensor_copy
        steps = [0]

        def step(ins):
            steps[0] += 1
            ins.then_inc(dve_step, 1)
            dve.wait_ge(dve_step, steps[0])

        def bc(a, *shape):
            return a.unsqueeze(len(a.shape)).to_broadcast(list(a.shape) + list(shape))

        dve.wait_ge(par_ps, 1)
        cp(par[:, :], psum[7][:, 0:R_N]).then_inc(par_rd, 1)
        dve.wait_ge(par_rd, 1)
        lam = par[:, R_LAM:R_LAM + 8]
        stt(sm[:, S_ABS:S_ABS + 8], lam, -1.0, lam, ALU.mult, ALU.max).then_inc(lam_abs, 1)
        dve.wait_ge(sil_rd, 1)
        dve.wait_ge(cond_0, 1)
        sil2 = sil[:, :].rearrange("p (g k) -> p k g", g=2)
        parts = cond[:, :, 0:4].rearrange("p k (g a) -> p k g a", a=2)
        step(cp(parts[:, :, :, 0], sil2))
        tt(parts[:, :, :, 1], sil2, parts[:, :, :, 0], ALU.subtract).then_inc(cond_rd, 1)
        for n in range(WS):
            split_lo(dve, "dve", n)
        dve.wait_ge(lam_exp, 1)
        u, s, s2, q = (sm[:, a:a + 8] for a in (S_EXP, 16, S_T, S_T + 8))
        step(ts(s, u, 2.0, None, ALU.add))
        step(nc.vector.reciprocal(s, s))
        step(tt(s, s, u, ALU.mult))
        step(tt(s2, s, s, ALU.mult))
        step(ts(q, s2, 1.0 / 17, None, ALU.mult))
        for k in (15, 13, 11, 9, 7, 5, 3):
            step(stt(q, q, 1.0 / k, s2, ALU.add, ALU.mult))
        step(stt(q, q, 1.0, s, ALU.add, ALU.mult))
        step(ts(s2, lam, -1.0, 0.0, ALU.mult, ALU.max))
        step(stt(s, q, 2.0, s2, ALU.mult, ALU.add))
        ts(sm[:, S_C8:S_C8 + 8], s, -8.0, None, ALU.mult)
        ts(sm[:, S_NC8:S_NC8 + 8], s, 8.0, None, ALU.mult).then_inc(c8_rd, 1)

        def rstd(dst, src, n):
            rstd_start(dst, src, n)
            roots[1] += 1
            dve.wait_ge(root_out, roots[1])

        roots = [0, 0]

        def rstd_start(dst, src, n):
            step(ts(dst, src, 1.0 / n, EPS, ALU.mult, ALU.add))
            nc.vector.reciprocal(dst, dst).then_inc(root_in, 1)
            roots[0] += 1

        dve.wait_ge(x_sq, TILES)
        rstd(sm[:, S_RSTD:S_RSTD + TILES], sm[:, S_SS:S_SS + TILES], D)
        for t in range(TILES):
            ts(x_in[:, t, :], x_in[:, t, :], sm[:, S_RSTD + t:S_RSTD + t + 1], None, ALU.mult).then_inc(xn_rd, 1)

        def row_copy(i, bank, dst):
            used(dve, ada_chunk(i) + 1)
            if 1 <= i < 9:
                dve.wait_ge(col_ps, i)
            cp(dst[0:4, :], psum[bank][0:4, :]).then_inc(ada_row, 1)

        def col_out(i, bank, at):
            dve.wait_ge(col_ps, i + 1)
            tt(modc[:, :, 4 * i:4 * i + 4], psum[bank][:, at:at + 8].rearrange("p (q g) -> p g q", g=2),
               par[:, R_ADAB + 4 * i:R_ADAB + 4 * i + 4].unsqueeze(1).to_broadcast([P, 2, 4]), ALU.add).then_inc(col_rd, 1)

        for m in range(N_WIN):
            split_lo(dve, "dve", m + WS)
            if m % 2:
                row_copy(m // 2, 6, rows[:, 0:512])
            elif m >= 4:
                col_out(m // 2 - 2, 7, 128)
        col_out(2, 7, 128)
        col_out(3, 7, 128)
        dve.wait_ge(col_rd, 4)
        for g in range(2):
            step(stt(aff[:, 0, g, :], modc[:, g, 8:16], 1.0, par[:, R_PRE:R_PRE + 8], ALU.add, ALU.mult))

        def h_low(kt):
            dve.wait_ge(h_hi, kt + 1)
            tt(hT_lo[:, kt, :], hT_tmp[:, kt % 2, :], hT_hi[:, kt, :], ALU.subtract).then_inc(h_lo, 1)

        for kt in range(KT):
            dve.wait_ge(xT_ps, kt + 1)
            if kt >= 2:
                dve.wait_ge(h_lo, kt - 1)
            ts(hT_tmp[:, kt % 2, 0:LAT], psum[kt % 2][:, :], aff[:, 0, 0, kt:kt + 1], modc[:, 0, kt:kt + 1], ALU.mult, ALU.add)
            ts(hT_tmp[:, kt % 2, LAT:], psum[2 + kt % 2][:, 0:P], aff[:, 0, 1, kt:kt + 1],
               modc[:, 1, kt:kt + 1], ALU.mult, ALU.add).then_inc(h_tmp, 1)
            if kt:
                h_low(kt - 1)
        h_low(KT - 1)

        def conv(parts):
            w = [[par[:, R_CW + 4 * tap + ct:R_CW + 4 * tap + ct + 1] for tap in range(4)] for ct in range(CT)]
            for ct, src, dst in parts:
                last = ts(dst, src, w[ct][2], par[:, R_CB + ct:R_CB + ct + 1], ALU.mult, ALU.add)
            step(last)
            for tap, lo, hi in ((0, 2, 0), (1, 1, 0), (3, 0, 1)):
                for ct, src, dst in parts:
                    n = dst.shape[1]
                    a, b = slice(lo, n - hi), slice(hi, n - lo)
                    last = stt(dst[:, a], src[:, b], w[ct][tap], dst[:, a], ALU.mult, ALU.add)
                if tap < 3:
                    step(last)
            last.then_inc(xl_ev, 1)

        def conv_lat(ct):
            win_ready(dve, 1, ct)
            conv([(ct, psum[ct][:, :], xc[:, ct, 0:LAT])])

        def conv_ctx():
            conv([(ct, psum[5][:, ct * P:(ct + 1) * P], xc[:, ct, LAT:]) for ct in range(CT)])

        def rope_terms(i, dst, h):
            n = 4 * i + h
            win_ready(dve, 2 + i, h)
            if n == 0:
                dve.wait_ge(rope_in, 32)
            if n >= 2:
                dve.wait_ge(qk_rd, n - 1)
            tt(dst[:, h, 0:LAT], psum[h][:, :], rope_c, ALU.mult)
            tt(rope_tmp[0:64, n % 2, :], psum[h][64:128, :], rope_s[64:128, :], ALU.mult)
            tt(rope_tmp[64:128, n % 2, :], psum[h][0:64, :], rope_s[0:64, :], ALU.mult).then_inc(rope_t, 1)

        def lru_weight(ct):
            dve.wait_ge(lr_exp, 4 * (ct + 1))
            step(tt(lr_r, lr_a, lr_a, ALU.mult))
            stt(lr_t, lr_r, 1.0, lr_t, ALU.add, ALU.mult).then_inc(lr_w, 1)

        def lru_scan(ct):
            dve.wait_ge(lr_sq, ct + 1)
            dve.wait_ge(lr_gx, ct + 1)
            step(tt(lr_t, lr_t, lr_g, ALU.mult))
            for d, h0 in ((0, par[:, R_H0 + ct:R_H0 + ct + 1]), (1, par[:, R_H0 + 4 + ct:R_H0 + 5 + ct])):
                for lo, n, init in ((0, LAT, h0), (LAT, CTX, 0.0)):
                    o, a, b = (x[:, d, lo:lo + n] for x in (lr_r, lr_a, lr_t))
                    if d:
                        o, a, b = o[:, ::-1], a[:, ::-1], b[:, ::-1]
                    last = nc.vector.tensor_tensor_scan(o, a, b, init, ALU.mult, ALU.add)
            step(last)

        def lru_out(ct):
            cp(sm[:, S_ST + ct:S_ST + ct + 1], lr_r[:, 0, TOK - 1:TOK])
            step(cp(sm[:, S_ST + 4 + ct:S_ST + 5 + ct], lr_r[:, 1, LAT:LAT + 1]))
            step(tt(lr_r[:, 0, :], lr_r[:, 0, :], lr_r[:, 1, :], ALU.add))
            dve.wait_ge(yl_ev, 2 * CT)
            tt(gel[:, ct, :], gel[:, ct, :], lr_r[:, 0, :], ALU.mult).then_inc(lr_done, 1)

        for m in range(N_WIN, N_MID):
            bi, half = (m - N_WIN) // 2, m % 2
            parts = (lru_weight, lru_scan, lru_out) if half and bi >= 2 else ()
            for u in range(CT - 1):
                if half and bi == 1:
                    conv_lat(u)
                if half and bi in (2, 3):
                    rope_terms(bi - 2, (qT, kT)[bi - 2], u)
                if parts:
                    parts[u](bi - 2)
            split_lo(dve, "dve", m + WS)
            if half and bi == 1:
                conv_lat(CT - 1)
                conv_ctx()
            if half and bi in (2, 3):
                rope_terms(bi - 2, (qT, kT)[bi - 2], CT - 1)
        dve.wait_ge(lst_ps, 1)
        cp(lrow, psum[6][0:8, 0:P]).then_inc(lst_ev, 1)
        for ct in range(CT):
            dve.wait_ge(cat_hi, ct + 1)
            tt(hT_lo[:, ct, :], gel[:, ct, :], hT_hi[:, ct, :], ALU.subtract).then_inc(cat_lo, 1)

        def ret_mask(h):
            dve.wait_ge(dec_in[h % 2], 32 * (h // 2 + 1))
            for j in range(4):
                dve.wait_ge(sc_ps, 4 * h + j + 1)
                tt(sc[:, j, :], psum[j % 2][:, :], dec[:, h % 2, 384 - P * j:896 - P * j], ALU.mult).then_inc(sc_ev, 1)
            dve.wait_ge(scc_ps, h + 1)
            tt(sc_c, psum[5][:, 0:P], dec[:, h % 2, 384:512], ALU.mult).then_inc(scc_ev, 1)
            dve.wait_ge(kt_ps, h + 1)
            ts(kz[:, 0, :], psum[6][:, 3 * P:], zeta[:, h, 0:1], None, ALU.mult)
            ts(kz[:, 1, :], psum[6][:, 3 * P:], zeta[:, h, 1:2], None, ALU.mult).then_inc(kz_ev, 1)

        def ret_sum(h):
            dve.wait_ge(pv_ps, h + 1)
            cp(o_t[:, 4, :], psum[5][:, P:2 * P])
            for d in range(2):
                for t in range(4):
                    cross = psum[3 + t // 2][:, (t % 2) * 2 * DK + d * DK:(t % 2) * 2 * DK + (d + 1) * DK]
                    if d == 0:
                        last = ts(o_t[:, t, :], cross, xi[:, t, h, 0:1], None, ALU.mult)
                    else:
                        last = stt(o_t[:, t, :], cross, xi[:, t, h, 1:2], o_t[:, t, :], ALU.mult, ALU.add)
                step(last)
            tt(o_t[:, 0:4, :], o_t[:, 0:4, :], psum[2][:, :].rearrange("p (t e) -> p t e", t=4), ALU.add).then_inc(ret_rd, 1)

        def ret_norm(h):
            dve.wait_ge(ret_rd, h + 1)
            if h:
                dve.wait_ge(rt_ps, h)
            step(tt(ro_t, o_t, o_t, ALU.mult))
            step(nc.vector.tensor_reduce(sm[:, S_O:S_O + TILES], ro_t, AX.X, ALU.add))
            rstd(sm[:, S_O:S_O + TILES], sm[:, S_O:S_O + TILES], DK)
            step(tt(ro_t, o_t, bc(sm[:, S_O:S_O + TILES], DK), ALU.mult))
            if h == 0:
                dve.wait_ge(g_ev, TILES)
            tt(ro_t, ro_t, sg[:, :, h * DK:(h + 1) * DK], ALU.mult).then_inc(ret_o, 1)

        ret_mask(0)
        ret_sum(0)
        for h in range(HEADS):
            m0 = N_MID + 2 * h
            if h + 1 < HEADS:
                ret_mask(h + 1)
            ret_norm(h)
            row_copy(4 + h, 7, rows[:, 0:512])
            if h + 1 < HEADS:
                ret_sum(h + 1)
            col_out(4 + h, 7, 0)
            split_lo(dve, "dve", m0 + WS)
            dve.wait_ge(rt_hi, 2 * h + 2)
            tt(hT_lo[:, 4 + h, 0:LAT], psum[7][:, :], hT_hi[:, 4 + h, 0:LAT], ALU.subtract).then_inc(rt_lo, 1)
            tt(hT_lo[:, 4 + h, LAT:], psum[6][:, 0:P], hT_hi[:, 4 + h, LAT:], ALU.subtract).then_inc(rt_lo, 1)
            split_lo(dve, "dve", m0 + 1 + WS)

        for i in range(8, 12):
            if i == 10:
                dve.wait_ge(out_ret, 32 * HEADS)
                dve.wait_ge(out_lru, 16)
            row_copy(i, i % 2, (mg1 if i < 10 else rows[:, :])[:, (i % 2) * 512:(i % 2 + 1) * 512])
            for n in (N_GATES + 2 * (i - 8) + WS, N_GATES + 2 * (i - 8) + 1 + WS):
                split_lo(dve, "dve", n)

        def gate_row(first, banks=(2, 3, 5, 6)):
            dve.wait_ge(post_in, 16 * (first // 4 + 1))
            for g in range(2):
                for half in range(2):
                    at = slice(half * 512, (half + 1) * 512)
                    dve.wait_ge(gr_ps, first + 2 * g + half + 1)
                    tt(g_row[:, g, at], psum[banks[2 * g + half]][:, :], post[:, at], ALU.mult).then_inc(gr_ev, 1)

        gate_row(0)
        dve.wait_ge(col_rd, 8)
        for g in range(2):
            step(stt(aff[:, 1, g, :], modc[:, g, 24:32], 1.0, par[:, R_FPRE:R_FPRE + 8], ALU.add, ALU.mult))
        for n2 in range(2):
            for t in range(TILES):
                wout_ready(dve, n2, t)
                cp(x1[:, t, n2 * 512:(n2 + 1) * 512], psum[t][:, :]).then_inc(wo_ev, 1)
                if t in (1, 3):
                    split_lo(dve, "dve", N_WOUT + WS + 2 * n2 + t // 2)
        dve.wait_ge(wo_sq, 2 * TILES)
        both = sm[:, S_WO:S_WO + 2 * TILES].rearrange("p (t n) -> p t n", n=2)
        dve.wait_ge(gr_ev, 4)
        dve.wait_ge(wo_ev, 2 * TILES)
        step(tt(sm[:, S_T:S_T + TILES], both[:, :, 0], both[:, :, 1], ALU.add))
        rstd(sm[:, S_T:S_T + TILES], sm[:, S_T:S_T + TILES], D)
        dve.wait_ge(x_re, 16 * TILES)

        def norm2_start(t):
            dve.wait_ge(x1_sq, t + 1)
            rstd_start(sm[:, S_O + t:S_O + t + 1], sm[:, S_X1 + t:S_X1 + t + 1], D)

        def normed2(t):
            roots[1] += 1
            dve.wait_ge(root_out, roots[1])
            ts(xn2[:, t, :], x1[:, t, :], sm[:, S_O + t:S_O + t + 1], None, ALU.mult).then_inc(xn2_rd, 1)

        for t in range(TILES):
            step(stt(x1[:, t, :], x1[:, t, :], sm[:, S_T + t:S_T + t + 1], g_row[:, t // 4, :], ALU.mult, ALU.mult))
            tt(x1[:, t, :], x1[:, t, :], xn2[:, t, :], ALU.add).then_inc(x1_rd, 1)
            if t >= 1:
                norm2_start(t - 1)
            if t >= 2:
                normed2(t - 2)
        norm2_start(TILES - 1)
        normed2(TILES - 2)
        normed2(TILES - 1)
        for t in range(TILES):
            dve.wait_ge(h2_ps, 2 * t + 2)
            if t >= 2:
                dve.wait_ge(lg_ps, t - 1)
            dst, g = h2T[:, t % 2, 4:8, :], t // 4
            step(tt(dst, psum[2 * (t % 2) + 1][:, :].rearrange("p (k t) -> p k t", k=4), bc(aff[:, 1, g, 4:8], P), ALU.mult))
            tt(dst, dst, bc(modc[:, g, 20:24], P), ALU.add).then_inc(h2_dve, 1)
        lg = psum[4][:, 0:TILES * NEXP].rearrange("p (t e) -> p t e", t=TILES)
        ex = sm[:, 0:TILES * NEXP].rearrange("p (t e) -> p t e", t=TILES)
        dve.wait_ge(lg_ps, TILES)
        step(nc.vector.tensor_reduce(sm[:, S_MAX:S_MAX + TILES], lg, AX.X, ALU.max))
        tt(ex, lg, bc(sm[:, S_MAX:S_MAX + TILES], NEXP), ALU.subtract).then_inc(lg_sub, 1)
        dve.wait_ge(lg_exp, 1)
        step(nc.vector.tensor_reduce(sm[:, S_SUM:S_SUM + TILES], ex, AX.X, ALU.add))
        step(nc.vector.reciprocal(sm[:, S_REC:S_REC + TILES], sm[:, S_SUM:S_SUM + TILES]))
        tt(sp[:, :, 0, :], ex, bc(sm[:, S_REC:S_REC + TILES], NEXP), ALU.mult).then_inc(pr_rd, 1)
        dve.wait_ge(pt_ps, 1)
        ex16 = slice(0, NEXP)
        cp(pW[ex16, 0:LAT], psum[5][ex16, :])
        step(cp(pW[ex16, LAT:], psum[6][ex16, 0:P]))
        m8 = sm[ex16, S_T:S_T + 8]
        for at, cap in ((slice(0, LAT), CAP_L), (slice(LAT, TOK), CAP_C)):
            for _ in range(cap // 8):
                step(nc.vector.max(m8, pW[ex16, at]))
                step(nc.vector.match_replace(pW[ex16, at], m8, pW[ex16, at], -1.0))
        nc.vector.memset(pC[ex16, :], 1.0)
        step(ts(pS[ex16, :], pW[ex16, :], 0.0, None, ALU.is_lt))
        for at in (slice(0, LAT), slice(LAT, TOK)):
            last = nc.vector.tensor_tensor_scan(pT[ex16, at], pC[ex16, at], pS[ex16, at], 0.0, ALU.mult, ALU.add)
        step(last)
        tt(pS[ex16, :], pS[ex16, :], pT[ex16, :], ALU.mult).then_inc(sl_rd, 1)
        dve.wait_ge(sl_ps, 1)
        step(cp(sp[:, :, 1, :], psum[7][:, 0:TILES * NEXP].rearrange("p (t e) -> p t e", t=TILES)))

        def onehot(e1, e):
            cp(ecol[:, :, :], sp[:, :, :, bass.ds(e1, 1)].rearrange("p t a o -> p t (a o)")).then_inc(ec_rd, 1)
            dve.wait_ge(ec_rd, e + 1) if not isinstance(e, int) or e else dve.wait_ge(ec_rd, 1)
            for t in range(TILES):
                last = ts(oneh[:, t, :], iota[:, t // 4, :], ecol[:, t, 1:2], None, ALU.is_equal)
            last.then_inc(oh_rd, 1)

        def gathered(e, hf):
            dve.wait_ge(ga_ps, 2 * e + (hf + 1))
            ps = psum[7][:, 0:4 * SLOTS].rearrange("p (k s) -> p k s", k=4)
            dst = xs_tmp[:, hf, :].rearrange("p (k s) -> p k s", k=4)
            k4 = slice(4 * hf, 4 * hf + 4)
            for g, at, n in ((0, slice(0, CAP_L), CAP_L), (1, slice(CAP_L, SLOTS), CAP_C)):
                last = tt(dst[:, :, at], ps[:, :, at], bc(aff[:, 1, g, k4], n), ALU.mult)
            last.then_inc(xs_m, 1)
            dve.wait_ge(xs_m, 2 * e + (hf + 1))
            for g, at, n in ((0, slice(0, CAP_L), CAP_L), (1, slice(CAP_L, SLOTS), CAP_C)):
                last = tt(dst[:, :, at], dst[:, :, at], bc(modc[:, g, 16 + 4 * hf:20 + 4 * hf], n), ALU.add)
            last.then_inc(xs_f, 1)

        def gathered_lo(e, pr2, hf):
            dve.wait_ge(xs_h, 2 * e + (hf + 1))
            k4 = slice(4 * hf, 4 * hf + 4)
            tt(xs[pr2][1][:, k4, :], xs_tmp[:, hf, :].rearrange("p (k s) -> p k s", k=4), xs[pr2][0][:, k4, :],
               ALU.subtract).then_inc(xs_l, 1)

        def hidden(n, e, own, b):
            used(dve, n, e)
            dve.wait_ge(sl_ev, 4 * own + (b + 1))
            tt(hid[0:SLOTS, b % 2, :], psum[2 + b % 2][0:SLOTS, :], sgl[0:SLOTS, b % 2, :], ALU.mult).then_inc(hid_rd, 1)

        def hidT_lo(e, b):
            dve.wait_ge(ht_hi, 4 * e + (b + 1))
            tt(hidT[b % 2][1], psum[6][:, 0:4 * SLOTS], hidT[b % 2][0], ALU.subtract).then_inc(ht_lo, 1)

        onehot(0, 0)
        gathered(0, 0)
        gathered(0, 1)
        gathered_lo(0, 0, 0)
        gathered_lo(0, 0, 1)
        for i, (kind, b, half) in enumerate(FIRST_CHUNKS):
            split_lo(dve, "dve", N_EXP + i + WS)
            if half and kind == "u":
                hidden(N_EXP + i, 0, 0, 0)
        hidT_lo(0, 0)
        nc.vector.memset(facc[:, 4, :], 0.0).then_inc(fs_add, 1)
        dve.wait_ge(fz, 1)
        dve.wait_ge(fs_add, 1)

        def body(e, pr2, last):
            chunks = body_chunks(last)
            for i, (kind, b, half, nxt) in enumerate(chunks):
                if not last and (kind, b, half) == ("g", 3, 0):
                    gathered(e + 1, 0)
                if not last and (kind, b, half) == ("d", 2, 0):
                    gathered(e + 1, 1)
                if not last or i + WS < len(chunks):
                    split_lo(dve, "dve", N_BODY + i + WS, e)
                if not last and (kind, b, half) == ("g", 3, 0):
                    gathered_lo(e + 1, 1 - pr2, 0)
                if not last and (kind, b, half) == ("d", 2, 0):
                    gathered_lo(e + 1, 1 - pr2, 1)
                if not half:
                    if nxt:
                        for j in SCATTER_AT.get((kind, b, half), ()):
                            scattered(e, j)
                    continue
                if kind == "g" and b:
                    hidT_lo(e + nxt, b - 1)
                if kind == "u":
                    hidden(N_BODY + i, e, e + nxt, b)
                if kind == "u" and b == 1 and not last:
                    dve.wait_ge(oht_ps, e + 1)
                    onehot(e + 1, e + 1)
                if kind == "d" and b == 2:
                    hidT_lo(e, 3)
                if kind == "d" and b == 3:
                    for hf in range(2):
                        dve.wait_ge(ye_h, 2 * e + (hf + 1))
                        at = slice(hf * 512, (hf + 1) * 512)
                        stt(ye[1][:, at], psum[4 + hf][0:SLOTS, :], gate[0:SLOTS, 0:1], ye[0][:, at], ALU.mult,
                            ALU.subtract).then_inc(ye_l, 1)
                if nxt:
                    for j in SCATTER_AT.get((kind, b, half), ()):
                        scattered(e, j)
            if last:
                for j in range(2 * TILES):
                    scattered(e, j)

        def scattered(e, i):
            dst = facc[:, i // 2, (i % 2) * 512:(i % 2 + 1) * 512]
            dve.wait_ge(fs_ps, 10 * e + (i + 1))
            tt(dst, dst, psum[SCATTER_BANKS[i]][:, :], ALU.add).then_inc(fs_add, 1)

        with dve.Fori(0, LAST - 1, 2) as e:
            body(e, 0, False)
            body(e + 1, 1, False)
        body(LAST - 1, 0, False)
        body(LAST, 1, True)
        gate_row(4)
        dve.wait_ge(fin_sq, TILES)
        rstd(sm[:, S_O:S_O + TILES], sm[:, S_FIN:S_FIN + TILES], D)
        dve.wait_ge(gr_ev, 8)
        for t in range(TILES):
            step(stt(facc[:, t, :], facc[:, t, :], sm[:, S_O + t:S_O + t + 1], g_row[:, t // 4, :], ALU.mult, ALU.mult))
            tt(facc[:, t, :], facc[:, t, :], x1[:, t, :], ALU.add).then_inc(fin_y, 1)

    @block.gpsimd
    def _(pool):
        nc.gpsimd.memset(cond[:, :, :].bitcast(F32), 0.0).then_inc(cond_0, 1)
        for n in range(WS):
            split_lo(pool, "pool", n)
        for m in range(N_WIN):
            split_lo(pool, "pool", m + WS)
        for m in range(N_WIN, N_MID):
            bi, half = (m - N_WIN) // 2, m % 2
            split_lo(pool, "pool", m + WS)
            if half and bi in (2, 3):
                for h in range(HEADS):
                    pool.wait_ge(rope_t, 4 * (bi - 2) + h + 1)
                    dst = (qT, kT)[bi - 2][:, h, 0:LAT]
                    nc.gpsimd.tensor_tensor(dst, dst, rope_tmp[:, h % 2, :], ALU.add).then_inc(qk_rd, 1)
            if m - N_WIN - 4 in GATES_AT:
                ct = GATES_AT[m - N_WIN - 4]
                pool.wait_ge(gt_ev, 8 * (ct + 1))
                nc.gpsimd.tensor_tensor(lr_g, lr_g, xc[:, ct, :].unsqueeze(1).to_broadcast([P, 2, TOK]), ALU.mult).then_inc(lr_gx, 1)
        for n in range(N_MID + WS, N_EXP + WS):
            split_lo(pool, "pool", n)
        pool.wait_ge(sl_ps, 1)
        nc.gpsimd.memset(facc[:, 0:4, :], 0.0).then_inc(fz, 1)
        for n in range(N_EXP + WS, N_BODY + WS):
            split_lo(pool, "pool", n)

        def body(e, last):
            for i in range(len(body_chunks(last)) - (WS if last else 0)):
                split_lo(pool, "pool", N_BODY + i + WS, e)

        with pool.Fori(0, LAST) as e:
            body(e, False)
        body(LAST, True)

    ctx.close()


def tables():
    import numpy as np

    f = np.float64
    dec_f = np.log1p(-np.exp2(-(5.0 + np.arange(HEADS, dtype=f))))
    dec_b = np.log1p(-np.exp2(-(5.5 + np.arange(HEADS, dtype=f))))
    scale = DK ** -0.5
    diff = np.arange(896)[None, :] - 384 - np.arange(P)[:, None]
    decay = np.where(diff >= 0, np.exp(np.maximum(diff, 0) * dec_f[:, None, None]),
                     np.exp(np.maximum(-diff, 0) * dec_b[:, None, None])) * scale
    pos = np.arange(LAT, dtype=f).reshape(4, P)
    xi = np.stack([np.exp((pos[..., None] + 1) * dec_f), np.exp((LAT - pos[..., None]) * dec_b)], -1) * scale
    j = np.arange(CTX, dtype=f)[:, None]
    zeta = np.stack([np.exp((CTX - 1 - j) * dec_f), np.exp(j * dec_b)], -1)
    const = np.zeros((P, C_N))
    const[:, C_ID:C_ID + P] = np.eye(P)
    const[:, C_XI:C_XI + 32] = xi.transpose(1, 0, 2, 3).reshape(P, 32)
    const[:, C_ZETA:C_ZETA + 8] = zeta.reshape(P, 8)
    const[:, C_IOTA:C_IOTA + 2 * SLOTS] = np.concatenate(
        [np.arange(1, CAP_L + 1), np.full(CAP_C, -1), np.full(CAP_L, -1), np.arange(1, CAP_C + 1)])
    const[0:4, C_SELC:C_SELC + 2] = [[1, 0], [1, 0], [0, 1], [0, 1]]
    selb = const[:, C_SELB:C_SELB + 2 * P].reshape(P, 2, P)
    for g in range(2):
        selb[2 * g:2 * g + 2, g, :] = 1
        selb[4, g, :] = 1
    const[:, C_SELB:C_SELB + 2 * P] = selb.reshape(P, 2 * P)
    grid = np.float32(64)
    row, col = np.arange(LAT) // 64, np.arange(LAT) % 64
    nf = DK // 4
    freqs = 10000.0 ** (-np.arange(nf, dtype=f) / nf)
    ang = np.concatenate([row[:, None] * freqs, col[:, None] * freqs], -1).T
    rope = np.stack([np.concatenate([np.cos(ang)] * 2), np.concatenate([np.sin(ang), -np.sin(ang)])])
    return {"consts": const.astype(np.float32), "decay": decay.astype(np.float32), "rope": rope.astype(np.float32)}


def kernel(x_prompt, x_sample, c, state_lru, state_ret, c_ctx, ada_w, ada_b, norm_mix_pre, norm_mix_post,
           norm_ffn_pre, norm_ffn_post, w_in, conv_w, conv_b, lru_wa, lru_ba, lru_wi, lru_bi, lru_lambda,
           w_out, router_w, exp_w_gate, exp_w_up, exp_w_down):
    import numpy as np
    import concourse.bacc as bacc
    from concourse.bass_utils import run_bass_kernel_spmd

    ins = {
        "x_ctx": x_prompt[0], "x_lat": x_sample[0], "c": c.reshape(8, P), "state_lru": state_lru.reshape(8, P),
        "state_ret": state_ret.reshape(2, HEADS, DK, DK), "c_ctx": c_ctx.reshape(8, P), "ada_w": ada_w[0],
        "ada_b": ada_b.reshape(48, P), "norm_mix_pre": norm_mix_pre.reshape(8, P), "norm_mix_post": norm_mix_post[0],
        "norm_ffn_pre": norm_ffn_pre.reshape(8, P), "norm_ffn_post": norm_ffn_post[0], "w_in": w_in[0],
        "conv_w": conv_w.reshape(16, P), "conv_b": conv_b.reshape(4, P), "lru_wa": lru_wa[0], "lru_ba": lru_ba.reshape(8, P),
        "lru_wi": lru_wi[0], "lru_bi": lru_bi.reshape(8, P), "lru_lambda": lru_lambda.reshape(8, P), "w_out": w_out[0],
        "router_w": router_w[0], "exp_gate": exp_w_gate[0], "exp_up": exp_w_up[0], "exp_down": exp_w_down[0],
        **tables(),
    }
    outs = {"y_ctx": (CTX, D), "y_lat": (LAT, D), "new_lru": (8, P), "new_ret": (2, HEADS, DK, DK)}
    nc = bacc.Bacc("TRN2", target_bir_lowering=False, num_devices=1)
    arrays, args = {}, {}
    for name, a in ins.items():
        arrays[f"in_{name}"] = np.ascontiguousarray(a)
        args[name] = nc.dram_tensor(f"in_{name}", a.shape, F32, kind="ExternalInput").ap()
    for name, shape in outs.items():
        args[name] = nc.dram_tensor(f"out_{name}", shape, F32, kind="ExternalOutput").ap()
    build(nc, **args)
    r = run_bass_kernel_spmd(nc, [arrays], core_ids=[0]).results[0]
    return (r["out_y_ctx"].reshape(1, CTX, D), r["out_y_lat"].reshape(1, LAT, D),
            r["out_new_lru"].reshape(1, 1, 2, LW), r["out_new_ret"].reshape(1, 1, 2, HEADS, DK, DK))
```

```python
from contextlib import ExitStack

import concourse.bass as bass
from concourse import mybir

F32 = mybir.dt.float32
F32R = mybir.dt.float32r
ALU = mybir.AluOpType
ACT = mybir.ActivationFunctionType
AX = mybir.AxisListType

P = 128
D = 1024
KT = D // P
LAT, CTX = 512, 128
TOK = LAT + CTX
TILES = TOK // P
LW = 512
CT = LW // P
HEADS, DK = 4, 128
NEXP = 16
CAP_L, CAP_C = 2 * LAT // NEXP, 2 * CTX // NEXP
SLOTS = CAP_L + CAP_C
FF = 2 * D
NB = FF // 512
EPS = 1e-6

RAW, WS = 4, 3
CH = 2048

ADA_FIRST = [0, 1, 2, 3]
WIN = [1, 0, 2, 3, 4, 5]
ADA_MID = [6, 7, 8, 9]
ADA_GATES = [4, 5, 10, 11]
N_WIN = 2 * len(ADA_FIRST)
N_MID = N_WIN + 2 * len(WIN)
N_GATES = N_MID + 2 * len(ADA_MID)
N_WOUT = N_GATES + 2 * len(ADA_GATES)
N_EXP = N_WOUT + 4
PER_E = 24
N_BODY = N_EXP + 6
DVE_COLS = 1536

S_ABS, S_EXP, S_C8, S_NC8, S_SS, S_RSTD, S_WO, S_X1 = 0, 8, 24, 32, 40, 58, 48, 64
S_FIN, S_MAX, S_SUM, S_REC, S_T, S_ST, S_O = 80, 88, 93, 98, 104, 112, 120
GATES_AT = {0: 0, 2: 1, 4: 2, 6: 3}
C_ID, C_XI, C_ZETA, C_IOTA, C_SELC, C_SELB = 0, 128, 160, 168, 328, 330
C_N = 586
R_C, R_PRE, R_FPRE, R_CW, R_CB, R_BA, R_BI, R_LAM, R_H0, R_ADAB = 0, 16, 24, 32, 48, 52, 60, 68, 76, 84
R_N = 116


def build(nc, x_ctx, x_lat, vectors, state_ret, ada_w, ada_b, norm_mix_post, norm_ffn_post, w_in, lru_wa, lru_wi,
          w_out, router_w, exp_gate, exp_up, exp_down, consts, decay, rope, y_ctx, y_lat, new_lru, new_ret):
    ctx = ExitStack()
    sb = lambda n, s, d=F32: ctx.enter_context(nc.sbuf_tensor(n, s, d))
    sem = lambda n: ctx.enter_context(nc.semaphore(n))

    raw = sb("raw", [P, RAW, CH])
    w_hi = sb("w_hi", [P, WS, CH], F32R)
    w_lo = sb("w_lo", [P, WS, CH], F32R)
    act_hi = sb("act_hi", [P, KT * TOK], F32R)
    act_lo = sb("act_lo", [P, KT * TOK], F32R)
    arena = sb("arena", [P, 18944])
    const = sb("const", [P, C_N])
    rows = sb("rows", [P, D])
    cond = sb("cond", [P, KT, 66], F32R)
    par = sb("par", [P, R_N])
    sil = sb("sil", [P, 16])
    modc = sb("modc", [P, 2, 32])
    aff = sb("aff", [P, 2, 2, KT])
    rw = sb("rw", [P, KT, NEXP])
    sp = sb("sp", [P, TILES, 2, NEXP])
    ecol = sb("ecol", [P, TILES, 2])
    gate = sb("gate", [P, 1])
    sm = sb("sm", [P, 128])
    psum = [ctx.enter_context(nc.psum_tensor(f"bank{i}", [P, 512], F32)) for i in range(8)]

    def region(at, *shape):
        n = 1
        for s in shape:
            n *= s
        v = arena[:, at:at + n]
        if len(shape) == 1:
            return v
        names = " ".join("abcd"[:len(shape)])
        return v.rearrange(f"p ({names}) -> p {names}", **{"abcd"[i]: shape[i] for i in range(len(shape))})

    gel = region(0, CT, TOK)
    qT = region(2560, HEADS, TOK)
    kT = region(5120, HEADS, TOK)
    v_t = region(7680, TILES, LW)
    xc = region(10240, CT, TOK)
    sg = region(10240, TILES, LW)
    x_in = region(12800, TILES, D)
    hT_tmp = region(0, 2, TOK)
    junk0 = region(5120, D)
    rope_tmp = region(7680, 2, LAT)
    par_rows = region(2560, P)
    lr_r, lr_g, lr_a, lr_t = (region(12800 + i * 2 * TOK, 2, TOK) for i in range(4))
    rope_c, rope_s = region(17920, LAT), region(17920 + LAT, LAT)
    sc = region(12800, 4, LAT)
    sc_c = region(14848, CTX)
    dec = region(14976, 2, 896)
    s0 = region(16768, 2, 2 * DK)
    o_t = region(17280 , TILES, DK)
    ro_t = region(17920, TILES, DK)
    kz = region(18560, 2, DK)
    x1 = region(0, TILES, D)
    xn2 = region(5120, TILES, D)
    facc = region(10240, TILES, D)
    h2T = region(10240, 2, KT, P)
    junk = region(12288, D)
    rw_mod = region(14336, 2, KT, NEXP)
    pT, pW, pS, pC = (region(10240 + i * TOK, TOK) for i in range(4))
    g_row = region(15360, 2, D)
    post = region(17408, D)
    mg1 = region(13312, D)
    sgl = region(15360, 2, 512)
    hid = region(16384, 2, 512)
    oneh = region(17408, TILES, SLOTS)
    xs_tmp = region(17808, 2, 4 * SLOTS)

    hT_hi = act_hi[:, :].rearrange("p (k t) -> p k t", k=KT)
    hT_lo = act_lo[:, :].rearrange("p (k t) -> p k t", k=KT)
    xs = [[a[:, i * KT * SLOTS:(i + 1) * KT * SLOTS].rearrange("p (k s) -> p k s", k=KT) for a in (act_hi, act_lo)]
          for i in range(2)]
    hidT = [[a[:, 1280 + i * 4 * SLOTS:1280 + (i + 1) * 4 * SLOTS] for a in (act_hi, act_lo)] for i in range(2)]
    ye = [a[0:SLOTS, 1920:1920 + D] for a in (act_hi, act_lo)]
    onehotT = act_hi[0:SLOTS, 2944:2944 + TOK]

    ident = const[:, C_ID:C_ID + P]
    xi = const[:, C_XI:C_XI + 32].rearrange("p (t h d) -> p t h d", t=4, h=HEADS)
    zeta = const[:, C_ZETA:C_ZETA + 8].rearrange("p (h d) -> p h d", h=HEADS)
    iota = const[:, C_IOTA:C_IOTA + 2 * SLOTS].rearrange("p (g s) -> p g s", g=2)
    selc = const[:, C_SELC:C_SELC + 2]
    selb = const[:, C_SELB:C_SELB + 2 * P].rearrange("p (g m) -> p g m", g=2)
    lst = rows[:, 512:768]
    lrow = rows[0:8, 768:896]
    gw = (region(8704, 2, 2, 2, P), rows[:, :].rearrange("p (c k d j) -> p c k d j", c=2, k=2, d=2))

    const_in, par_in, x_ld, x_re, rw_in, gw_in, rope_in = map(sem, (
        "const_in", "par_in", "x_loaded", "x_reloaded", "router_in", "lru_gates_in", "rope_in"))
    gbias1, gbias2, post_in, dec_in = map(sem, ("gate1_bias_in", "gate2_bias_in", "post_gain_in", "decay_in"))
    dec_in = [dec_in, sem("decay_in_odd")]
    raw_in = [sem(f"raw_in{i}") for i in range(RAW)]
    out_lru, out_ret, out_y = map(sem, ("lru_state_out", "ret_state_out", "y_out"))
    hi_done, lo_dve, lo_pool, w_used = map(sem, ("hi_done", "lo_done_dve", "lo_done_pool", "w_used"))
    dve_step, act_step, pool_step = map(sem, ("dve_step", "act_step", "pool_step"))
    par_ps, par_rd, sil_rd, lam_abs, lam_exp, cond_0, cond_rd, c8_rd = map(sem, (
        "par_ps", "par_ready", "silu_ready", "lambda_abs", "lambda_exp", "cond_zeroed", "cond_ready", "c8_ready"))
    ada_row, col_ps, col_rd = map(sem, ("ada_row", "columns_ps", "columns_ready"))
    x_sq, xn_rd, xT_ps, h_tmp, h_hi, h_lo = map(sem, ("x_squares", "xn_ready", "xT_ps", "h_tmp", "h_hi", "h_lo"))
    win_ps, yl_ev, xl_ev, rope_t, qk_rd, qk_ctx, v_ev, g_ev = map(sem, (
        "win_ps", "yl_out", "conv_done", "rope_terms", "qk_ready", "qk_ctx_out", "v_out", "g_out"))
    gt_ps, gt_ev, lr_exp, lr_gx, lr_w, lr_sq, lr_done = map(sem, (
        "lru_gate_ps", "lru_gates_out", "lru_exp", "lru_gx", "lru_w", "lru_sqrt", "lru_done"))
    cat_hi, cat_lo = sem("lru_cat_hi"), sem("lru_cat_lo")
    sc_ps, sc_ev, scc_ps, scc_ev, pv_ps, ret_rd, kt_ps, kz_ev, st_ps, st_ev, ret_o, rt_ps, rt_hi, rt_lo = map(sem, (
        "score_ps", "score_masked", "ctx_score_ps", "ctx_score_masked", "pv_ps", "ret_read", "kT_ps", "kz_ready",
        "state_ps", "state_copied", "ret_out", "ret_T_ps", "ret_T_hi", "ret_T_lo"))
    lst_ps, lst_ev = sem("lru_state_ps"), sem("lru_state_row")
    gr_ps, gr_ev, wo_ps, wo_ev, wo_sq, x1_rd, x1_sq, xn2_rd = map(sem, (
        "gate_row_ps", "gate_row", "wout_ps", "wout_copied", "wout_squares", "x1_ready", "x1_squares", "xn2_ready"))
    h2_ps, h2_act, h2_dve, lg_ps, lg_sub, lg_exp, pr_rd, pt_ps, sl_rd, sl_ps, fz = map(sem, (
        "h2_ps", "h2_act", "h2_dve", "logits_ps", "logits_less_max", "logits_exp", "probs_ready", "probsT_ps",
        "slots_ready", "slots_ps", "facc_zeroed"))
    sl_ev, hid_rd, ht_ps, ht_hi, ht_lo = map(sem, ("silu_out", "hid_ready", "hidT_ps", "hidT_hi", "hidT_lo"))
    oh_rd, oht_ps, oht_ev, ga_ps, xs_f, xs_h, xs_l, ye_h, ye_l, fs_ps, fs_add = map(sem, (
        "onehot_ready", "onehotT_ps", "onehotT_out", "gather_ps", "gathered", "gathered_hi", "gathered_lo",
        "ye_hi", "ye_lo", "scatter_ps", "scatter_added"))
    rwm_rd, gw_0 = sem("router_modulated"), sem("lru_gates_zeroed")
    ec_rd, xs_m = sem("expert_columns"), sem("gathered_scaled")
    root_in, root_out = sem("root_argument"), sem("root_taken")
    fin_sq, fin_y = sem("f_squares"), sem("y_ready")

    aw = ada_w.rearrange("(k p) n -> p k n", p=P)
    wi = w_in.rearrange("(k p) n -> p k n", p=P)
    wo = w_out.rearrange("(k p) n -> p k n", p=P)

    def block_cols(w, blk, half):
        return w[:, 4 * half:4 * half + 4, blk * 512:(blk + 1) * 512]

    def prologue_source(n):
        if n < N_WIN:
            return block_cols(aw, ADA_FIRST[n // 2], n % 2)
        if n < N_MID:
            return block_cols(wi, WIN[(n - N_WIN) // 2], n % 2)
        if n < N_GATES:
            return block_cols(aw, ADA_MID[(n - N_MID) // 2], n % 2)
        if n < N_WOUT:
            return block_cols(aw, ADA_GATES[(n - N_GATES) // 2], n % 2)
        return block_cols(wo, (n - N_WOUT) // 2, n % 2)

    def expert_source(e, kind, b, half):
        if kind == "d":
            w = exp_down[bass.ds(e, 1), b * 512:(b + 1) * 512, :].rearrange("o (p j) n -> p (o j) n", p=P)
            return w[:, 2 * half:2 * half + 2, :]
        w = {"g": exp_gate, "u": exp_up}[kind]
        w = w[bass.ds(e, 1), :, b * 512:(b + 1) * 512].rearrange("o (k p) n -> p (o k) n", p=P)
        return w[:, 4 * half:4 * half + 4, :]

    def body_chunks(last):
        order = [("u", 1, 0), ("d", 0, 0), ("g", 2, 0), ("u", 2, 0), ("d", 1, 0), ("g", 3, 0), ("u", 3, 0), ("d", 2, 0)]
        if not last:
            order += [("g", 0, 1)]
        order += [("d", 3, 0)]
        if not last:
            order += [("u", 0, 1), ("g", 1, 1)]
        return [(kind, b, half, nxt) for kind, b, nxt in order for half in range(2)]

    FIRST_CHUNKS = [(kind, b, half) for kind, b in (("g", 0), ("u", 0), ("g", 1)) for half in range(2)]

    SCATTER_BANKS = (7, 6, 4, 5, 7, 6, 4, 5, 7, 4)
    SCATTER_AT = {("u", 0, 1): range(0, 4), ("g", 1, 0): range(4, 7), ("g", 1, 1): range(7, 10)}

    def chunk_view(ring, n, cols):
        return ring[:, n % ring.shape[1], :].rearrange("p (k n) -> p k n", n=cols)

    def load(sp_e, n, e, src, cols):
        if n >= RAW or not isinstance(e, int):
            sp_e.wait_ge(lo_pool, e * PER_E + (n - RAW + 1))
            sp_e.wait_ge(lo_dve, e * PER_E + (n - RAW + 1))
        sp_e.dma_start(chunk_view(raw, n, cols), src).then_inc(raw_in[n % RAW], 16)

    def split_hi(act, n, e=0):
        act.wait_ge(raw_in[n % RAW], e * (16 * PER_E // RAW) + 16 * (n // RAW + 1))
        if n >= WS:
            act.wait_ge(w_used, e * PER_E + (n - WS + 1))
        nc.scalar.copy(w_hi[:, n % WS, :], raw[:, n % RAW, :]).then_inc(hi_done, 1)

    def split_lo(eng, who, n, e=0):
        eng.wait_ge(hi_done, e * PER_E + (n + 1))
        ops, done, at = {"dve": (nc.vector, lo_dve, slice(0, DVE_COLS)), "pool": (nc.gpsimd, lo_pool, slice(DVE_COLS, CH))}[who]
        ops.tensor_tensor(w_lo[:, n % WS, at], raw[:, n % RAW, at], w_hi[:, n % WS, at], ALU.subtract).then_inc(done, 1)

    def chunk_ready(pe, n, e=0):
        pe.wait_ge(lo_dve, e * PER_E + (n + 1))
        pe.wait_ge(lo_pool, e * PER_E + (n + 1))

    def used(eng, n, e=0):
        eng.wait_ge(w_used, e * PER_E + (n + 1))

    def ada_chunk(i):
        return (0, N_MID - 8, N_GATES - 16)[i // 4] + 2 * i

    def win_ready(eng, bi, u):
        if u == (CT if bi < 4 else TILES) - 1:
            used(eng, N_WIN + 2 * bi + 1)
        else:
            eng.wait_ge(win_ps, (0, 3, 6, 9, 12, 16)[bi] + u + 1)

    def wout_ready(eng, n2, t):
        if t == TILES - 1:
            used(eng, N_WOUT + 2 * n2 + 1)
        else:
            eng.wait_ge(wo_ps, 4 * n2 + t + 1)

    def three(out, lh, ll, rh, rl, start, stop, **kw):
        nc.tensor.matmul(out, lh, rl, start=start, stop=False, **kw)
        nc.tensor.matmul(out, ll, rh, start=False, stop=False, **kw)
        return nc.tensor.matmul(out, lh, rh, start=False, stop=stop, **kw)

    LAST = NEXP - 1
    block = ctx.enter_context(nc.Block())

    @block.sync
    def _(sync):
        for n in range(N_EXP):
            load(sync, n, 0, prologue_source(n), 512)
            if n == N_WIN + 6:
                sync.wait_ge(gw_0, 2)
                for kind, w in ((0, lru_wa), (1, lru_wi)):
                    for par_h in range(2):
                        at = slice(64 * par_h, 64 * par_h + 64)
                        for d in range(2):
                            heads = w[d, par_h::2].rearrange("h i j -> i h j")
                            for i in range(2):
                                sync.dma_start(gw[i][at, :, kind, d, at], heads[:, 2 * i:2 * i + 2, :]).then_inc(gw_in, 16)
        for i, (kind, b, half) in enumerate(FIRST_CHUNKS):
            load(sync, N_EXP + i, 0, expert_source(0, kind, b, half), 512)

        def body(e, last):
            for i, (kind, b, half, nxt) in enumerate(body_chunks(last)):
                load(sync, N_BODY + i, e, expert_source(e + nxt, kind, b, half), D if kind == "d" else 512)

        with sync.Fori(0, LAST) as e:
            sync.compute_val(e * (FF * D) * 4)
            body(e, False)
        body(LAST, True)
        sync.wait_ge(out_lru, 16)
        sync.wait_ge(out_ret, 16 * 2 * HEADS)
        sync.wait_ge(out_y, 16 * TILES)

    @block.scalar
    def _(act):
        act.dma_start(par_rows[0:R_N, :], vectors).then_inc(par_in, 16)
        act.dma_start(const[:, :], consts).then_inc(const_in, 16)
        for t in range(TILES):
            act.dma_start(x_in[:, t, :], x_lat[t * P:(t + 1) * P, :] if t < 4 else x_ctx).then_inc(x_ld, 16)
        split_hi(act, 0)
        act.wait_ge(par_rd, 1)
        nc.scalar.activation(sil[:, :], par[:, R_C:R_C + 16], ACT.Silu).then_inc(sil_rd, 1)
        split_hi(act, 1)
        split_hi(act, 2)
        act.dma_start(rw[:, :, :], router_w.rearrange("(k p) n -> p k n", p=P)).then_inc(rw_in, 16)
        act.dma_start(rope_c, rope[0]).then_inc(rope_in, 16)
        act.dma_start(rope_s, rope[1]).then_inc(rope_in, 16)
        split_hi(act, WS)
        act.wait_ge(x_ld, 16 * TILES)
        for t in range(TILES):
            if t:
                act.wait_ge(x_sq, t)
            nc.scalar.activation(junk0, x_in[:, t, :], ACT.Square, accum_out=sm[:, S_SS + t:S_SS + t + 1]).then_inc(x_sq, 1)
            if t == 1:
                split_hi(act, WS + 1)
        roots = [0]

        def root(at, n=TILES):
            roots[0] += 1
            act.wait_ge(root_in, roots[0])
            nc.scalar.activation(sm[:, at:at + n], sm[:, at:at + n], ACT.Sqrt).then_inc(root_out, 1)

        for n in range(WS + 2, N_WIN + WS):
            split_hi(act, n)
            if n == WS + 4:
                root(S_RSTD)
        act.wait_ge(lam_abs, 1)
        nc.scalar.activation(sm[:, S_EXP:S_EXP + 8], sm[:, S_ABS:S_ABS + 8], ACT.Exp, scale=-1.0).then_inc(lam_exp, 1)
        for kt in range(KT):
            act.wait_ge(h_tmp, kt + 1)
            nc.scalar.copy(hT_hi[:, kt, :], hT_tmp[:, kt % 2, :]).then_inc(h_hi, 1)

        def yl_out(ct):
            win_ready(act, 0, ct)
            if ct == 0:
                act.wait_ge(h_lo, KT)
            nc.scalar.activation(gel[:, ct, 0:LAT], psum[ct][:, :], ACT.Gelu_apprx_tanh).then_inc(yl_ev, 1)

        def yl_ctx_out(ct):
            nc.scalar.activation(gel[:, ct, LAT:], psum[4][:, ct * P:(ct + 1) * P], ACT.Gelu_apprx_tanh).then_inc(yl_ev, 1)

        def qk_ctx_out(i, dst, bank):
            win_ready(act, 2 + i, CT - 1)
            nc.scalar.copy(dst[:, :, LAT:], psum[bank][:, :].rearrange("p (h t) -> p h t", h=HEADS)).then_inc(qk_ctx, 1)

        def lru_gates_out(s):
            ct, d, ctxp = s // 4, s // 2 % 2, s % 2
            act.wait_ge(gt_ps, s + 1)
            if s % 4 == 0:
                if ct:
                    act.wait_ge(lr_done, ct)
                else:
                    act.wait_ge(xn_rd, TILES)
                    act.wait_ge(xT_ps, KT)
            for kind, dst, r0 in ((0, lr_r, R_BA), (1, lr_g, R_BI)):
                src = psum[6][:, kind * P:(kind + 1) * P] if ctxp else psum[6 + kind][:, :]
                at = slice(LAT, TOK) if ctxp else slice(0, LAT)
                nc.scalar.activation(dst[:, d, at], src, ACT.Sigmoid,
                                     bias=par[:, r0 + 4 * d + ct:r0 + 4 * d + ct + 1]).then_inc(gt_ev, 1)

        def lru_exp(ct):
            act.wait_ge(gt_ev, 8 * (ct + 1))
            if ct == 0:
                act.wait_ge(c8_rd, 1)
            for d in range(2):
                j = 4 * d + ct
                nc.scalar.activation(lr_a[:, d, :], lr_r[:, d, :], ACT.Exp, scale=sm[:, S_C8 + j:S_C8 + j + 1]).then_inc(lr_exp, 1)
                nc.scalar.activation(lr_t[:, d, :], lr_r[:, d, :], ACT.Tanh, scale=sm[:, S_NC8 + j:S_NC8 + j + 1]).then_inc(lr_exp, 1)

        def lru_sqrt(ct):
            act.wait_ge(lr_w, ct + 1)
            nc.scalar.activation(lr_t[:, :, :], lr_t[:, :, :], ACT.Sqrt).then_inc(lr_sq, 1)

        def lru_cat(ct):
            act.wait_ge(lr_done, ct + 1)
            if ct == 0:
                used(act, N_MID - 1)
            nc.scalar.copy(hT_hi[:, ct, :], gel[:, ct, :]).then_inc(cat_hi, 1)

        def tok_out(i, t):
            win_ready(act, 4 + i, t)
            bank = psum[t] if t < 4 else psum[4 + i]
            if i == 0:
                if t == 0:
                    act.wait_ge(qk_rd, 2 * HEADS)
                nc.scalar.copy(v_t[:, t, :], bank[:, :]).then_inc(v_ev, 1)
            else:
                if t == 0:
                    act.wait_ge(lr_gx, CT)
                nc.scalar.activation(sg[:, t, :], bank[:, :], ACT.Silu).then_inc(g_ev, 1)

        def ret_loads(h):
            if h == 0:
                act.wait_ge(lr_done, CT)
                act.wait_ge(rope_t, 2 * HEADS)
                act.wait_ge(qk_rd, 2 * HEADS)
            if h >= 2:
                act.wait_ge(sc_ev, 4 * (h - 1))
                act.wait_ge(scc_ev, h - 1)
                act.wait_ge(pv_ps, h - 1)
            act.dma_start(dec[:, h % 2, :], decay[h]).then_inc(dec_in[h % 2], 16)
            act.dma_start(s0[:, h % 2, :].rearrange("p (d e) -> p d e", d=2),
                          state_ret[:, h].rearrange("d k e -> k d e")).then_inc(dec_in[h % 2], 16)

        for m in range(N_WIN, N_MID):
            bi, half = (m - N_WIN) // 2, m % 2
            ct = GATES_AT.get(m - N_WIN - 4)
            if ct is not None:
                for s in range(4 * ct, 4 * ct + 4):
                    lru_gates_out(s)
            if half and bi == 0:
                for u in range(CT - 1):
                    yl_out(u)
            if half and bi >= 4:
                for t in range(TILES - 1):
                    tok_out(bi - 4, t)
            if half and bi == 5:
                tok_out(1, TILES - 1)
                ret_loads(0)
                ret_loads(1)
            split_hi(act, m + WS)
            if half and bi == 0:
                yl_out(CT - 1)
                for u in range(CT):
                    yl_ctx_out(u)
            if half and bi in (2, 3):
                qk_ctx_out(bi - 2, (qT, kT)[bi - 2], 4 + bi % 2)
            if half and bi == 4:
                tok_out(0, TILES - 1)
            if ct is not None:
                lru_exp(ct)
                lru_sqrt(ct)
        for ct in range(CT):
            lru_cat(ct)
        act.wait_ge(lst_ev, 1)
        act.dma_start(new_lru, lrow).then_inc(out_lru, 16)

        def ret_state(h):
            act.wait_ge(st_ps, h + 1)
            if h >= 1:
                act.wait_ge(out_ret, 32 * h)
            nc.scalar.copy(lst[:, 0:2 * DK], psum[6][:, P:3 * P]).then_inc(st_ev, 1)
            act.wait_ge(st_ev, h + 1)
            for d in range(2):
                act.dma_start(new_ret[d, h], lst[:, d * DK:(d + 1) * DK]).then_inc(out_ret, 16)
            if h + 2 < HEADS:
                ret_loads(h + 2)

        ret_state(0)
        for h in range(HEADS):
            m0 = N_MID + 2 * h
            root(S_O)
            if h + 1 < HEADS:
                ret_state(h + 1)
            split_hi(act, m0 + WS)
            act.wait_ge(rt_ps, h + 1)
            nc.scalar.copy(hT_hi[:, 4 + h, 0:LAT], psum[7][:, :]).then_inc(rt_hi, 1)
            nc.scalar.copy(hT_hi[:, 4 + h, LAT:], psum[6][:, 0:P]).then_inc(rt_hi, 1)
            split_hi(act, m0 + 1 + WS)
        act.wait_ge(ret_o, HEADS)
        act.wait_ge(rt_ps, HEADS)
        act.wait_ge(kt_ps, HEADS)
        act.dma_start(mg1[4:5, :], ada_b[16:24, :].rearrange("(o a) b -> o (a b)", o=1)).then_inc(gbias1, 16)
        act.dma_start(post, norm_mix_post.partition_broadcast(P)).then_inc(post_in, 16)
        act.wait_ge(col_ps, 8)
        act.wait_ge(out_ret, 32 * HEADS)
        act.wait_ge(out_lru, 16)
        act.dma_start(rows[4:5, :], ada_b[40:48, :].rearrange("(o a) b -> o (a b)", o=1)).then_inc(gbias2, 16)
        for n in range(N_GATES + WS, N_WOUT + WS):
            split_hi(act, n)
        act.wait_ge(pv_ps, HEADS)
        act.wait_ge(st_ps, HEADS)
        for t in range(TILES):
            act.dma_start(xn2[:, t, :], x_lat[t * P:(t + 1) * P, :] if t < 4 else x_ctx).then_inc(x_re, 16)

        def wo_square(n2, t):
            act.wait_ge(wo_ev, 5 * n2 + t + 1)
            if n2 or t:
                act.wait_ge(wo_sq, 5 * n2 + t)
            if n2 and t >= 2:
                act.wait_ge(x1_sq, t - 1)
            nc.scalar.activation(junk[:, 0:512], x1[:, t, n2 * 512:(n2 + 1) * 512], ACT.Square,
                                 accum_out=sm[:, S_WO + 2 * t + n2:S_WO + 2 * t + n2 + 1]).then_inc(wo_sq, 1)
            if t == 1 or t == 3 and n2 == 0:
                split_hi(act, N_WOUT + WS + 2 * n2 + t // 2)

        for t in range(TILES):
            wo_square(0, t)
        for i in range(TILES + 3):
            if i < TILES:
                wo_square(1, i)
            if 1 <= i <= TILES:
                root(S_T + i - 1, 1)
            if 2 <= i <= TILES + 1:
                t = i - 2
                root(S_O + t, 1)
                act.wait_ge(root_out, roots[0])
                nc.scalar.mul(xn2[:, t, :], x1[:, t, :], sm[:, S_O + t:S_O + t + 1]).then_inc(xn2_rd, 1)
            if i >= 3:
                t = i - 3
                act.wait_ge(h2_ps, 2 * t + 1)
                if t >= 2:
                    act.wait_ge(lg_ps, t - 1)
                nc.scalar.copy(h2T[:, t % 2, 0:4, :], psum[(5, 0)[t % 2]][:, :].rearrange("p (k t) -> p k t", k=4)).then_inc(h2_act, 1)
            if 1 <= i <= TILES:
                t = i - 1
                act.wait_ge(x1_rd, t + 1)
                act.wait_ge(wo_sq, TILES + min(i + 1, TILES))
                if t:
                    act.wait_ge(x1_sq, t)
                nc.scalar.activation(junk, x1[:, t, :], ACT.Square, accum_out=sm[:, S_X1 + t:S_X1 + t + 1]).then_inc(x1_sq, 1)
        split_hi(act, N_EXP + 2)
        act.wait_ge(lg_sub, 1)
        nc.scalar.activation(sm[:, 0:80], sm[:, 0:80], ACT.Exp).then_inc(lg_exp, 1)

        def gathered_half(e, pr2, hf):
            act.wait_ge(xs_f, 2 * e + (hf + 1))
            nc.scalar.copy(xs[pr2][0][:, 4 * hf:4 * hf + 4, :], xs_tmp[:, hf, :].rearrange("p (k s) -> p k s", k=4)).then_inc(xs_h, 1)

        gathered_half(0, 0, 0)
        gathered_half(0, 0, 1)

        def silu(n, e, b):
            used(act, n, e)
            nc.scalar.activation(sgl[0:SLOTS, b % 2, :], psum[b % 2][0:SLOTS, :], ACT.Silu).then_inc(sl_ev, 1)

        def hidT_hi(e, b):
            act.wait_ge(ht_ps, 4 * e + (b + 1))
            nc.scalar.copy(hidT[b % 2][0], psum[6][:, 0:4 * SLOTS]).then_inc(ht_hi, 1)

        for i, (kind, b, half) in enumerate(FIRST_CHUNKS):
            split_hi(act, N_EXP + i + WS)
            if half and kind == "g":
                silu(N_EXP + i, 0, b)
        hidT_hi(0, 0)

        def body(e, pr2, last):
            for i, (kind, b, half, nxt) in enumerate(body_chunks(last)):
                if not last and (kind, b, half) == ("g", 3, 0):
                    gathered_half(e + 1, 1 - pr2, 0)
                if not last and (kind, b, half) == ("d", 2, 0):
                    gathered_half(e + 1, 1 - pr2, 1)
                if not last or i + WS < len(body_chunks(last)):
                    split_hi(act, N_BODY + i + WS, e)
                if half and kind == "g":
                    silu(N_BODY + i, e, b)
                    if b:
                        hidT_hi(e + nxt, b - 1)
                if kind == "u" and b == 1 and half:
                    act.wait_ge(oht_ps, e + 1)
                    nc.scalar.copy(onehotT[:, 0:LAT], psum[6][0:SLOTS, :]).then_inc(oht_ev, 1)
                    nc.scalar.copy(onehotT[:, LAT:], psum[7][0:SLOTS, 0:P]).then_inc(oht_ev, 1)
                    nc.scalar.copy(gate[0:SLOTS, :], psum[7][0:SLOTS, P:P + 1]).then_inc(oht_ev, 1)
                    if last:
                        act.wait_ge(xs_l, 2 * NEXP)
                        act.dma_start(post, norm_ffn_post.partition_broadcast(P)).then_inc(post_in, 16)
                if kind == "d" and b == 2 and half:
                    hidT_hi(e, 3)
                if kind == "d" and b == 3 and half:
                    used(act, N_BODY + i, e)
                    for hf in range(2):
                        nc.scalar.activation(ye[0][:, hf * 512:(hf + 1) * 512], psum[4 + hf][0:SLOTS, :], ACT.Copy,
                                             scale=gate[0:SLOTS, 0:1]).then_inc(ye_h, 1)

        with act.Fori(0, LAST - 1, 2) as e:
            body(e, 0, False)
            body(e + 1, 1, False)
        body(LAST - 1, 0, False)
        body(LAST, 1, True)
        for t in range(TILES):
            act.wait_ge(fs_add, 10 * LAST + 2 * t + 3)
            if t:
                act.wait_ge(fin_sq, t)
            else:
                act.wait_ge(x1_sq, TILES)
            nc.scalar.activation(xn2[:, 0, :], facc[:, t, :], ACT.Square, accum_out=sm[:, S_FIN + t:S_FIN + t + 1]).then_inc(fin_sq, 1)
        root(S_O)
        for t in range(TILES):
            act.wait_ge(fin_y, t + 1)
            act.dma_start(y_lat[t * P:(t + 1) * P, :] if t < 4 else y_ctx, facc[:, t, :]).then_inc(out_y, 16)


    @block.tensor
    def _(pe):
        mm, tr = nc.tensor.matmul, nc.tensor.transpose

        pe.wait_ge(const_in, 16)
        pe.wait_ge(par_in, 16)
        tr(psum[7][:, 0:R_N], par_rows[0:R_N, :], ident[0:R_N, 0:R_N]).then_inc(par_ps, 1)

        def ada_block(i, bank):
            for half in range(2):
                n = ada_chunk(i) + half
                chunk_ready(pe, n)
                wh, wl = chunk_view(w_hi, n, 512), chunk_view(w_lo, n, 512)
                for k in range(4):
                    kk = 4 * half + k
                    mm(psum[bank][0:66, :], cond[:, kk, :], wl[:, k, :], start=(kk == 0), stop=False)
                    last = mm(psum[bank][0:66, :], cond[:, kk, :], wh[:, k, :], start=False, stop=(kk == 7))
                last.then_inc(w_used, 1)

        def columns(i, bank, at):
            pe.wait_ge(ada_row, i + 1)
            for q in range(4):
                last = mm(psum[bank][:, at + 2 * q:at + 2 * q + 2], rows[0:4, q * P:(q + 1) * P], selc[0:4, :],
                          start=True, stop=True)
            last.then_inc(col_ps, 1)

        pe.wait_ge(cond_rd, 1)
        for i in range(4):
            if i >= 2:
                pe.wait_ge(ada_row, i - 1)
            ada_block(i, 5 + i % 2)
            if i:
                if i >= 3:
                    pe.wait_ge(col_rd, i - 2)
                columns(i - 1, (7, 4)[(i - 1) % 2], 128)
        pe.wait_ge(col_rd, 2)
        columns(3, 4, 128)

        pe.wait_ge(xn_rd, TILES)
        for kt in range(KT):
            if kt >= 2:
                pe.wait_ge(h_tmp, kt - 1)
            for t in range(4):
                tr(psum[kt % 2][:, t * P:(t + 1) * P], x_in[:, t, kt * P:(kt + 1) * P], ident)
            tr(psum[2 + kt % 2][:, 0:P], x_in[:, 4, kt * P:(kt + 1) * P], ident).then_inc(xT_ps, 1)

        def lru_gates(s):
            ct, d, ctxp = s // 4, s // 2 % 2, s % 2
            if s:
                pe.wait_ge(gt_ev, 2 * s)
            else:
                pe.wait_ge(col_rd, 4)
                pe.wait_ge(gw_in, 16 * 16)
            pe.wait_ge(xl_ev, CT + 1 if ctxp else ct + 1)
            for kind in range(2):
                dst = psum[6][:, kind * P:(kind + 1) * P] if ctxp else psum[6 + kind][:, :]
                src = xc[:, ct, LAT:] if ctxp else xc[:, ct, 0:LAT]
                last = mm(dst, gw[ct // 2][:, ct % 2, kind, d, :], src, start=True, stop=True)
            last.then_inc(gt_ps, 1)

        def bank_free(bi, u):
            if bi == 0:
                pe.wait_ge(h_tmp, KT)
            elif bi == 1:
                pe.wait_ge(yl_ev, u + 1)
            elif bi == 2:
                pe.wait_ge(xl_ev, u + 1)
                if u == 0:
                    pe.wait_ge(yl_ev, 2 * CT)
            elif bi == 3:
                pe.wait_ge(rope_t, u + 1)
                if u == 0:
                    pe.wait_ge(xl_ev, CT + 1)
            elif bi == 4:
                pe.wait_ge(rope_t, HEADS + u + 1) if u < 4 else pe.wait_ge(qk_ctx, 1)
            else:
                pe.wait_ge(v_ev, u + 1) if u < 4 else pe.wait_ge(qk_ctx, 2)

        for n in range(N_WIN, N_MID):
            bi, half = (n - N_WIN) // 2, n % 2
            chunk_ready(pe, n)
            pe.wait_ge(h_lo, 4 * (half + 1) if bi == 0 else KT)
            wh, wl = chunk_view(w_hi, n, 512), chunk_view(w_lo, n, 512)
            units = CT if bi < 4 else TILES
            for u in range(units):
                if half == 0:
                    bank_free(bi, u)
                for k in range(4):
                    kk = 4 * half + k
                    first, final = kk == 0, kk == 7
                    if bi < 4:
                        a, b = wh[:, k, u * P:(u + 1) * P], wl[:, k, u * P:(u + 1) * P]
                        three(psum[u][:, :], a, b, hT_hi[:, kk, 0:LAT], hT_lo[:, kk, 0:LAT], first, final)
                        last = three(psum[4 + bi % 2][:, u * P:(u + 1) * P], a, b, hT_hi[:, kk, LAT:], hT_lo[:, kk, LAT:],
                                     first and u == 0, final and u == 3, skip_group_check=True)
                    else:
                        at = slice(u * P, (u + 1) * P)
                        last = three(psum[u if u < 4 else bi][:, :], hT_hi[:, kk, at], hT_lo[:, kk, at],
                                     wh[:, k, :], wl[:, k, :], first, final)
                if u == units - 1:
                    last.then_inc(w_used, 1)
                elif half:
                    last.then_inc(win_ps, 1)
                if n - N_WIN - 4 in GATES_AT and u < 4:
                    lru_gates(4 * GATES_AT[n - N_WIN - 4] + u)

        def ret_scores(h):
            for j in range(4):
                if j >= 2:
                    pe.wait_ge(sc_ev, 4 * h + j - 1)
                mm(psum[j % 2][:, :], kT[:, h, j * P:(j + 1) * P], qT[:, h, 0:LAT], start=True, stop=True).then_inc(sc_ps, 1)
                if j == 1:
                    pe.wait_ge(ret_rd, h) if h else pe.wait_ge(g_ev, TILES)
                    pe.wait_ge(dec_in[h % 2], 32 * (h // 2 + 1))
                    for t in range(4):
                        mm(psum[3 + t // 2][:, (t % 2) * 2 * DK:(t % 2 + 1) * 2 * DK], qT[:, h, t * P:(t + 1) * P],
                           s0[:, h % 2, :], start=True, stop=True)
            mm(psum[5][:, 0:P], kT[:, h, LAT:], qT[:, h, LAT:], start=True, stop=True).then_inc(scc_ps, 1)
            if h:
                pe.wait_ge(st_ev, h)
            if h >= 2:
                pe.wait_ge(rt_lo, 2 * (h - 1))
            tr(psum[6][:, 3 * P:], kT[:, h, LAT:], ident).then_inc(kt_ps, 1)

        def ret_values(h):
            hc = slice(h * DK, (h + 1) * DK)
            pe.wait_ge(scc_ev, h + 1)
            mm(psum[5][:, P:2 * P], sc_c, v_t[:, 4, hc], start=True, stop=True)
            pe.wait_ge(sc_ev, 4 * h + 4)
            for t in range(4):
                for j in range(4):
                    last = mm(psum[2][:, t * DK:(t + 1) * DK], sc[:, j, t * P:(t + 1) * P], v_t[:, j, hc],
                              start=(j == 0), stop=(j == 3))
            last.then_inc(pv_ps, 1)
            pe.wait_ge(kz_ev, h + 1)
            for d in range(2):
                last = mm(psum[6][:, (1 + d) * P:(2 + d) * P], kz[:, d, :], v_t[:, 4, hc], start=True, stop=True)
            last.then_inc(st_ps, 1)

        pe.wait_ge(qk_rd, 2 * HEADS)
        pe.wait_ge(qk_ctx, 2)
        pe.wait_ge(v_ev, TILES)
        pe.wait_ge(g_ev, 2)
        ret_scores(0)
        pe.wait_ge(lr_done, CT)
        pe.wait_ge(gt_ev, 32)
        tr(psum[7][0:8, 0:P], sm[:, S_ST:S_ST + 8], ident).then_inc(lst_ps, 1)
        ret_values(0)
        for h in range(HEADS):
            if h + 1 < HEADS:
                ret_scores(h + 1)
            pe.wait_ge(rt_lo, 2 * h) if h else pe.wait_ge(lst_ev, 1)
            ada_block(4 + h, 7)
            if h + 1 < HEADS:
                ret_values(h + 1)
            columns(4 + h, 7, 0)
            pe.wait_ge(col_rd, 5 + h)
            pe.wait_ge(ret_o, h + 1)
            pe.wait_ge(st_ev, min(h + 2, HEADS))
            for t in range(4):
                tr(psum[7][:, t * P:(t + 1) * P], ro_t[:, t, :], ident)
            tr(psum[6][:, 0:P], ro_t[:, 4, :], ident).then_inc(rt_ps, 1)

        pe.wait_ge(col_rd, 8)
        def gate_rows(src, gate_banks):
            for g in range(2):
                for half in range(2):
                    mm(psum[gate_banks[2 * g + half]][:, :], selb[0:5, g, :], src[0:5, half * 512:(half + 1) * 512],
                       start=True, stop=True).then_inc(gr_ps, 1)

        for i in range(8, 12):
            pe.wait_ge(ada_row, i if i < 10 else i - 1)
            ada_block(i, i % 2)
        pe.wait_ge(rt_lo, 2 * HEADS)
        pe.wait_ge(st_ev, HEADS)
        pe.wait_ge(ada_row, 12)
        pe.wait_ge(gbias1, 16)
        gate_rows(mg1, (2, 3, 5, 6))

        pe.wait_ge(cat_lo, CT)
        for n in range(N_WOUT, N_EXP):
            n2, half = (n - N_WOUT) // 2, n % 2
            chunk_ready(pe, n)
            wh, wl = chunk_view(w_hi, n, 512), chunk_view(w_lo, n, 512)
            for t in range(TILES):
                if half == 0 and n2 == 0 and t == 2:
                    pe.wait_ge(gr_ev, 4)
                if half == 0 and n2:
                    pe.wait_ge(wo_ev, t + 1)
                at = slice(t * P, (t + 1) * P)
                for k in range(4):
                    kk = 4 * half + k
                    last = three(psum[t][:, :], hT_hi[:, kk, at], hT_lo[:, kk, at], wh[:, k, :], wl[:, k, :], kk == 0, kk == 7)
                if t == TILES - 1:
                    last.then_inc(w_used, 1)
                elif half:
                    last.then_inc(wo_ps, 1)

        pe.wait_ge(rw_in, 16)
        pe.wait_ge(rwm_rd, 1)

        def logits(t):
            pe.wait_ge(h2_act, t + 1)
            pe.wait_ge(h2_dve, t + 1)
            g, dst = t // 4, psum[7][:, 64 + t * NEXP:64 + (t + 1) * NEXP]
            for k in range(KT):
                last = mm(dst, h2T[:, t % 2, k, :], rw_mod[:, g, k, :], start=(k == 0), stop=(k == 7))
            last.then_inc(lg_ps, 1)

        for g in range(2):
            for k in range(KT):
                mm(psum[7][:, g * NEXP:(g + 1) * NEXP], modc[:, g, 16 + k:17 + k].to_broadcast([P, P]), rw[:, k, :],
                   start=(k == 0), stop=(k == 7))

        for t in range(TILES):
            pe.wait_ge(xn2_rd, t + 1)
            if t == 1:
                pe.wait_ge(wo_ev, TILES + 2)
            if t >= 2:
                pe.wait_ge(h2_act, t - 1)
                pe.wait_ge(h2_dve, t - 1)
            for k in range(KT):
                last = tr(psum[(5, 0)[t % 2] + k // 4][:, (k % 4) * P:(k % 4 + 1) * P], xn2[:, t, k * P:(k + 1) * P], ident)
                if k % 4 == 3:
                    last.then_inc(h2_ps, 1)
            if t:
                logits(t - 1)
        logits(TILES - 1)
        pe.wait_ge(pr_rd, 1)
        for t in range(TILES):
            dst = psum[5][0:NEXP, t * P:(t + 1) * P] if t < 4 else psum[6][0:NEXP, 0:P]
            last = tr(dst, sp[:, t, 0, :], ident)
        last.then_inc(pt_ps, 1)
        pe.wait_ge(sl_rd, 1)
        for t in range(TILES):
            last = tr(psum[7][:, t * NEXP:(t + 1) * NEXP], pS[0:NEXP, t * P:(t + 1) * P], ident[0:NEXP, 0:NEXP])
        last.then_inc(sl_ps, 1)

        def gather(hf):
            for k in range(4):
                for t in range(TILES):
                    last = mm(psum[7][:, k * SLOTS:(k + 1) * SLOTS], xn2[:, t, (4 * hf + k) * P:(4 * hf + k + 1) * P],
                              oneh[:, t, :], start=(t == 0), stop=(t == 4))
            last.then_inc(ga_ps, 1)

        def up_or_gate(n, e, bank, half, x):
            dst = psum[bank][0:SLOTS, :]
            wh, wl = chunk_view(w_hi, n, 512), chunk_view(w_lo, n, 512)
            pe.wait_ge(hi_done, e * PER_E + (n + 1))
            for k in range(4):
                kk = 4 * half + k
                mm(dst, x[1][:, kk, :], wh[:, k, :], start=(kk == 0), stop=False)
                mm(dst, x[0][:, kk, :], wh[:, k, :], start=False, stop=False)
            chunk_ready(pe, n, e)
            for k in range(4):
                kk = 4 * half + k
                last = mm(dst, x[0][:, kk, :], wl[:, k, :], start=False, stop=(kk == 7))
            last.then_inc(w_used, 1)

        def down(n, e, b, half):
            wh, wl = chunk_view(w_hi, n, D), chunk_view(w_lo, n, D)
            steps = [(j, [a[:, (2 * half + j) * SLOTS:(2 * half + j + 1) * SLOTS] for a in hidT[b % 2]], q)
                     for j in range(2) for q in range(2)]
            pe.wait_ge(hi_done, e * PER_E + (n + 1))
            for j, x, q in steps:
                at = slice(q * 512, (q + 1) * 512)
                mm(psum[4 + q][0:SLOTS, :], x[1], wh[:, j, at], start=(b == 0 and half == 0 and j == 0), stop=False)
                mm(psum[4 + q][0:SLOTS, :], x[0], wh[:, j, at], start=False, stop=False)
            chunk_ready(pe, n, e)
            for j, x, q in steps:
                last = mm(psum[4 + q][0:SLOTS, :], x[0], wl[:, j, q * 512:(q + 1) * 512], start=False,
                          stop=(b == 3 and half == 1 and j == 1))
            last.then_inc(w_used, 1)

        def hid_T(e, b):
            pe.wait_ge(hid_rd, 4 * e + (b + 1))
            hb = hid[0:SLOTS, b % 2, :].rearrange("s (p j) -> s j p", j=4)
            for j in range(4):
                last = tr(psum[6][:, j * SLOTS:(j + 1) * SLOTS], hb[:, j, :], ident[0:SLOTS, 0:SLOTS])
            last.then_inc(ht_ps, 1)

        pe.wait_ge(oh_rd, 1)
        gather(0)
        pe.wait_ge(xs_f, 1)
        gather(1)
        pe.wait_ge(xs_l, 2)
        for i, (kind, b, half) in enumerate(FIRST_CHUNKS):
            up_or_gate(N_EXP + i, 0, b + (2 if kind == "u" else 0), half, xs[0])
        hid_T(0, 0)

        def scatter(e, i):
            if i == 0:
                pe.wait_ge(ye_l, 2 * e + 2)
            if i >= 4:
                pe.wait_ge(fs_add, 10 * e + 2 + (i - 4 if i < 9 else 6))
            at = slice((i % 2) * 512, (i % 2 + 1) * 512)
            t = i // 2
            mm(psum[SCATTER_BANKS[i]][:, :], onehotT[:, t * P:(t + 1) * P], ye[1][:, at], start=True, stop=False)
            mm(psum[SCATTER_BANKS[i]][:, :], onehotT[:, t * P:(t + 1) * P], ye[0][:, at], start=False, stop=True).then_inc(fs_ps, 1)

        def body(e, pr2, last):
            for i, (kind, b, half, nxt) in enumerate(body_chunks(last)):
                n, own = N_BODY + i, e + nxt
                if kind in "gu":
                    if half == 0:
                        if kind == "g":
                            if b == 0:
                                pe.wait_ge(xs_l, 2 * own + 2)
                            pe.wait_ge(sl_ev, 4 * own + (b - 1))
                        elif b != 1:
                            pe.wait_ge(hid_rd, 4 * own + (b - 1))
                    up_or_gate(n, e, b % 2 + (2 if kind == "u" else 0), half, xs[1 - pr2 if nxt else pr2])
                else:
                    if half == 0:
                        pe.wait_ge(ht_lo, 4 * e + (b + 1))
                    down(n, e, b, half)
                if half and kind == "g" and b:
                    if b == 1:
                        pe.wait_ge(fs_add, 10 * e + 7)
                    else:
                        pe.wait_ge(ht_lo, 4 * e + (b - 1))
                        if b == 2:
                            pe.wait_ge(oht_ev, 3 * e + 3)
                    hid_T(own, b - 1)
                if half and kind == "u" and b == 1:
                    pe.wait_ge(ht_lo, 4 * e + 1)
                    pe.wait_ge(fs_add, 10 * e + 1)
                    for t in range(TILES):
                        dst = psum[6][0:SLOTS, t * P:(t + 1) * P] if t < 4 else psum[7][0:SLOTS, 0:P]
                        tr(dst, oneh[:, t, :], ident)
                    for t in range(TILES):
                        last_mm = mm(psum[7][0:SLOTS, P:P + 1], oneh[:, t, :], ecol[:, t, 0:1], start=(t == 0), stop=(t == 4))
                    last_mm.then_inc(oht_ps, 1)
                if not last and half and kind == "d" and b == 1:
                    pe.wait_ge(oht_ev, 3 * e + 3)
                    pe.wait_ge(oh_rd, e + 2)
                    gather(0)
                if not last and half and kind == "u" and b == 3:
                    pe.wait_ge(xs_f, 2 * e + 3)
                    gather(1)
                if half and kind == "d" and b == 2:
                    pe.wait_ge(ht_lo, 4 * e + 3)
                    hid_T(e, 3)
                    if last:
                        pe.wait_ge(gbias2, 16)
                        pe.wait_ge(sl_ev, 4 * NEXP)
                        gate_rows(rows, (0, 1, 2, 3))
                if nxt and (kind, b, half) in SCATTER_AT:
                    if b == 0:
                        pe.wait_ge(xs_f, 2 * e + 4)
                    for j in SCATTER_AT[kind, b, half]:
                        scatter(e, j)
            if last:
                for j in range(2 * TILES):
                    scatter(e, j)

        with pe.Fori(0, LAST - 1, 2) as e:
            body(e, 0, False)
            body(e + 1, 1, False)
        body(LAST - 1, 0, False)
        body(LAST, 1, True)

    @block.vector
    def _(dve):
        tt, ts, stt, cp = nc.vector.tensor_tensor, nc.vector.tensor_scalar, nc.vector.scalar_tensor_tensor, nc.vector.tensor_copy
        steps = [0]

        def step(ins):
            steps[0] += 1
            ins.then_inc(dve_step, 1)
            dve.wait_ge(dve_step, steps[0])

        def bc(a, *shape):
            return a.unsqueeze(len(a.shape)).to_broadcast(list(a.shape) + list(shape))

        dve.wait_ge(par_ps, 1)
        cp(par[:, :], psum[7][:, 0:R_N]).then_inc(par_rd, 1)
        dve.wait_ge(par_rd, 1)
        lam = par[:, R_LAM:R_LAM + 8]
        stt(sm[:, S_ABS:S_ABS + 8], lam, -1.0, lam, ALU.mult, ALU.max).then_inc(lam_abs, 1)
        split_lo(dve, "dve", 0)
        dve.wait_ge(sil_rd, 1)
        dve.wait_ge(cond_0, 1)
        sil2 = sil[:, :].rearrange("p (g k) -> p k g", g=2)
        parts = cond[:, :, 0:4].rearrange("p k (g a) -> p k g a", a=2)
        step(cp(parts[:, :, :, 0], sil2))
        tt(parts[:, :, :, 1], sil2, parts[:, :, :, 0], ALU.subtract).then_inc(cond_rd, 1)
        split_lo(dve, "dve", 1)
        split_lo(dve, "dve", 2)
        def rstd(dst, src, n):
            rstd_start(dst, src, n)
            roots[1] += 1
            dve.wait_ge(root_out, roots[1])

        roots = [0, 0]

        def rstd_start(dst, src, n):
            step(ts(dst, src, 1.0 / n, EPS, ALU.mult, ALU.add))
            nc.vector.reciprocal(dst, dst).then_inc(root_in, 1)
            roots[0] += 1

        def row_copy(i, bank, dst):
            used(dve, ada_chunk(i) + 1)
            if 1 <= i < 9:
                dve.wait_ge(col_ps, i)
            cp(dst[0:4, :], psum[bank][0:4, :]).then_inc(ada_row, 1)

        def col_out(i, bank, at):
            dve.wait_ge(col_ps, i + 1)
            tt(modc[:, :, 4 * i:4 * i + 4], psum[bank][:, at:at + 8].rearrange("p (q g) -> p g q", g=2),
               par[:, R_ADAB + 4 * i:R_ADAB + 4 * i + 4].unsqueeze(1).to_broadcast([P, 2, 4]), ALU.add).then_inc(col_rd, 1)

        for m in range(N_WIN):
            split_lo(dve, "dve", m + WS)
            if m % 2:
                row_copy(m // 2, 5 + m // 2 % 2, rows[:, 0:512])
            elif m >= 4:
                col_out(m // 2 - 2, (7, 4)[m // 2 % 2], 128)
            if m == 3:
                dve.wait_ge(x_sq, TILES)
                rstd(sm[:, S_RSTD:S_RSTD + TILES], sm[:, S_SS:S_SS + TILES], D)
            for t in {3: (0,), 4: (1,), 5: (2,), 6: (3,), 7: (4,)}.get(m, ()):
                ts(x_in[:, t, :], x_in[:, t, :], sm[:, S_RSTD + t:S_RSTD + t + 1], None, ALU.mult).then_inc(xn_rd, 1)
        col_out(2, 7, 128)
        col_out(3, 4, 128)
        dve.wait_ge(col_rd, 4)
        for g in range(2):
            step(stt(aff[:, 0, g, :], modc[:, g, 8:16], 1.0, par[:, R_PRE:R_PRE + 8], ALU.add, ALU.mult))

        for kt in range(KT):
            dve.wait_ge(xT_ps, kt + 1)
            if kt >= 2:
                dve.wait_ge(h_lo, kt - 1)
            ts(hT_tmp[:, kt % 2, 0:LAT], psum[kt % 2][:, :], aff[:, 0, 0, kt:kt + 1], modc[:, 0, kt:kt + 1], ALU.mult, ALU.add)
            ts(hT_tmp[:, kt % 2, LAT:], psum[2 + kt % 2][:, 0:P], aff[:, 0, 1, kt:kt + 1],
               modc[:, 1, kt:kt + 1], ALU.mult, ALU.add).then_inc(h_tmp, 1)

        dve.wait_ge(lam_exp, 1)
        u, s, s2, q = (sm[:, a:a + 8] for a in (S_EXP, 16, S_T, S_T + 8))
        step(ts(s, u, 2.0, None, ALU.add))
        step(nc.vector.reciprocal(s, s))
        step(tt(s, s, u, ALU.mult))
        step(tt(s2, s, s, ALU.mult))
        step(ts(q, s2, 1.0 / 17, None, ALU.mult))
        for k in (15, 13, 11, 9, 7, 5, 3):
            step(stt(q, q, 1.0 / k, s2, ALU.add, ALU.mult))
        step(stt(q, q, 1.0, s, ALU.add, ALU.mult))
        step(ts(s2, lam, -1.0, 0.0, ALU.mult, ALU.max))
        step(stt(s, q, 2.0, s2, ALU.mult, ALU.add))
        ts(sm[:, S_C8:S_C8 + 8], s, -8.0, None, ALU.mult)
        ts(sm[:, S_NC8:S_NC8 + 8], s, 8.0, None, ALU.mult).then_inc(c8_rd, 1)

        def conv(parts):
            w = [[par[:, R_CW + 4 * tap + ct:R_CW + 4 * tap + ct + 1] for tap in range(4)] for ct in range(CT)]
            for ct, src, dst in parts:
                last = ts(dst, src, w[ct][2], par[:, R_CB + ct:R_CB + ct + 1], ALU.mult, ALU.add)
            step(last)
            for tap, lo, hi in ((0, 2, 0), (1, 1, 0), (3, 0, 1)):
                for ct, src, dst in parts:
                    n = dst.shape[1]
                    a, b = slice(lo, n - hi), slice(hi, n - lo)
                    last = stt(dst[:, a], src[:, b], w[ct][tap], dst[:, a], ALU.mult, ALU.add)
                if tap < 3:
                    step(last)
            last.then_inc(xl_ev, 1)

        def conv_lat(ct):
            win_ready(dve, 1, ct)
            conv([(ct, psum[ct][:, :], xc[:, ct, 0:LAT])])

        def conv_ctx():
            conv([(ct, psum[5][:, ct * P:(ct + 1) * P], xc[:, ct, LAT:]) for ct in range(CT)])

        def rope_terms(i, dst, h):
            n = 4 * i + h
            win_ready(dve, 2 + i, h)
            if n == 0:
                dve.wait_ge(rope_in, 32)
            if n >= 2:
                dve.wait_ge(qk_rd, n - 1)
            tt(dst[:, h, 0:LAT], psum[h][:, :], rope_c, ALU.mult)
            tt(rope_tmp[0:64, n % 2, :], psum[h][64:128, :], rope_s[64:128, :], ALU.mult)
            tt(rope_tmp[64:128, n % 2, :], psum[h][0:64, :], rope_s[0:64, :], ALU.mult).then_inc(rope_t, 1)

        def lru_weight(ct):
            dve.wait_ge(lr_exp, 4 * (ct + 1))
            step(tt(lr_r, lr_a, lr_a, ALU.mult))
            stt(lr_t, lr_r, 1.0, lr_t, ALU.add, ALU.mult).then_inc(lr_w, 1)

        def lru_scan(ct):
            dve.wait_ge(lr_sq, ct + 1)
            dve.wait_ge(lr_gx, ct + 1)
            step(tt(lr_t, lr_t, lr_g, ALU.mult))
            for d, h0 in ((0, par[:, R_H0 + ct:R_H0 + ct + 1]), (1, par[:, R_H0 + 4 + ct:R_H0 + 5 + ct])):
                for lo, n, init in ((0, LAT, h0), (LAT, CTX, 0.0)):
                    o, a, b = (x[:, d, lo:lo + n] for x in (lr_r, lr_a, lr_t))
                    if d:
                        o, a, b = o[:, ::-1], a[:, ::-1], b[:, ::-1]
                    last = nc.vector.tensor_tensor_scan(o, a, b, init, ALU.mult, ALU.add)
            step(last)

        def lru_out(ct):
            cp(sm[:, S_ST + ct:S_ST + ct + 1], lr_r[:, 0, TOK - 1:TOK])
            step(cp(sm[:, S_ST + 4 + ct:S_ST + 5 + ct], lr_r[:, 1, LAT:LAT + 1]))
            step(tt(lr_r[:, 0, :], lr_r[:, 0, :], lr_r[:, 1, :], ALU.add))
            dve.wait_ge(yl_ev, 2 * CT)
            tt(gel[:, ct, :], gel[:, ct, :], lr_r[:, 0, :], ALU.mult).then_inc(lr_done, 1)

        for m in range(N_WIN, N_MID):
            bi, half = (m - N_WIN) // 2, m % 2
            parts = (lru_weight, lru_scan, lru_out) if half and bi >= 2 else ()
            for u in range(CT - 1):
                if half and bi == 1:
                    conv_lat(u)
                if half and bi in (2, 3):
                    rope_terms(bi - 2, (qT, kT)[bi - 2], u)
                if parts:
                    parts[u](bi - 2)
            split_lo(dve, "dve", m + WS)
            if half and bi == 1:
                conv_lat(CT - 1)
                conv_ctx()
            if half and bi in (2, 3):
                rope_terms(bi - 2, (qT, kT)[bi - 2], CT - 1)

        def ret_mask(h):
            dve.wait_ge(dec_in[h % 2], 32 * (h // 2 + 1))
            for j in range(4):
                dve.wait_ge(sc_ps, 4 * h + j + 1)
                tt(sc[:, j, :], psum[j % 2][:, :], dec[:, h % 2, 384 - P * j:896 - P * j], ALU.mult).then_inc(sc_ev, 1)
            dve.wait_ge(scc_ps, h + 1)
            tt(sc_c, psum[5][:, 0:P], dec[:, h % 2, 384:512], ALU.mult).then_inc(scc_ev, 1)
            dve.wait_ge(kt_ps, h + 1)
            ts(kz[:, 0, :], psum[6][:, 3 * P:], zeta[:, h, 0:1], None, ALU.mult)
            ts(kz[:, 1, :], psum[6][:, 3 * P:], zeta[:, h, 1:2], None, ALU.mult).then_inc(kz_ev, 1)

        def ret_sum(h):
            dve.wait_ge(pv_ps, h + 1)
            cp(o_t[:, 4, :], psum[5][:, P:2 * P])
            for d in range(2):
                for t in range(4):
                    cross = psum[3 + t // 2][:, (t % 2) * 2 * DK + d * DK:(t % 2) * 2 * DK + (d + 1) * DK]
                    if d == 0:
                        last = ts(o_t[:, t, :], cross, xi[:, t, h, 0:1], None, ALU.mult)
                    else:
                        last = stt(o_t[:, t, :], cross, xi[:, t, h, 1:2], o_t[:, t, :], ALU.mult, ALU.add)
                step(last)
            tt(o_t[:, 0:4, :], o_t[:, 0:4, :], psum[2][:, :].rearrange("p (t e) -> p t e", t=4), ALU.add).then_inc(ret_rd, 1)

        def ret_norm(h):
            dve.wait_ge(ret_rd, h + 1)
            if h:
                dve.wait_ge(rt_ps, h)
            step(tt(ro_t, o_t, o_t, ALU.mult))
            step(nc.vector.tensor_reduce(sm[:, S_O:S_O + TILES], ro_t, AX.X, ALU.add))
            rstd(sm[:, S_O:S_O + TILES], sm[:, S_O:S_O + TILES], DK)
            step(tt(ro_t, o_t, bc(sm[:, S_O:S_O + TILES], DK), ALU.mult))
            if h == 0:
                dve.wait_ge(g_ev, TILES)
            tt(ro_t, ro_t, sg[:, :, h * DK:(h + 1) * DK], ALU.mult).then_inc(ret_o, 1)

        ret_mask(0)
        dve.wait_ge(lst_ps, 1)
        cp(lrow, psum[7][0:8, 0:P]).then_inc(lst_ev, 1)
        for ct in range(CT):
            dve.wait_ge(cat_hi, ct + 1)
            tt(hT_lo[:, ct, :], gel[:, ct, :], hT_hi[:, ct, :], ALU.subtract).then_inc(cat_lo, 1)
        ret_sum(0)
        for h in range(HEADS):
            m0 = N_MID + 2 * h
            if h + 1 < HEADS:
                ret_mask(h + 1)
            ret_norm(h)
            row_copy(4 + h, 7, rows[:, 0:512])
            if h + 1 < HEADS:
                ret_sum(h + 1)
            col_out(4 + h, 7, 0)
            split_lo(dve, "dve", m0 + WS)
            dve.wait_ge(rt_hi, 2 * h + 2)
            tt(hT_lo[:, 4 + h, 0:LAT], psum[7][:, :], hT_hi[:, 4 + h, 0:LAT], ALU.subtract).then_inc(rt_lo, 1)
            tt(hT_lo[:, 4 + h, LAT:], psum[6][:, 0:P], hT_hi[:, 4 + h, LAT:], ALU.subtract).then_inc(rt_lo, 1)
            split_lo(dve, "dve", m0 + 1 + WS)

        for i in range(8, 12):
            if i == 10:
                dve.wait_ge(out_ret, 32 * HEADS)
                dve.wait_ge(out_lru, 16)
            row_copy(i, i % 2, (mg1 if i < 10 else rows[:, :])[:, (i % 2) * 512:(i % 2 + 1) * 512])
            for n in (N_GATES + 2 * (i - 8) + WS, N_GATES + 2 * (i - 8) + 1 + WS):
                split_lo(dve, "dve", n)

        def gate_row(first, banks):
            dve.wait_ge(post_in, 16 * (first // 4 + 1))
            for g in range(2):
                for half in range(2):
                    at = slice(half * 512, (half + 1) * 512)
                    dve.wait_ge(gr_ps, first + 2 * g + half + 1)
                    tt(g_row[:, g, at], psum[banks[2 * g + half]][:, :], post[:, at], ALU.mult).then_inc(gr_ev, 1)

        gate_row(0, (2, 3, 5, 6))
        dve.wait_ge(col_rd, 8)
        for g in range(2):
            step(stt(aff[:, 1, g, :], modc[:, g, 24:32], 1.0, par[:, R_FPRE:R_FPRE + 8], ALU.add, ALU.mult))
        dve.wait_ge(rw_in, 16)
        for g in range(2):
            last = tt(rw_mod[:, g, :, :], rw[:, :, :], bc(aff[:, 1, g, :], NEXP), ALU.mult)
        last.then_inc(rwm_rd, 1)

        def wo_copy(n2, t):
            wout_ready(dve, n2, t)
            cp(x1[:, t, n2 * 512:(n2 + 1) * 512], psum[t][:, :]).then_inc(wo_ev, 1)
            if t == 1 or t == 3 and n2 == 0:
                split_lo(dve, "dve", N_WOUT + WS + 2 * n2 + t // 2)

        root_of_mix = {}
        for t in range(TILES):
            wo_copy(0, t)
        for i in range(TILES + 3):
            if i < TILES:
                wo_copy(1, i)
            if 1 <= i <= TILES:
                t = i - 1
                dve.wait_ge(wo_sq, TILES + t + 1)
                step(tt(sm[:, S_T + t:S_T + t + 1], sm[:, S_WO + 2 * t:S_WO + 2 * t + 1],
                        sm[:, S_WO + 2 * t + 1:S_WO + 2 * t + 2], ALU.add))
                rstd_start(sm[:, S_T + t:S_T + t + 1], sm[:, S_T + t:S_T + t + 1], D)
                root_of_mix[t] = roots[0]
            if 2 <= i <= TILES + 1:
                dve.wait_ge(x1_sq, i - 1)
                rstd_start(sm[:, S_O + i - 2:S_O + i - 1], sm[:, S_X1 + i - 2:S_X1 + i - 1], D)
            if 1 <= i <= TILES:
                dve.wait_ge(root_out, root_of_mix[t])
                if t == 0:
                    dve.wait_ge(gr_ev, 4)
                    dve.wait_ge(x_re, 16 * TILES)
                step(stt(x1[:, t, :], x1[:, t, :], sm[:, S_T + t:S_T + t + 1], g_row[:, t // 4, :], ALU.mult, ALU.mult))
                tt(x1[:, t, :], x1[:, t, :], xn2[:, t, :], ALU.add).then_inc(x1_rd, 1)
            if i >= 3:
                t = i - 3
                dve.wait_ge(h2_ps, 2 * t + 2)
                if t >= 2:
                    dve.wait_ge(lg_ps, t - 1)
                cp(h2T[:, t % 2, 4:8, :], psum[(5, 0)[t % 2] + 1][:, :].rearrange("p (k t) -> p k t", k=4)).then_inc(h2_dve, 1)
        roots[1] = roots[0]
        split_lo(dve, "dve", N_EXP + 2)
        lg_x = psum[7][:, 64:64 + TILES * NEXP].rearrange("p (t e) -> p t e", t=TILES)
        ex = sm[:, 0:TILES * NEXP].rearrange("p (t e) -> p t e", t=TILES)
        dve.wait_ge(lg_ps, TILES)
        cp(ex[:, 0:4, :], psum[7][:, 0:NEXP].unsqueeze(1).to_broadcast([P, 4, NEXP]))
        step(cp(ex[:, 4, :], psum[7][:, NEXP:2 * NEXP]))
        step(tt(ex, ex, lg_x, ALU.add))
        step(nc.vector.tensor_reduce(sm[:, S_MAX:S_MAX + TILES], ex, AX.X, ALU.max))
        tt(ex, ex, bc(sm[:, S_MAX:S_MAX + TILES], NEXP), ALU.subtract).then_inc(lg_sub, 1)
        dve.wait_ge(lg_exp, 1)
        step(nc.vector.tensor_reduce(sm[:, S_SUM:S_SUM + TILES], ex, AX.X, ALU.add))
        step(nc.vector.reciprocal(sm[:, S_REC:S_REC + TILES], sm[:, S_SUM:S_SUM + TILES]))
        tt(sp[:, :, 0, :], ex, bc(sm[:, S_REC:S_REC + TILES], NEXP), ALU.mult).then_inc(pr_rd, 1)
        dve.wait_ge(pt_ps, 1)
        ex16 = slice(0, NEXP)
        cp(pW[ex16, 0:LAT], psum[5][ex16, :])
        step(cp(pW[ex16, LAT:], psum[6][ex16, 0:P]))
        m8 = sm[ex16, S_T:S_T + 8]
        for at, cap in ((slice(0, LAT), CAP_L), (slice(LAT, TOK), CAP_C)):
            for _ in range(cap // 8):
                step(nc.vector.max(m8, pW[ex16, at]))
                step(nc.vector.match_replace(pW[ex16, at], m8, pW[ex16, at], -1.0))
        nc.vector.memset(pC[ex16, :], 1.0)
        step(ts(pS[ex16, :], pW[ex16, :], 0.0, None, ALU.is_lt))
        for at in (slice(0, LAT), slice(LAT, TOK)):
            last = nc.vector.tensor_tensor_scan(pT[ex16, at], pC[ex16, at], pS[ex16, at], 0.0, ALU.mult, ALU.add)
        step(last)
        tt(pS[ex16, :], pS[ex16, :], pT[ex16, :], ALU.mult).then_inc(sl_rd, 1)
        dve.wait_ge(sl_ps, 1)
        step(cp(sp[:, :, 1, :], psum[7][:, 0:TILES * NEXP].rearrange("p (t e) -> p t e", t=TILES)))

        def onehot(e1, e):
            cp(ecol[:, :, :], sp[:, :, :, bass.ds(e1, 1)].rearrange("p t a o -> p t (a o)")).then_inc(ec_rd, 1)
            dve.wait_ge(ec_rd, e + 1) if not isinstance(e, int) or e else dve.wait_ge(ec_rd, 1)
            for t in range(TILES):
                last = ts(oneh[:, t, :], iota[:, t // 4, :], ecol[:, t, 1:2], None, ALU.is_equal)
            last.then_inc(oh_rd, 1)

        def gathered(e, hf):
            dve.wait_ge(ga_ps, 2 * e + (hf + 1))
            ps = psum[7][:, 0:4 * SLOTS].rearrange("p (k s) -> p k s", k=4)
            dst = xs_tmp[:, hf, :].rearrange("p (k s) -> p k s", k=4)
            k4 = slice(4 * hf, 4 * hf + 4)
            for g, at, n in ((0, slice(0, CAP_L), CAP_L), (1, slice(CAP_L, SLOTS), CAP_C)):
                last = tt(dst[:, :, at], ps[:, :, at], bc(aff[:, 1, g, k4], n), ALU.mult)
            last.then_inc(xs_m, 1)
            dve.wait_ge(xs_m, 2 * e + (hf + 1))
            for g, at, n in ((0, slice(0, CAP_L), CAP_L), (1, slice(CAP_L, SLOTS), CAP_C)):
                last = tt(dst[:, :, at], dst[:, :, at], bc(modc[:, g, 16 + 4 * hf:20 + 4 * hf], n), ALU.add)
            last.then_inc(xs_f, 1)

        def gathered_lo(e, pr2, hf):
            dve.wait_ge(xs_h, 2 * e + (hf + 1))
            k4 = slice(4 * hf, 4 * hf + 4)
            tt(xs[pr2][1][:, k4, :], xs_tmp[:, hf, :].rearrange("p (k s) -> p k s", k=4), xs[pr2][0][:, k4, :],
               ALU.subtract).then_inc(xs_l, 1)

        def hidden(n, e, own, b):
            used(dve, n, e)
            dve.wait_ge(sl_ev, 4 * own + (b + 1))
            tt(hid[0:SLOTS, b % 2, :], psum[2 + b % 2][0:SLOTS, :], sgl[0:SLOTS, b % 2, :], ALU.mult).then_inc(hid_rd, 1)

        def hidT_lo(e, b):
            dve.wait_ge(ht_hi, 4 * e + (b + 1))
            tt(hidT[b % 2][1], psum[6][:, 0:4 * SLOTS], hidT[b % 2][0], ALU.subtract).then_inc(ht_lo, 1)

        onehot(0, 0)
        gathered(0, 0)
        gathered(0, 1)
        gathered_lo(0, 0, 0)
        gathered_lo(0, 0, 1)
        for i, (kind, b, half) in enumerate(FIRST_CHUNKS):
            split_lo(dve, "dve", N_EXP + i + WS)
            if half and kind == "u":
                hidden(N_EXP + i, 0, 0, 0)
        hidT_lo(0, 0)
        nc.vector.memset(facc[:, 4, :], 0.0).then_inc(fs_add, 1)
        dve.wait_ge(fz, 1)
        dve.wait_ge(fs_add, 1)

        def body(e, pr2, last):
            chunks = body_chunks(last)
            for i, (kind, b, half, nxt) in enumerate(chunks):
                if not last and (kind, b, half) == ("g", 3, 0):
                    gathered(e + 1, 0)
                    gathered_lo(e + 1, 1 - pr2, 0)
                if not last and (kind, b, half) == ("d", 2, 0):
                    gathered(e + 1, 1)
                    gathered_lo(e + 1, 1 - pr2, 1)
                if nxt and (kind, b, half) in SCATTER_AT:
                    if kind == "u":
                        hidden(N_BODY + i, e, e + 1, b)
                    for j in SCATTER_AT[kind, b, half]:
                        scattered(e, j)
                if not last or i + WS < len(chunks):
                    split_lo(dve, "dve", N_BODY + i + WS, e)
                if not half:
                    continue
                if kind == "g" and b:
                    hidT_lo(e + nxt, b - 1)
                if kind == "u" and not nxt:
                    hidden(N_BODY + i, e, e, b)
                if kind == "u" and b == 1 and not last:
                    dve.wait_ge(oht_ps, e + 1)
                    onehot(e + 1, e + 1)
                if kind == "d" and b == 2:
                    hidT_lo(e, 3)
                    if last:
                        gate_row(4, (0, 1, 2, 3))
                if kind == "d" and b == 3:
                    for hf in range(2):
                        dve.wait_ge(ye_h, 2 * e + (hf + 1))
                        at = slice(hf * 512, (hf + 1) * 512)
                        stt(ye[1][:, at], psum[4 + hf][0:SLOTS, :], gate[0:SLOTS, 0:1], ye[0][:, at], ALU.mult,
                            ALU.subtract).then_inc(ye_l, 1)
            if last:
                for j in range(2 * TILES):
                    scattered(e, j)

        def scattered(e, i):
            dst = facc[:, i // 2, (i % 2) * 512:(i % 2 + 1) * 512]
            dve.wait_ge(fs_ps, 10 * e + (i + 1))
            tt(dst, dst, psum[SCATTER_BANKS[i]][:, :], ALU.add).then_inc(fs_add, 1)

        with dve.Fori(0, LAST - 1, 2) as e:
            body(e, 0, False)
            body(e + 1, 1, False)
        body(LAST - 1, 0, False)
        body(LAST, 1, True)
        dve.wait_ge(fin_sq, TILES)
        rstd(sm[:, S_O:S_O + TILES], sm[:, S_FIN:S_FIN + TILES], D)
        dve.wait_ge(gr_ev, 8)
        for t in range(TILES):
            step(stt(facc[:, t, :], facc[:, t, :], sm[:, S_O + t:S_O + t + 1], g_row[:, t // 4, :], ALU.mult, ALU.mult))
            tt(facc[:, t, :], facc[:, t, :], x1[:, t, :], ALU.add).then_inc(fin_y, 1)

    @block.gpsimd
    def _(pool):
        nc.gpsimd.memset(cond[:, :, :].bitcast(F32), 0.0).then_inc(cond_0, 1)
        for n in range(WS):
            split_lo(pool, "pool", n)
        for m in range(N_WIN):
            split_lo(pool, "pool", m + WS)
        nc.gpsimd.memset(gw[0], 0.0).then_inc(gw_0, 1)
        pool.wait_ge(col_ps, 4)
        nc.gpsimd.memset(gw[1], 0.0).then_inc(gw_0, 1)
        for kt in range(KT):
            pool.wait_ge(h_hi, kt + 1)
            nc.gpsimd.tensor_tensor(hT_lo[:, kt, :], hT_tmp[:, kt % 2, :], hT_hi[:, kt, :], ALU.subtract).then_inc(h_lo, 1)
        for m in range(N_WIN, N_MID):
            bi, half = (m - N_WIN) // 2, m % 2
            split_lo(pool, "pool", m + WS)
            if half and bi in (2, 3):
                for h in range(HEADS):
                    pool.wait_ge(rope_t, 4 * (bi - 2) + h + 1)
                    dst = (qT, kT)[bi - 2][:, h, 0:LAT]
                    nc.gpsimd.tensor_tensor(dst, dst, rope_tmp[:, h % 2, :], ALU.add).then_inc(qk_rd, 1)
            if m - N_WIN - 4 in GATES_AT:
                ct = GATES_AT[m - N_WIN - 4]
                pool.wait_ge(gt_ev, 8 * (ct + 1))
                nc.gpsimd.tensor_tensor(lr_g, lr_g, xc[:, ct, :].unsqueeze(1).to_broadcast([P, 2, TOK]), ALU.mult).then_inc(lr_gx, 1)
        for n in range(N_MID + WS, N_EXP + WS):
            split_lo(pool, "pool", n)
        pool.wait_ge(sl_ps, 1)
        nc.gpsimd.memset(facc[:, 0:4, :], 0.0).then_inc(fz, 1)
        for n in range(N_EXP + WS, N_BODY + WS):
            split_lo(pool, "pool", n)

        def body(e, last):
            for i in range(len(body_chunks(last)) - (WS if last else 0)):
                split_lo(pool, "pool", N_BODY + i + WS, e)

        with pool.Fori(0, LAST) as e:
            body(e, False)
        body(LAST, True)

    ctx.close()


def tables():
    import numpy as np

    f = np.float64
    dec_f = np.log1p(-np.exp2(-(5.0 + np.arange(HEADS, dtype=f))))
    dec_b = np.log1p(-np.exp2(-(5.5 + np.arange(HEADS, dtype=f))))
    scale = DK ** -0.5
    diff = np.arange(896)[None, :] - 384 - np.arange(P)[:, None]
    decay = np.where(diff >= 0, np.exp(np.maximum(diff, 0) * dec_f[:, None, None]),
                     np.exp(np.maximum(-diff, 0) * dec_b[:, None, None])) * scale
    pos = np.arange(LAT, dtype=f).reshape(4, P)
    xi = np.stack([np.exp((pos[..., None] + 1) * dec_f), np.exp((LAT - pos[..., None]) * dec_b)], -1) * scale
    j = np.arange(CTX, dtype=f)[:, None]
    zeta = np.stack([np.exp((CTX - 1 - j) * dec_f), np.exp(j * dec_b)], -1)
    const = np.zeros((P, C_N))
    const[:, C_ID:C_ID + P] = np.eye(P)
    const[:, C_XI:C_XI + 32] = xi.transpose(1, 0, 2, 3).reshape(P, 32)
    const[:, C_ZETA:C_ZETA + 8] = zeta.reshape(P, 8)
    const[:, C_IOTA:C_IOTA + 2 * SLOTS] = np.concatenate(
        [np.arange(1, CAP_L + 1), np.full(CAP_C, -1), np.full(CAP_L, -1), np.arange(1, CAP_C + 1)])
    const[0:4, C_SELC:C_SELC + 2] = [[1, 0], [1, 0], [0, 1], [0, 1]]
    selb = const[:, C_SELB:C_SELB + 2 * P].reshape(P, 2, P)
    for g in range(2):
        selb[2 * g:2 * g + 2, g, :] = 1
        selb[4, g, :] = 1
    const[:, C_SELB:C_SELB + 2 * P] = selb.reshape(P, 2 * P)
    grid = np.float32(64)
    row, col = np.arange(LAT) // 64, np.arange(LAT) % 64
    nf = DK // 4
    freqs = 10000.0 ** (-np.arange(nf, dtype=f) / nf)
    ang = np.concatenate([row[:, None] * freqs, col[:, None] * freqs], -1).T
    rope = np.stack([np.concatenate([np.cos(ang)] * 2), np.concatenate([np.sin(ang), -np.sin(ang)])])
    return {"consts": const.astype(np.float32), "decay": decay.astype(np.float32), "rope": rope.astype(np.float32)}


def kernel(x_prompt, x_sample, c, state_lru, state_ret, c_ctx, ada_w, ada_b, norm_mix_pre, norm_mix_post,
           norm_ffn_pre, norm_ffn_post, w_in, conv_w, conv_b, lru_wa, lru_ba, lru_wi, lru_bi, lru_lambda,
           w_out, router_w, exp_w_gate, exp_w_up, exp_w_down):
    import numpy as np
    import concourse.bacc as bacc
    from concourse.bass_utils import run_bass_kernel_spmd

    rows = [c, c_ctx, norm_mix_pre, norm_ffn_pre, conv_w, conv_b, lru_ba, lru_bi, lru_lambda, state_lru,
            ada_b[:, 0:2 * D], ada_b[:, 3 * D:5 * D]]
    vectors = np.concatenate([a.reshape(-1, P) for a in rows])
    ins = {
        "x_ctx": x_prompt[0], "x_lat": x_sample[0], "vectors": vectors, "state_ret": state_ret.reshape(2, HEADS, DK, DK),
        "ada_w": ada_w[0], "ada_b": ada_b.reshape(48, P), "norm_mix_post": norm_mix_post[0],
        "norm_ffn_post": norm_ffn_post[0], "w_in": w_in[0], "lru_wa": lru_wa[0], "lru_wi": lru_wi[0], "w_out": w_out[0],
        "router_w": router_w[0], "exp_gate": exp_w_gate[0], "exp_up": exp_w_up[0], "exp_down": exp_w_down[0],
        **tables(),
    }
    outs = {"y_ctx": (CTX, D), "y_lat": (LAT, D), "new_lru": (8, P), "new_ret": (2, HEADS, DK, DK)}
    nc = bacc.Bacc("TRN2", target_bir_lowering=False, num_devices=1)
    arrays, args = {}, {}
    for name, a in ins.items():
        arrays[f"in_{name}"] = np.ascontiguousarray(a)
        args[name] = nc.dram_tensor(f"in_{name}", a.shape, F32, kind="ExternalInput").ap()
    for name, shape in outs.items():
        args[name] = nc.dram_tensor(f"out_{name}", shape, F32, kind="ExternalOutput").ap()
    build(nc, **args)
    r = run_bass_kernel_spmd(nc, [arrays], core_ids=[0]).results[0]
    return (r["out_y_ctx"].reshape(1, CTX, D), r["out_y_lat"].reshape(1, LAT, D),
            r["out_new_lru"].reshape(1, 1, 2, LW), r["out_new_ret"].reshape(1, 1, 2, HEADS, DK, DK))
```
